# Optimizing a Trainium2 kernel written in Bass

```python
import jax, jax.numpy as jnp
from jax import lax
import numpy as np

D_MODEL = 1024
BATCH = 1
SEQ = 512
DEPTH = 1
DEC_BATCH = 8
DEC_SEQ = 1
PAST_LEN = 2048
PAGE_SIZE = 128

N_HEADS = 8
HEAD_DIM = 64
N_KV_HEADS = 2
ROT_DIM = HEAD_DIM // 4
ROPE_THETA = 500000.0
IDX_HEADS = 4
IDX_DIM = 64
TOPK_MAX = 256
Q_BLOCK = 128
GM_WIDTH = D_MODEL // 2
GM_GROUPS = 8
GM_GROUP_DIM = GM_WIDTH // GM_GROUPS
CHUNK = 128
N_EXPERT_GROUPS = 4
EXPERTS_PER_GROUP = 8
N_EXPERTS = N_EXPERT_GROUPS * EXPERTS_PER_GROUP
EXPERT_TOP_K = 2
D_EXPERT = D_MODEL // 4
EPS = 1e-6
ATTN_WIDTH = N_HEADS * HEAD_DIM
KV_WIDTH = N_KV_HEADS * HEAD_DIM
IN_SIZES = (ATTN_WIDTH, KV_WIDTH, KV_WIDTH, IDX_HEADS * IDX_DIM, IDX_DIM, IDX_HEADS, GM_WIDTH, GM_WIDTH, 2 * D_MODEL)
D_IN = sum(IN_SIZES)
N_PAGES = PAST_LEN // PAGE_SIZE
N_POOL_PAGES = (DEC_BATCH * N_PAGES * 5) // 4

kernel_name = "hybrid_dsa_gmlp_hmoe_step"

def rms_norm(x, g):
    xf = x.astype(jnp.float32)
    y = xf * lax.rsqrt(jnp.mean(xf * xf, axis=-1, keepdims=True) + EPS)
    return (y * g.astype(jnp.float32)).astype(x.dtype)

def layer_norm(x, g, b):
    xf = x.astype(jnp.float32)
    mu = jnp.mean(xf, axis=-1, keepdims=True)
    var = jnp.mean(jnp.square(xf - mu), axis=-1, keepdims=True)
    return ((xf - mu) * lax.rsqrt(var + EPS) * g.astype(jnp.float32) + b.astype(jnp.float32)).astype(x.dtype)

def partial_rope(x, pos):
    half = ROT_DIM // 2
    inv_freq = ROPE_THETA ** (-jnp.arange(half, dtype=jnp.float32) / half)
    ang = pos.astype(jnp.float32)[:, None] * inv_freq[None, :]
    cos = jnp.cos(ang)[:, None, :]
    sin = jnp.sin(ang)[:, None, :]
    xf = x.astype(jnp.float32)
    x1, x2 = xf[..., :half], xf[..., half:ROT_DIM]
    out = jnp.concatenate([x1 * cos - x2 * sin, x2 * cos + x1 * sin, xf[..., ROT_DIM:]], axis=-1)
    return out.astype(x.dtype)

def adaln_terms(c, w_ada, b_ada):
    mod = jax.nn.silu(c) @ w_ada + b_ada
    return [m[:, None, :] for m in jnp.split(mod, 6, axis=-1)]

def modulate(x, g, shift, scale):
    return rms_norm(x, g) * (1.0 + scale) + shift

def project_inputs(h, pos, w_in, q_norm_g, k_norm_g, kidx_norm_g, gm_ln_g, gm_ln_b):
    B, S, _ = h.shape
    offsets = np.cumsum(IN_SIZES)[:-1].tolist()
    q, k, v, qi, ki, wi, u, vg, gates = jnp.split(h @ w_in, offsets, axis=-1)
    q = partial_rope(rms_norm(q.reshape(B, S, N_HEADS, HEAD_DIM), q_norm_g), pos)
    k = partial_rope(rms_norm(k.reshape(B, S, N_KV_HEADS, HEAD_DIM), k_norm_g), pos)
    v = v.reshape(B, S, N_KV_HEADS, HEAD_DIM)
    qi = partial_rope(qi.reshape(B, S, IDX_HEADS, IDX_DIM), pos)
    ki = partial_rope(rms_norm(ki, kidx_norm_g)[:, :, None, :], pos)[:, :, 0, :]
    u = jax.nn.gelu(u)
    vg = layer_norm(jax.nn.gelu(vg), gm_ln_g, gm_ln_b)
    gate_attn, gate_gmlp = jnp.split(jax.nn.sigmoid(gates), 2, axis=-1)
    return q, k, v, qi, ki, wi, u, vg, gate_attn, gate_gmlp

def index_scores(qi, wi, ki):
    dots = jnp.einsum('bqhd,bld->bqhl', qi, ki).astype(jnp.float32) * (IDX_DIM ** -0.5)
    return jnp.einsum('bqhl,bqh->bql', jax.nn.relu(dots), wi.astype(jnp.float32)) * (IDX_HEADS ** -0.5)

def select_keys(scores, q_pos, topk):
    L = scores.shape[-1]
    admissible = jnp.arange(L)[None, None, :] <= q_pos[None, :, None]
    _, idx = lax.top_k(jnp.where(admissible, scores, -jnp.inf), topk)
    valid = idx <= q_pos[None, :, None]
    return idx, valid

def sparse_attend(q, k_sel, v_sel, valid):
    B, Q = q.shape[:2]
    qg = q.reshape(B, Q, N_KV_HEADS, N_HEADS // N_KV_HEADS, HEAD_DIM)
    s = jnp.einsum('bqhgd,bqkhd->bqhgk', qg, k_sel).astype(jnp.float32) * (HEAD_DIM ** -0.5)
    s = jnp.where(valid[:, :, None, None, :], s, -jnp.inf)
    p = jax.nn.softmax(s, axis=-1).astype(v_sel.dtype)
    o = jnp.einsum('bqhgk,bqkhd->bqhgd', p, v_sel)
    return o.reshape(B, Q, ATTN_WIDTH)

def prompt_sparse_attention(q, k, v, qi, wi, ki):
    B, S = q.shape[:2]
    nb = S // Q_BLOCK
    topk = min(TOPK_MAX, S // 4)
    bidx = jnp.arange(B)[:, None, None]

    def to_blocks(a):
        return jnp.moveaxis(a.reshape((B, nb, Q_BLOCK) + a.shape[2:]), 1, 0)

    def block(args):
        q_b, qi_b, wi_b, blk = args
        q_pos = blk * Q_BLOCK + jnp.arange(Q_BLOCK)
        idx, valid = select_keys(index_scores(qi_b, wi_b, ki), q_pos, topk)
        return sparse_attend(q_b, k[bidx, idx], v[bidx, idx], valid)

    out = lax.map(block, (to_blocks(q), to_blocks(qi), to_blocks(wi), jnp.arange(nb)))
    return jnp.moveaxis(out, 0, 1).reshape(B, S, ATTN_WIDTH)

def sample_sparse_attention(q, k_new, v_new, qi, wi, ki_new, cache_k, cache_v, cache_kidx, page_table, layer):
    DB, DS = q.shape[:2]
    L = PAST_LEN + DS
    topk = min(TOPK_MAX, L // 4)
    q_pos = PAST_LEN + jnp.arange(DS)
    ki_past = cache_kidx[layer, page_table].reshape(DB, PAST_LEN, IDX_DIM)
    ki_all = jnp.concatenate([ki_past, ki_new.astype(ki_past.dtype)], axis=1)
    idx, valid = select_keys(index_scores(qi, wi, ki_all), q_pos, topk)
    page = jnp.minimum(idx // PAGE_SIZE, N_PAGES - 1)
    phys = jnp.take_along_axis(page_table, page.reshape(DB, -1), axis=1).reshape(idx.shape)
    off = idx % PAGE_SIZE
    new_i = jnp.clip(idx - PAST_LEN, 0, DS - 1)
    is_new = (idx >= PAST_LEN)[..., None, None]
    bidx = jnp.arange(DB)[:, None, None]
    k_sel = jnp.where(is_new, k_new[bidx, new_i], cache_k[layer, phys, off])
    v_sel = jnp.where(is_new, v_new[bidx, new_i], cache_v[layer, phys, off])
    return sparse_attend(q, k_sel, v_sel, valid)

def chunk_spatial_gating(u, vg, gm_spatial_w, gm_spatial_b):
    B, S, _ = u.shape
    pad = (-S) % CHUNK
    nc = (S + pad) // CHUNK
    vc = jnp.pad(vg, ((0, 0), (0, pad), (0, 0))).reshape(B, nc, CHUNK, GM_GROUPS, GM_GROUP_DIM)
    causal = jnp.tril(jnp.ones((CHUNK, CHUNK), dtype=bool))
    w = jnp.where(causal[None], gm_spatial_w, 0.0).astype(vc.dtype)
    mixed = jnp.einsum('gts,bcsgd->bctgd', w, vc) + gm_spatial_b.T[None, None, :, :, None]
    mixed = mixed.reshape(B, nc * CHUNK, GM_WIDTH)[:, :S]
    return u * mixed

def merge_branches(attn, gm, gate_attn, gate_gmlp, w_proj_attn, w_proj_gmlp, w_out):
    return (gate_attn * (attn @ w_proj_attn) + gate_gmlp * (gm @ w_proj_gmlp)) @ w_out

def hierarchical_moe(h, w_rg, b_rg, w_re, b_re, w_gate, w_up, w_down):
    B, S, D = h.shape
    t = h.reshape(B * S, D)
    g_logits = (t @ w_rg).astype(jnp.float32) + b_rg.astype(jnp.float32)
    g_probs = jax.nn.softmax(g_logits, axis=-1)
    g_sel = jnp.argmax(g_logits, axis=-1)
    g_w = jnp.take_along_axis(g_probs, g_sel[:, None], axis=-1)
    e_logits = ((t @ w_re).astype(jnp.float32) + b_re.astype(jnp.float32)).reshape(-1, N_EXPERT_GROUPS, EXPERTS_PER_GROUP)
    e_logits = jnp.take_along_axis(e_logits, g_sel[:, None, None], axis=1)[:, 0]
    top_p, top_i = lax.top_k(jax.nn.softmax(e_logits, axis=-1), EXPERT_TOP_K)
    top_p = top_p / jnp.sum(top_p, axis=-1, keepdims=True)
    expert_id = g_sel[:, None] * EXPERTS_PER_GROUP + top_i
    gate = jnp.sum(jax.nn.one_hot(expert_id, N_EXPERTS, dtype=jnp.float32) * (g_w * top_p)[..., None], axis=1)
    out = jnp.zeros_like(t)
    for g in range(N_EXPERT_GROUPS):
        sl = slice(g * EXPERTS_PER_GROUP, (g + 1) * EXPERTS_PER_GROUP)
        hid = jax.nn.silu(jnp.einsum('td,edf->tef', t, w_gate[sl])) * jnp.einsum('td,edf->tef', t, w_up[sl])
        hid = hid * gate[:, sl, None].astype(hid.dtype)
        out = out + jnp.einsum('tef,efd->td', hid, w_down[sl])
    return out.reshape(B, S, D)

def setup_inputs(seed: int = 0) -> dict:
    key = jax.random.key(seed)
    ks = iter(jax.random.split(key, 40))
    f32 = jnp.float32

    def nrm(shape, scale):
        return scale * jax.random.normal(next(ks), shape, f32)

    def gain(shape):
        return 1.0 + 0.1 * jax.random.normal(next(ks), shape, f32)

    x_prompt = nrm((BATCH, SEQ, D_MODEL), 1.0)
    x_sample = nrm((DEC_BATCH, DEC_SEQ, D_MODEL), 1.0)
    c_prompt = nrm((BATCH, D_MODEL), 1.0)
    c_sample = nrm((DEC_BATCH, D_MODEL), 1.0)
    cache_k = nrm((DEPTH, N_POOL_PAGES, PAGE_SIZE, N_KV_HEADS, HEAD_DIM), 1.0)
    cache_v = nrm((DEPTH, N_POOL_PAGES, PAGE_SIZE, N_KV_HEADS, HEAD_DIM), 1.0)
    cache_kidx = nrm((DEPTH, N_POOL_PAGES, PAGE_SIZE, IDX_DIM), 1.0)
    perm = jax.random.permutation(next(ks), N_POOL_PAGES)
    page_table = perm[:DEC_BATCH * N_PAGES].reshape(DEC_BATCH, N_PAGES).astype(jnp.int32)
    return {
        "x_prompt": x_prompt,
        "x_sample": x_sample,
        "c_prompt": c_prompt,
        "c_sample": c_sample,
        "cache_k": cache_k,
        "cache_v": cache_v,
        "cache_kidx": cache_kidx,
        "page_table": page_table,
        "w_ada": nrm((DEPTH, D_MODEL, 6 * D_MODEL), 0.5 * D_MODEL ** -0.5),
        "b_ada": nrm((DEPTH, 6 * D_MODEL), 0.02),
        "norm_mix_g": gain((DEPTH, D_MODEL)),
        "norm_ffn_g": gain((DEPTH, D_MODEL)),
        "w_in": nrm((DEPTH, D_MODEL, D_IN), D_MODEL ** -0.5),
        "q_norm_g": gain((DEPTH, HEAD_DIM)),
        "k_norm_g": gain((DEPTH, HEAD_DIM)),
        "kidx_norm_g": gain((DEPTH, IDX_DIM)),
        "gm_ln_g": gain((DEPTH, GM_WIDTH)),
        "gm_ln_b": nrm((DEPTH, GM_WIDTH), 0.02),
        "gm_spatial_w": nrm((DEPTH, GM_GROUPS, CHUNK, CHUNK), CHUNK ** -0.5),
        "gm_spatial_b": gain((DEPTH, GM_GROUPS, CHUNK)),
        "w_proj_attn": nrm((DEPTH, ATTN_WIDTH, D_MODEL), ATTN_WIDTH ** -0.5),
        "w_proj_gmlp": nrm((DEPTH, GM_WIDTH, D_MODEL), GM_WIDTH ** -0.5),
        "w_out": nrm((DEPTH, D_MODEL, D_MODEL), D_MODEL ** -0.5),
        "w_router_group": nrm((DEPTH, D_MODEL, N_EXPERT_GROUPS), D_MODEL ** -0.5),
        "b_router_group": nrm((DEPTH, N_EXPERT_GROUPS), 0.01),
        "w_router_expert": nrm((DEPTH, D_MODEL, N_EXPERTS), D_MODEL ** -0.5),
        "b_router_expert": nrm((DEPTH, N_EXPERTS), 0.01),
        "w_expert_gate": nrm((DEPTH, N_EXPERTS, D_MODEL, D_EXPERT), D_MODEL ** -0.5),
        "w_expert_up": nrm((DEPTH, N_EXPERTS, D_MODEL, D_EXPERT), D_MODEL ** -0.5),
        "w_expert_down": nrm((DEPTH, N_EXPERTS, D_EXPERT, D_MODEL), D_EXPERT ** -0.5),
    }

def reference(x_prompt, x_sample, c_prompt, c_sample, cache_k, cache_v, cache_kidx, page_table,
              w_ada, b_ada, norm_mix_g, norm_ffn_g, w_in, q_norm_g, k_norm_g, kidx_norm_g,
              gm_ln_g, gm_ln_b, gm_spatial_w, gm_spatial_b, w_proj_attn, w_proj_gmlp, w_out,
              w_router_group, b_router_group, w_router_expert, b_router_expert,
              w_expert_gate, w_expert_up, w_expert_down):
    pos_p = jnp.arange(SEQ, dtype=jnp.int32)
    pos_s = PAST_LEN + jnp.arange(DEC_SEQ, dtype=jnp.int32)
    xp, xs = x_prompt, x_sample
    k_p_rows, v_p_rows, ki_p_rows = [], [], []
    k_s_rows, v_s_rows, ki_s_rows, gv_s_rows = [], [], [], []
    for l in range(DEPTH):
        mp = adaln_terms(c_prompt, w_ada[l], b_ada[l])
        ms = adaln_terms(c_sample, w_ada[l], b_ada[l])

        hp = modulate(xp, norm_mix_g[l], mp[0], mp[1])
        q, k, v, qi, ki, wi, u, vg, ga, gb = project_inputs(hp, pos_p, w_in[l], q_norm_g[l], k_norm_g[l],
                                                            kidx_norm_g[l], gm_ln_g[l], gm_ln_b[l])
        attn_p = prompt_sparse_attention(q, k, v, qi, wi, ki)
        gm_p = chunk_spatial_gating(u, vg, gm_spatial_w[l], gm_spatial_b[l])
        xp = xp + mp[2] * merge_branches(attn_p, gm_p, ga, gb, w_proj_attn[l], w_proj_gmlp[l], w_out[l])
        k_p_rows.append(k)
        v_p_rows.append(v)
        ki_p_rows.append(ki)

        hs = modulate(xs, norm_mix_g[l], ms[0], ms[1])
        q, k, v, qi, ki, wi, u, vg, ga, gb = project_inputs(hs, pos_s, w_in[l], q_norm_g[l], k_norm_g[l],
                                                            kidx_norm_g[l], gm_ln_g[l], gm_ln_b[l])
        attn_s = sample_sparse_attention(q, k, v, qi, wi, ki, cache_k, cache_v, cache_kidx, page_table, l)
        gm_s = chunk_spatial_gating(u, vg, gm_spatial_w[l], gm_spatial_b[l])
        xs = xs + ms[2] * merge_branches(attn_s, gm_s, ga, gb, w_proj_attn[l], w_proj_gmlp[l], w_out[l])
        k_s_rows.append(k)
        v_s_rows.append(v)
        ki_s_rows.append(ki)
        gv_s_rows.append(vg)

        xp = xp + mp[5] * hierarchical_moe(modulate(xp, norm_ffn_g[l], mp[3], mp[4]), w_router_group[l],
                                            b_router_group[l], w_router_expert[l], b_router_expert[l],
                                            w_expert_gate[l], w_expert_up[l], w_expert_down[l])
        xs = xs + ms[5] * hierarchical_moe(modulate(xs, norm_ffn_g[l], ms[3], ms[4]), w_router_group[l],
                                            b_router_group[l], w_router_expert[l], b_router_expert[l],
                                            w_expert_gate[l], w_expert_up[l], w_expert_down[l])
    return (xp, xs, jnp.stack(k_p_rows), jnp.stack(v_p_rows), jnp.stack(ki_p_rows),
            jnp.stack(k_s_rows), jnp.stack(v_s_rows), jnp.stack(ki_s_rows), jnp.stack(gv_s_rows))


_drawn_inputs = setup_inputs


def setup_inputs(seed=0):
    import zlib

    import numpy as np

    out = dict(_drawn_inputs(seed))
    spreads = {}
    factors = {'gm_ln_b': 2.979, 'b_router_expert': 25.54}
    for name, (base, spread) in spreads.items():
        noise = np.random.default_rng([zlib.crc32(name.encode()), seed]).standard_normal(out[name].shape)
        drawn = base * np.exp(spread * noise) if base else spread * noise
        out[name] = __import__('jax').numpy.asarray(drawn.astype(out[name].dtype))
    for name, factor in factors.items():
        out[name] = (out[name] * factor).astype(out[name].dtype)
    return out
```

```python
from contextlib import ExitStack

import numpy as np

import concourse.bass as bass
from concourse import mybir

F32 = mybir.dt.float32
I32 = mybir.dt.int32
U32 = mybir.dt.uint32
ALU = mybir.AluOpType
ACT = mybir.ActivationFunctionType
AX_X = mybir.AxisListType.X

P = 128
D = 1024
KD = D // P
SEQ = 512
NT = SEQ // P
NS = 8
TOK = SEQ + NS
HALF = TOK // 2
PAST = 2048
PAGE = 128
N_PAGES = PAST // PAGE
POOL_PAGES = 160
NH, HD, NKV = 8, 64, 2
ROT = HD // 4
THETA = 500000.0
IH, ID = 4, 64
TOPK_P = min(256, SEQ // 4)
TOPK_S = min(256, (PAST + 1) // 4)
GM, GG, GD = 512, 8, 64
CHUNK = 128
NEG, EPG = 4, 8
NE = NEG * EPG
DE = D // 4
EPS = 1e-6
BIG = 1e30
TAKEN = -3e38

QI, KI, WI, VV = 0, 256, 320, 324
NA = VV + NKV * HD
NB = NH * HD
VG0 = 192
NC = NKV * HD + VG0
ND = GM - VG0
HEAD_ORDER = [h for j in range(4) for h in (j, j + 4)]

STREAM = ([(f"ada{c}", KD * 512) for c in range(4)] + [("A", KD * NA), ("B", KD * NB), ("C", KD * NC), ("D", KD * ND)]
          + [("U", KD * 512)] + [(f"G{c}", KD * 512) for c in range(4)]
          + [("WA", 4 * D), ("WG", 4 * D)] + [(f"ada{c}", KD * 512) for c in range(4, 12)]
          + [("O0", KD * 512), ("O1", KD * 512)])
SLOT_OF = {name: n for n, (name, _) in enumerate(STREAM)}
RING = 3

SB = 64
ASSIGNED = 2 * TOK
N_OVER = ASSIGNED // (SB + 1)
N_ITEMS = NE + N_OVER

O_GATES, O_QT, O_ATT, O_U, O_KT, O_QIT, O_KIT = 0, 8320, 10400, 12480, 14560, 15080, 16120
O_VG, O_QR, O_KR, O_AR, O_WS, O_BT, O_S, O_PT, O_WORK, O_SC = (
    16640, 19200, 21760, 22400, 24660, 25684, 26196, 28244, 29268, 30420)
ARENA = 33024


def constant_fields():
    eye = np.eye(P, dtype=np.float32)
    row = np.arange(P)
    f = {}
    f["ident"] = eye
    sel_p = np.zeros((P, P)); sel_p[8::32, :] = 1.0
    f["sel_p"] = sel_p
    sel_s = np.zeros((P, NS))
    for i in range(NS):
        sel_s[i::32, i] = 1.0
    f["sel_s"] = sel_s
    f["before"] = (row[:, None] < row[None, :]).astype(np.float32)
    f["ones"] = np.ones((P, P))
    f["causal"] = np.where(row[None, :] <= row[:, None], 0.0, -BIG)
    pos = np.zeros((P, NT + 1), np.float32)
    for t in range(NT):
        pos[:, t] = t * P + row
    pos[:, NT] = PAST
    half = ROT // 2
    inv = np.float32(THETA) ** (-np.arange(half, dtype=np.float32) / np.float32(half))
    ang = (pos[:, :, None] * inv[None, None, :].astype(np.float32)).astype(np.float32)
    cos, sin = np.cos(ang), np.sin(ang)
    f["cos"] = np.concatenate([cos, cos], -1).reshape(P, -1)
    f["sin"] = np.concatenate([-sin, sin], -1).reshape(P, -1)
    f["iota"] = np.tile(np.arange(P, dtype=np.float32), (P, 1))
    tok = np.zeros((P, NT + 1)); valid = np.zeros((P, NT + 1))
    for t in range(NT):
        tok[:, t] = t * P + row; valid[:, t] = 1.0
    tok[:NS, NT] = SEQ + row[:NS]; valid[:NS, NT] = 1.0
    f["tok"] = tok
    f["valid"] = valid
    f["page_seg"] = (row % 8)[:, None]
    place = np.zeros((P, 2, 2, 4, 8, 4))
    for b in range(NS):
        for par in range(2):
            place[b, b // 4, par, b % 4, par, :] = 1.0
    f["place"] = place.reshape(P, -1)
    spread = np.zeros((P, 2, P)); gather = np.zeros((P, 2, NS))
    for b in range(NS):
        spread[b, b // 4, 32 * (b % 4):32 * (b % 4) + NH] = 1.0
        gather[32 * (b % 4):32 * (b % 4) + NH, b // 4, b] = 1.0
    f["spread"] = spread.reshape(P, -1)
    f["gather"] = gather.reshape(P, -1)
    f["head"] = (row[:, None] % 32 == np.arange(NH)[None, :])
    f["own"] = np.repeat(np.eye(NS), NH, axis=1) if False else np.concatenate(
        [np.repeat(np.eye(NS), NH, axis=1), np.zeros((P - NS, NS * NH))])
    f["rev4"] = np.tile(4.0 - np.arange(4), (P, 1))
    f["rev32"] = np.tile(32.0 - np.arange(32), (P, 1))
    f["first_slot"] = np.tile(SB * np.arange(NE), (P, 1))
    f["over"] = np.tile(SB * np.arange(1, 9), (P, 1))
    f["one"] = np.ones((P, 1))
    return {k: np.ascontiguousarray(v, dtype=np.float32) for k, v in f.items()}


CONSTS = constant_fields()
CONST_AT = {}
_n = 0
for _k, _v in CONSTS.items():
    CONST_AT[_k] = (_n, _v.shape[1])
    _n += _v.shape[1]
N_CONST = _n


class Lane:

    def __init__(self, engine, semaphore):
        self.engine, self.semaphore, self.count = engine, semaphore, 0

    def mark(self, instruction):
        instruction.then_inc(self.semaphore, 1)
        self.count += 1

    def wait(self):
        if self.count:
            self.engine.wait_ge(self.semaphore, self.count)

    def then(self, instruction):
        self.mark(instruction)
        self.wait()


class Banks:

    def __init__(self, full, free):
        self.full, self.free = full, free
        self.count = [0] * 8
        self.last = [None] * 8
        self.at = {}

    def begin(self, pe, name, *banks):
        before = {self.at[self.last[b]] for b in banks if self.last[b] is not None}
        lead = banks[0]
        self.at[name] = (lead, self.count[lead])
        self.count[lead] += 1
        for b in banks:
            self.last[b] = name
        for b, n in sorted(before):
            pe.wait_ge(self.free[b], n + 1)

    def filled(self, instruction, name):
        instruction.then_inc(self.full[self.at[name][0]], 1)

    def wait_full(self, engine, name):
        b, n = self.at[name]
        engine.wait_ge(self.full[b], n + 1)

    def drained(self, instruction, name):
        instruction.then_inc(self.free[self.at[name][0]], 1)

    def wait_drained(self, engine, name):
        b, n = self.at[name]
        engine.wait_ge(self.free[b], n + 1)


def spread_dim(ap, axis, n):
    wide = ap.unsqueeze(axis)
    shape = list(wide.shape)
    shape[axis] = n
    return wide.broadcast_to(shape)


def decoder_step(nc, io):
    ctx = ExitStack()
    with ctx:
        def sb(name, shape, dt=F32):
            return ctx.enter_context(nc.sbuf_tensor(name, shape, dt))

        def sem(name):
            return ctx.enter_context(nc.semaphore(name))

        ring = sb("ring", [P, RING, KD * 512])
        hT = sb("hT", [P, KD, TOK])
        hTs = sb("hTs", [P, KD, 32])
        c_T = sb("c_T", [P, KD, 32])
        bn = sb("bn", [P, NT + 1, 6])
        zeros = sb("zeros", [P, 256])
        arena = sb("arena", [P, ARENA])
        const = sb("const", [P, N_CONST])
        gains = sb("gains", [P, 3 * HD])
        stat = sb("stat", [P, 256])
        psum = ctx.enter_context(nc.psum_tensor("psum", [P, 8, 512], F32))

        def at(offset, size):
            return arena[:, offset:offset + size]

        def C(name):
            o, n = CONST_AT[name]
            return const[:, o:o + n]

        ident = C("ident")
        early = O_GATES
        mod1 = at(early, 4096).rearrange("p (g m n) -> p g m n", g=2, m=2)
        ln = at(early + 4096, 2 * GM).rearrange("p (m n) -> p m n", m=2)
        xbuf = at(early + 5120, (NT + 1) * D).rearrange("p (t n) -> p t n", n=D)
        relu_p = at(early, 4 * 512).rearrange("p (h n) -> p h n", h=4)
        ki_pages = at(early + 2048, 2 * D).rearrange("p (b n) -> p b n", b=2)
        ki_T = at(early + 5120, 2 * D).rearrange("p (b n) -> p b n", b=2)
        relu_s = at(early + 5120 + 2 * D, 2 * D).rearrange("p (b n) -> p b n", b=2)
        bias1 = at(O_VG, 4 * 512).rearrange("p (c n) -> p c n", c=4)
        gain1 = at(O_QR, D)
        junk = at(O_QR + D, D)
        G = at(O_PT, 2 * 512).rearrange("p (b n) -> p b n", b=2)
        gates = at(O_GATES, 16 * TOK).rearrange("p (f n) -> p f n", f=16)
        qT = at(O_QT, 4 * TOK).rearrange("p (j n) -> p j n", j=4)
        attT = at(O_ATT, 4 * TOK).rearrange("p (j n) -> p j n", j=4)
        uT = at(O_U, 4 * TOK).rearrange("p (j n) -> p j n", j=4)
        kT = at(O_KT, TOK)
        qiT = at(O_QIT, 2 * TOK).rearrange("p (j n) -> p j n", j=2)
        kiT = at(O_KIT, TOK)
        vg = at(O_VG, (NT + 1) * GM).rearrange("p (t n) -> p t n", n=GM)
        qraw = at(O_QR, (NT + 1) * NB).rearrange("p (t n) -> p t n", n=NB)
        kraw = at(O_KR, (NT + 1) * NKV * HD).rearrange("p (t n) -> p t n", n=NKV * HD)
        araw = at(O_AR, (NT + 1) * NA).rearrange("p (t n) -> p t n", n=NA)
        wsT = at(O_WS, GG * CHUNK).rearrange("p (g n) -> p g n", g=GG)
        bT = at(O_BT, 4 * CHUNK).rearrange("p (j n) -> p j n", j=4)
        ki_twice = at(O_S, (NT + 1) * P).rearrange("p (t n) -> p t n", n=P)
        qi_twice = at(O_S + 640, IH * P).rearrange("p (h c d) -> p h c d", h=IH, c=2)
        qi_lhs = at(O_S + 1152, NS * 32).rearrange("p (b m) -> p b m", b=NS)
        wi_lhs = at(O_S + 1408, 4 * NS).rearrange("p (c b) -> p c b", c=4)
        wi_place = at(O_S + 1440, 512)
        work = at(O_WORK, 1152)
        norm_tmp = at(O_S, 2560)
        scores = at(O_SC, PAST + 1)
        idx = at(O_SC + 2056, TOPK_S)
        page_rows = stat[:, 0:NS].bitcast(I32)
        page_rep = stat[:, NS:2 * NS].bitcast(I32)
        ssq = stat[:, 16:21]
        rstd = stat[:, 24:29]
        ki_ms = stat[:, 32:37]
        ki_r = stat[:, 40:45]
        k_ms = stat[:, 48:58]
        k_r = stat[:, 60:70]
        q_ms = stat[:, 72:112]
        q_r = stat[:, 112:152]
        new_dots = stat[:, 152:156]
        top8 = stat[:, 160:192]
        mu_var = stat[:, 192:202].rearrange("p (t m) -> p t m", m=2)
        vg_r = stat[:, 204:209]
        minus_half = stat[:, 212:252]

        norm_tmp2 = at(O_S, 2048).rearrange("p (h n) -> p h n", h=4)
        soft = [norm_tmp2, at(O_QR, 2048).rearrange("p (h n) -> p h n", h=4)]
        probsT = at(O_VG, 4 * 512).rearrange("p (c n) -> p c n", c=4)
        gm_w0 = stat[:, 252:256]
        pages_i = at(O_SC + 2312, N_PAGES * NS).bitcast(I32)
        pages_f = at(O_SC + 2440, N_PAGES * NS)
        k_sel = at(O_QR, 2048).rearrange("p (a n) -> p a n", n=P)
        v_sel = at(O_VG, 2048).rearrange("p (a n) -> p a n", n=P)
        k_selT = at(O_S, 2048).rearrange("p (b n) -> p b n", b=NS)
        soft_s = at(O_PT, 2 * 257).rearrange("p (g n) -> p g n", g=2)
        page_hot = at(O_WORK, 256).rearrange("p (a n) -> p a n", n=N_PAGES)
        q_lhs = at(O_WORK + 256, 256).rearrange("p (b m) -> p b m", b=NS)
        probsT_s = at(O_WORK + 512, 512).rearrange("p (a n) -> p a n", n=P)
        sel_tmp = at(O_WORK + 1024, 128)
        new_probs = sel_tmp[:, 0:2 * NH].rearrange("p (g h) -> p g h", g=2)
        new_spread = sel_tmp[:, 16:16 + NS * NH]
        slot_f = at(O_PT + 520, 16)
        slot_i = at(O_PT + 540, 16).bitcast(I32)
        off_i = at(O_PT + 560, 16).bitcast(I32)
        page_f = at(O_PT + 580, 16)
        off_f = at(O_PT + 600, 16)
        sel_rows = at(O_PT + 620, 16).bitcast(I32)
        idx_u = idx.bitcast(U32)
        key_bias = scores[:, 0:TOPK_S + 1]
        idx_f = scores[:, 512:512 + TOPK_S]
        sstat = sb("sstat", [P, 64])
        mx4 = [sstat[:, 0:4], sstat[:, 4:8]]
        sum4 = [sstat[:, 8:12], sstat[:, 12:16]]
        inv4 = [sstat[:, 16:20], sstat[:, 20:24]]
        mx2, sum2, inv2 = sstat[:, 24:26], sstat[:, 26:28], sstat[:, 28:30]
        top8_s = sstat[:, 32:40]
        idx8_s = sstat[:, 40:48].bitcast(U32)
        idx_max = sstat[:, 48:49]

        x2 = at(0, (NT + 1) * D).rearrange("p (t n) -> p t n", n=D)
        mod2 = {m: at(o, 2 * D).rearrange("p (g n) -> p g n", g=2)
                for m, o in (("gate2", 5120), ("gate1", 7168), ("shift2", 9216), ("scale2", 11264))}
        t2 = at(13312, (NT + 1) * D).rearrange("p (t n) -> p t n", n=D)
        bias2 = at(19456, 8 * 512).rearrange("p (c n) -> p c n", c=8)
        gain2 = at(23552, D)
        w_tmp = at(25600, 1024).rearrange("p (b n) -> p b n", b=2)
        w_router = at(26624, KD * (NEG + NE)).rearrange("p (k n) -> p k n", k=KD)
        b_router = at(26912, NEG + NE)
        junk2 = at(19456, D)
        router_at = [27648]

        def rt(n):
            router_at[0] += n
            assert router_at[0] <= ARENA
            return at(router_at[0] - n, n)

        T5 = NT + 1
        logits_T = rt(TOK)
        logits = rt(T5 * (NEG + NE)).rearrange("p (t n) -> p t n", t=T5)
        e_logits, hot1, hot2, e_tmp, chosen, place = (rt(T5 * NE).rearrange("p (t n) -> p t n", t=T5) for _ in range(6))
        before_sum = rt((T5 + 1) * NE).rearrange("p (t n) -> p t n", n=NE)
        g_tmp = rt(T5 * NEG).rearrange("p (t n) -> p t n", t=T5)
        g_exp = rt(T5 * NEG).rearrange("p (t n) -> p t n", t=T5)
        slot_hot = rt(2 * T5 * P).rearrange("p (a n) -> p a n", n=P)
        item_hot = rt(2 * T5 * 2 * N_ITEMS).rearrange("p (a n) -> p a n", n=2 * N_ITEMS)
        over_cmp = at(26960, NE * 8).rearrange("p (e m) -> p e m", m=8)
        over_hot = at(26960, N_OVER * NE).rearrange("p (j e) -> p j e", e=NE)
        r = sb("router", [P, 400])
        g_max, e_max1, e_max2, w_max, g_sum, p_first, e_ratio = (r[:, 5 * i:5 * i + 5] for i in range(7))
        rank = r[:, 40:50].rearrange("p (c t) -> p c t", c=2)
        gate_of = r[:, 50:60].rearrange("p (c t) -> p c t", c=2)
        token_of = r[:, 60:70].rearrange("p (c t) -> p c t", c=2)
        rank_i = r[:, 70:80].bitcast(I32)
        slot_of_i, item_of_i = r[:, 80:90].bitcast(I32), r[:, 90:100].bitcast(I32)
        slot_of, item_of = r[:, 100:110], r[:, 110:120]
        n_over, over_end, over_shift, counts = (r[:, 120 + 32 * i:152 + 32 * i] for i in range(4))
        over_expert_f, over_expert = r[:, 248:264], r[:, 264:280].bitcast(I32)
        over_total = r[:, 280:281].bitcast(I32)
        gate_tab = r[:, 288:288 + N_ITEMS]
        token_tab = r[:, 336:336 + N_ITEMS].bitcast(I32)
        rank_scaled = r[:, 384:389]

        flat_ring = ring.rearrange("p r n -> p (r n)")
        EW = KD * 2 * DE + 2 * D
        expert_w = [flat_ring[:, 0:EW], flat_ring[:, EW:2 * EW], at(7168, EW), at(13312, EW)]
        w_gu = [w[:, 0:KD * 2 * DE].rearrange("p (k n) -> p k n", k=KD) for w in expert_w]
        w_dn = [w[:, KD * 2 * DE:EW].rearrange("p (f n) -> p f n", f=2) for w in expert_w]
        x_rows = at(19456, 2 * D).rearrange("p (b n) -> p b n", b=2)
        y_rows = at(21504, 1024).rearrange("p (b n) -> p b n", b=2)
        silu_g = at(22528, 2 * DE).rearrange("p (b n) -> p b n", b=2)
        hidden = at(23040, 2 * DE).rearrange("p (b n) -> p b n", b=2)
        x_T = at(23552, 2 * KD * SB).rearrange("p (b k n) -> p b k n", b=2, k=KD)
        hidden_T = at(24576, 4 * SB).rearrange("p (b f n) -> p b f n", b=2, f=2)
        over_token = at(24832, 1).bitcast(I32)
        picked = flat_ring[:, 0:4 * D].rearrange("p (b c n) -> p b c n", b=2, c=2)

        bank_full = [sem(f"bank_full{b}") for b in range(8)]
        bank_free = [sem(f"bank_free{b}") for b in range(8)]
        banks = Banks(bank_full, bank_free)
        ring_full = [sem(f"ring_full{i}") for i in range(RING)]
        const_in = sem("const_in")
        c_in = sem("c_in")
        bias_in = sem("bias_in")
        ln_in = sem("ln_in")
        gmlp_in, ws_in = sem("gmlp_in"), sem("ws_in")
        x_in = [sem(f"x_in{t}") for t in range(NT + 1)]
        pages_in = sem("pages_in")
        c_silu = sem("c_silu")
        zeroed = sem("zeroed")
        ssq_ready = sem("ssq_ready")
        rstd_asked, rstd_ready = sem("rstd_asked"), sem("rstd_ready")
        h_ready = sem("h_ready")
        a_ready = sem("a_ready")
        k_ready = sem("k_ready")
        q_ready = sem("q_ready")
        vg_ready = sem("vg_ready")
        qi_dup_ready = sem("qi_dup_ready")
        qi_lhs_ready = sem("qi_lhs_ready")
        relu_p_read = sem("relu_p_read")
        page_rows_ready = sem("page_rows_ready")
        ki_in = [sem(f"ki_in{i}") for i in range(2)]
        ki_used = sem("ki_used")
        scores_ready = sem("scores_ready")
        outs, y_outs = sem("outs"), sem("y_outs")
        late_in = sem("late_in")
        over_zeroed = sem("over_zeroed")
        x2_in = sem("x2_in")
        router_in = sem("router_in")
        x2_half, x2_ready = sem("x2_half"), sem("x2_ready")
        ssq2_ready = sem("ssq2_ready")
        t2_ready = sem("t2_ready")
        t2_stored = sem("t2_stored")
        g_diff_ready, g_exp_ready = sem("g_diff_ready"), sem("g_exp_ready")
        e_diff_ready, e_exp_ready = sem("e_diff_ready"), sem("e_exp_ready")
        chosen_ready = sem("chosen_ready")
        tables_hot_ready, tables_ready = sem("tables_hot_ready"), sem("tables_ready")
        w_got = [sem(f"w_got{i}") for i in range(4)]
        x_got = [sem(f"x_got{i}") for i in range(2)]
        y_stored = [sem(f"y_stored{i}") for i in range(2)]
        (xT_full, xT_out, gu_full, silu_done, hidden_done, hT_full, hT_out, y_full, y_out) = (
            sem(n) for n in ("xT_full", "xT_out", "gu_full", "silu_done", "hidden_done", "hT_full", "hT_out", "y_full",
                             "y_out"))
        (o_w, o_token, o_x, o_xT_full, o_xT_out, o_gu, o_silu, o_hidden, o_hT_full, o_hT_out, o_y, o_y_out, o_stored) = (
            sem(n) for n in ("o_w", "o_token", "o_x", "o_xT_full", "o_xT_out", "o_gu", "o_silu", "o_hidden", "o_hT_full",
                             "o_hT_out", "o_y", "o_y_out", "o_stored"))
        experts_done = sem("experts_done")
        pe_passed, o_pe_passed, o_pool_passed = (
            sem(n) for n in ("pe_passed", "o_pe_passed", "o_pool_passed"))
        picked_in = [sem(f"picked_in{i}") for i in range(2)]
        picked_used = sem("picked_used")
        y_ready = sem("y_ready")
        ws_masked = sem("ws_masked")
        gm_ready, gm_tile = sem("gm_ready"), sem("gm_tile")
        max_ready, exp_ready, probs_ready = sem("max_ready"), sem("exp_ready"), sem("probs_ready")
        idx_ready = sem("idx_ready")
        pages_all_in = sem("pages_all_in")
        sel_rows_ready = sem("sel_rows_ready")
        k_sel_in, v_sel_in = sem("k_sel_in"), sem("v_sel_in")
        key_bias_ready = sem("key_bias_ready")
        q_lhs_ready = sem("q_lhs_ready")
        max_s_ready, exp_s_ready, probs_s_ready = sem("max_s_ready"), sem("exp_s_ready"), sem("probs_s_ready")
        new_spread_ready = sem("new_spread_ready")
        merged = sem("merged")
        values_done = sem("values_done")
        vector_lane, scalar_lane, pool_lane = sem("vector_lane"), sem("scalar_lane"), sem("pool_lane")
        n_outs = [0]
        last_use = {}
        ORDER = [(0, P, 0), (1, P, 1), ("S", NS, NT), (2, P, 2), (3, P, 3)]

        def lone_wait(engine, semaphore, value, passed):
            engine.wait_ge(semaphore, value)
            engine.sem_inc(passed, 1)

        def ring_wait(pe, name):
            n = SLOT_OF[name]
            pe.wait_ge(ring_full[n % RING], 16 * (n // RING + 1))

        def ring_at(name, width):
            kk = STREAM[SLOT_OF[name]][1] // width
            return ring[:, SLOT_OF[name] % RING, 0:kk * width].rearrange("p (k n) -> p k n", k=kk)

        def pair(b0):
            return psum[:, b0:b0 + 2, 0:HALF]

        def halves(ap):
            return ap.rearrange("p (s n) -> p s n", s=2)

        block = ctx.enter_context(nc.Block())

        @block.tensor
        def _(pe):
            def grouped(name, b, width, weights, lhs):
                banks.begin(pe, name, b)
                for k in range(KD):
                    j = k % 4
                    mm = pe.matmul(psum[32 * j:32 * j + 32, b, 0:width], lhs[:, k, :], weights[:, k, :],
                                   start=(k < 4), stop=(k >= 4), tile_position=(0, 32 * j))
                banks.filled(mm, name)

            def ada_product(c):
                ring_wait(pe, f"ada{c}")
                grouped(("ada", c), c % 2, 512, ring_at(f"ada{c}", 512), c_T)

            def ada_spread(c):
                banks.wait_drained(pe, ("ada", c))
                for name, sel, b, rows in (("adaP", "sel_p", 2 + c % 2, P), ("adaS", "sel_s", 4 + c % 2, NS)):
                    banks.begin(pe, (name, c), b)
                    mm = pe.matmul(psum[0:rows, b, :], C(sel), G[:, c % 2, :], start=True, stop=True)
                    banks.filled(mm, (name, c))

            pe.wait_ge(const_in, 16)
            pe.wait_ge(c_silu, 1)
            for c in range(5):
                if c < 4:
                    ada_product(c)
                    last_use[f"ada{c}"] = ("ada", c)
                if c >= 1:
                    ada_spread(c - 1)

            for t in range(NT + 1):
                n = P if t < NT else NS
                pe.wait_ge(h_ready, t + 1)
                for j in range(2):
                    b = 6 + j
                    banks.begin(pe, ("hT", t, j), b)
                    for k in range(4):
                        mm = pe.transpose(psum[:, b, k * n:(k + 1) * n], xbuf[0:n, t, (4 * j + k) * P:(4 * j + k + 1) * P],
                                          ident[0:n, 0:n])
                    banks.filled(mm, ("hT", t, j))

            def rows_slice(name, width):
                ring_wait(pe, name)
                w = ring_at(name, width)
                for t in range(NT):
                    if name == "A":
                        for j in range(2):
                            banks.wait_drained(pe, ("hT", t, j))
                    b = t % 2
                    banks.begin(pe, (name, t), b)
                    for k in range(KD):
                        mm = pe.matmul(psum[:, b, 0:width], hT[:, k, t * P:(t + 1) * P], w[:, k, :],
                                       start=(k == 0), stop=(k == KD - 1))
                    banks.filled(mm, (name, t))
                    if t == 0:
                        if name == "A":
                            for j in range(2):
                                banks.wait_drained(pe, ("hT", NT, j))
                        grouped((name, "s"), 2, width, w, hTs)
                    if t == 1:
                        banks.wait_drained(pe, (name, "s"))
                        banks.begin(pe, (name, "S"), 3)
                        mm = pe.matmul(psum[0:NS, 3, 0:width], C("sel_s"), G[:, 1, 0:width], start=True, stop=True)
                        banks.filled(mm, (name, "S"))
                last_use[name] = (name, NT - 1)

            def feature_block(name, w, rhs, b0, f, first=True, last=True):
                kk = w.shape[1]
                for k in range(kk):
                    for s in range(2):
                        mm = pe.matmul(psum[:, b0 + s, 0:HALF], w[:, k, f * P:(f + 1) * P],
                                       rhs[:, k, s * HALF:(s + 1) * HALF],
                                       start=(first and k == 0), stop=(last and k == kk - 1))
                return mm

            rows_slice("A", NA)

            pe.wait_ge(a_ready, 1)
            for t in range(NT):
                b = 4 + t % 2
                banks.begin(pe, ("qkiT", t), b)
                for j in range(3):
                    src = araw[:, t, j * P:(j + 1) * P] if j < 2 else ki_twice[:, t, :]
                    mm = pe.transpose(psum[:, b, j * P:(j + 1) * P], src, ident)
                banks.filled(mm, ("qkiT", t))
            pe.wait_ge(qi_dup_ready, 1)
            banks.begin(pe, "qi_sample", 4)
            for h in range(IH):
                mm = pe.transpose(psum[:, 4, h * NS:(h + 1) * NS], qi_twice[0:NS, h].rearrange("p c d -> p (c d)"),
                                  ident[0:NS, 0:NS])
            banks.filled(mm, "qi_sample")
            banks.begin(pe, "wi_sample", 5)
            for c in range(4):
                mm = pe.transpose(psum[:, 5, c * NS:(c + 1) * NS], wi_place[0:NS, c * P:(c + 1) * P], ident[0:NS, 0:NS])
            banks.filled(mm, "wi_sample")

            for qb in range(1, NT):
                L = (qb + 1) * P
                if qb == 1:
                    for t in range(NT):
                        banks.wait_drained(pe, ("qkiT", t))
                banks.begin(pe, ("dots", qb), 0, 1, 2, 3)
                for h in range(IH):
                    o = HD * (h % 2)
                    mm = pe.matmul(psum[:, h, 0:L], qiT[o:o + ID, h // 2, qb * P:(qb + 1) * P], kiT[o:o + ID, 0:L],
                                   start=True, stop=True)
                banks.filled(mm, ("dots", qb))

            for b in range(NS):
                pe.wait_ge(ki_in[b % 2], 16 * (b // 2 + 1))
                for j in range(2):
                    banks.begin(pe, ("kiT", b, j), 4 + j)
                    for k in range(4):
                        r = 4 * j + k
                        mm = pe.transpose(psum[:, 4 + j, k * P:(k + 1) * P], ki_pages[:, b % 2, r * P:(r + 1) * P], ident)
                    banks.filled(mm, ("kiT", b, j))
                q = 32 * (b % 4)
                for j in range(2):
                    banks.wait_drained(pe, ("kiT", b, j))
                    if b % 4 == 0 and j == 0:
                        banks.wait_drained(pe, "qi_sample")
                        banks.begin(pe, ("dotsS", b // 4), 0 + 2 * (b // 4), 1 + 2 * (b // 4))
                    mm = pe.matmul(psum[q:q + 32, 2 * (b // 4) + j, :], qi_lhs[:, b, :],
                                   ki_T[:, b % 2, j * 512:(j + 1) * 512], start=True, stop=True, tile_position=(0, q))
                if b % 4 < 3:
                    mm.then_inc(ki_used, 1)
                else:
                    banks.filled(mm, ("dotsS", b // 4))
            banks.wait_drained(pe, "wi_sample")
            banks.wait_drained(pe, ("dotsS", 0))
            banks.wait_drained(pe, ("dotsS", 1))
            banks.begin(pe, "scoresS", 0, 1, 2, 3)
            for par in range(2):
                for j in range(2):
                    for g in range(2):
                        mm = pe.matmul(psum[0:NS, 2 * par + j, :], wi_lhs[:, 2 * g + par, :],
                                       relu_s[:, g, j * 512:(j + 1) * 512], start=(g == 0), stop=(g == 1))
            banks.filled(mm, "scoresS")

            rows_slice("B", NB)
            rows_slice("C", NC)
            rows_slice("D", ND)
            def blocks(ring_name, key, rhs, n, b_of):
                ring_wait(pe, ring_name)
                w = ring_at(ring_name, 512)
                for f in range(n):
                    banks.begin(pe, (key, f), b_of(f), b_of(f) + 1)
                    mm = feature_block((key, f), w, rhs, b_of(f), f)
                    banks.filled(mm, (key, f))
                last_use[ring_name] = (key, n - 1)

            blocks("U", "U", hT, 4, lambda f: 2 * (f % 2))

            pe.wait_ge(q_ready, 1)
            for t in range(NT):
                b = 4 + t % 2
                banks.begin(pe, ("qT", t), b)
                for j in range(4):
                    mm = pe.transpose(psum[:, b, j * P:(j + 1) * P], qraw[:, t, j * P:(j + 1) * P], ident)
                banks.filled(mm, ("qT", t))
            pe.wait_ge(k_ready, 1)
            banks.begin(pe, "kT", 6)
            for t in range(NT):
                mm = pe.transpose(psum[:, 6, t * P:(t + 1) * P], kraw[:, t, :], ident)
            banks.filled(mm, "kT")
            banks.begin(pe, "qkT_s", 7)
            for j in range(5):
                src = qraw[0:NS, NT, j * P:(j + 1) * P] if j < 4 else kraw[0:NS, NT, :]
                mm = pe.transpose(psum[:, 7, j * NS:(j + 1) * NS], src, ident[0:NS, 0:NS])
            banks.filled(mm, "qkT_s")

            pe.wait_ge(vg_ready, 1)
            pe.wait_ge(ws_masked, 1)
            for j in range(4):
                b = 4 + j % 2
                banks.begin(pe, ("mix", j), b)
                for c in range(NT):
                    for par in range(2):
                        g = 2 * j + par
                        mm = pe.matmul(psum[GD * par:GD * par + GD, b, c * P:(c + 1) * P], vg[:, c, g * GD:(g + 1) * GD],
                                       wsT[:, g, :], start=True, stop=True, tile_position=(0, GD * par))
                banks.filled(mm, ("mix", j))
            banks.begin(pe, "vgT_s", 6)
            for j in range(4):
                mm = pe.transpose(psum[:, 6, j * NS:(j + 1) * NS], vg[0:NS, NT, j * P:(j + 1) * P], ident[0:NS, 0:NS])
            banks.filled(mm, "vgT_s")

            groups = [(qb, kv) for qb in range(NT) for kv in range(NKV)]

            def att_scores(g):
                qb, kv = groups[g]
                L = (qb + 1) * P
                o = HD * kv
                if g == 0:
                    for t in range(NT):
                        banks.wait_drained(pe, ("qT", t))
                    banks.wait_drained(pe, "kT")
                banks.begin(pe, ("att_s", g), 0, 1, 2, 3)
                for j in range(4):
                    mm = pe.matmul(psum[:, j, 0:L], qT[o:o + HD, j, qb * P:(qb + 1) * P], kT[o:o + HD, 0:L],
                                   start=True, stop=True)
                banks.filled(mm, ("att_s", g))

            def att_values(g):
                qb, kv = groups[g]
                pe.wait_ge(probs_ready, g + 1)
                for c in range(qb + 1):
                    b = 4 + c % 2
                    banks.begin(pe, ("probsT", g, c), b)
                    for j in range(4):
                        mm = pe.transpose(psum[:, b, j * P:(j + 1) * P], soft[g % 2][:, j, c * P:(c + 1) * P], ident)
                    banks.filled(mm, ("probsT", g, c))
                if kv == 0:
                    banks.begin(pe, ("att", qb), 6 + qb % 2)
                for c in range(qb + 1):
                    banks.wait_drained(pe, ("probsT", g, c))
                    mm = pe.matmul(psum[HD * kv:HD * kv + HD, 6 + qb % 2, :], araw[:, c, VV + HD * kv:VV + HD * kv + HD],
                                   probsT[:, c, :], start=(c == 0), stop=(c == qb), tile_position=(0, HD * kv))
                if kv == 1:
                    banks.filled(mm, ("att", qb))
                else:
                    mm.then_inc(values_done, 1)

            att_scores(0)
            for g in range(len(groups)):
                if g + 1 < len(groups):
                    att_scores(g + 1)
                att_values(g)

            for c in range(4):
                blocks(f"G{c}", f"G{c}", hT, 4, lambda f: 2 * (f % 2))

            pe.wait_ge(idx_ready, 1)
            banks.begin(pe, "idxT", 4)
            for h in range(2):
                mm = pe.transpose(psum[:, 4, h * NS:(h + 1) * NS], idx_f[0:NS, h * P:(h + 1) * P], ident[0:NS, 0:NS])
            banks.filled(mm, "idxT")
            pe.wait_ge(k_sel_in, 16 * 2 * NS)
            for b in range(NS):
                bank = 6 + b % 2
                banks.begin(pe, ("k_selT", b), bank)
                for h in range(2):
                    mm = pe.transpose(psum[:, bank, h * P:(h + 1) * P], k_sel[:, h * NS + b, :], ident)
                banks.filled(mm, ("k_selT", b))
            pe.wait_ge(key_bias_ready, 1)
            pe.wait_ge(q_lhs_ready, 2)
            spread = C("spread").rearrange("p (g n) -> p g n", g=2)
            for g in range(2):
                banks.begin(pe, ("att_ss", g), g)
                pe.matmul(psum[:, g, 0:TOPK_S + 1], spread[0:NS, g, :], key_bias[0:NS, :], start=True, stop=False,
                          skip_group_check=True)
                for i in range(4):
                    b = 4 * g + i
                    banks.wait_drained(pe, ("k_selT", b))
                    pe.matmul(psum[32 * i:32 * i + 32, g, 0:TOPK_S], q_lhs[:, b, :], k_selT[:, b, :],
                              start=False, stop=True, skip_group_check=True, tile_position=(0, 32 * i))
                    mm = pe.matmul(psum[32 * i:32 * i + 32, g, TOPK_S:TOPK_S + 1], q_lhs[:, b, :],
                                   kT[:, SEQ + b:SEQ + b + 1], start=False, stop=True, skip_group_check=True,
                                   tile_position=(0, 32 * i))
                banks.filled(mm, ("att_ss", g))
            pe.wait_ge(probs_s_ready, 1)
            banks.begin(pe, "probsT_s", 2)
            for g in range(2):
                for h in range(2):
                    a = 2 * g + h
                    mm = pe.transpose(psum[:, 2, a * P:(a + 1) * P], soft_s[:, g, h * P:(h + 1) * P], ident)
            banks.filled(mm, "probsT_s")
            banks.begin(pe, "new_probs", 3)
            rows_of = C("gather").rearrange("p (g b) -> p g b", g=2)
            for g in range(2):
                mm = pe.matmul(psum[0:NS, 3, 0:NH], rows_of[:, g, :], new_probs[:, g, :], start=(g == 0), stop=(g == 1))
            banks.filled(mm, "new_probs")
            pe.wait_ge(new_spread_ready, 1)
            pe.wait_ge(v_sel_in, 16 * 2 * NS)
            banks.wait_drained(pe, "probsT_s")
            banks.begin(pe, "att_samples", 4)
            pe.matmul(psum[:, 4, 0:NS * NH], araw[0:NS, NT, VV:VV + NKV * HD], new_spread[0:NS, :], start=True, stop=False,
                      skip_group_check=True)
            for b in range(NS):
                for h in range(2):
                    o = 32 * (b % 4)
                    mm = pe.matmul(psum[:, 4, b * NH:(b + 1) * NH], v_sel[:, h * NS + b, :],
                                   probsT_s[:, 2 * (b // 4) + h, o:o + NH], start=False, stop=True, skip_group_check=True)
            banks.filled(mm, "att_samples")

            ring_wait(pe, "WA")
            ring_wait(pe, "WG")
            pe.wait_ge(gm_ready, 1)
            banks.wait_drained(pe, "att_samples")
            for t in range(NT):
                banks.wait_drained(pe, ("att", t))
            for f in range(KD):
                for name, rhs, b in (("WA", attT, 0), ("WG", uT, 2)):
                    b += 4 * (f % 2)
                    banks.begin(pe, (name, f), b, b + 1)
                    mm = feature_block((name, f), ring_at(name, D), rhs, b, f)
                    banks.filled(mm, (name, f))
                    last_use[name] = (name, f)
            for c in range(4, 13):
                if c < 12:
                    ada_product(c)
                    last_use[f"ada{c}"] = ("ada", c)
                if c >= 5:
                    ada_spread(c - 1)

            pe.wait_ge(merged, KD)
            rows_slice("O0", 512)
            rows_slice("O1", 512)

            for i, (_, n, t) in enumerate(ORDER):
                pe.wait_ge(t2_ready, i + 1)
                for j in range(2):
                    b = 4 + j
                    banks.begin(pe, ("t2T", t, j), b)
                    for k in range(4):
                        mm = pe.transpose(psum[:, b, k * n:(k + 1) * n], t2[0:n, t, (4 * j + k) * P:(4 * j + k + 1) * P],
                                          ident[0:n, 0:n])
                    banks.filled(mm, ("t2T", t, j))
            for t in range(T5):
                for j in range(2):
                    banks.wait_drained(pe, ("t2T", t, j))
            pe.wait_ge(router_in, 32)
            banks.begin(pe, "logits", 0, 1)
            for k in range(KD):
                for s in range(2):
                    mm = pe.matmul(psum[0:NEG + NE, s, 0:HALF], w_router[:, k, :], hT[:, k, s * HALF:(s + 1) * HALF],
                                   start=(k == 0), stop=(k == KD - 1))
            banks.filled(mm, "logits")
            banks.wait_drained(pe, "logits")
            banks.begin(pe, "logits_rows", 2)
            for t in range(T5):
                n = P if t < NT else NS
                mm = pe.transpose(psum[0:n, 2, t * 36:t * 36 + 36], logits_T[0:36, t * P:t * P + n], ident[0:36, 0:36])
            banks.filled(mm, "logits_rows")
            pe.wait_ge(chosen_ready, 1)
            banks.begin(pe, "places", 3)
            for t in range(T5):
                o = slice(t * NE, (t + 1) * NE)
                pe.matmul(psum[:, 3, o], C("before"), chosen[:, t, :], start=True, stop=False, skip_group_check=True)
                pe.matmul(psum[:, 3, o], C("ones"), before_sum[:, t, :], start=False, stop=True, skip_group_check=True)
            mm = pe.matmul(psum[:, 3, T5 * NE:(T5 + 1) * NE], C("ones"), before_sum[:, T5, :], start=True, stop=True)
            banks.filled(mm, "places")
            pe.wait_ge(tables_hot_ready, 1)
            banks.begin(pe, "tables", 4)
            for a in range(2 * T5):
                mm = pe.matmul(psum[:, 4, 0:2 * N_ITEMS], slot_hot[:, a, :], item_hot[:, a, :],
                               start=(a == 0), stop=(a == 2 * T5 - 1))
            banks.filled(mm, "tables")

            def x_transposes(p, full):
                for k in range(KD):
                    mm = pe.transpose(psum[:, p, k * SB:(k + 1) * SB], x_rows[0:SB, p, k * P:(k + 1) * P],
                                      ident[0:SB, 0:SB])
                mm.then_inc(full, 1)

            def gate_up(p, w, full):
                for k in range(KD):
                    for half in range(2):
                        col = DE * (1 - half)
                        mm = pe.matmul(psum[SB * half:SB * half + SB, 2 + p, 0:DE], x_T[:, p, k, :],
                                       w[:, k, col:col + DE], start=(k == 0), stop=(k == KD - 1),
                                       tile_position=(0, SB * half))
                mm.then_inc(full, 1)

            def hidden_transposes(p, full):
                for f in range(2):
                    mm = pe.transpose(psum[:, 4 + p, f * SB:(f + 1) * SB], hidden[0:SB, p, f * P:(f + 1) * P],
                                      ident[0:SB, 0:SB])
                mm.then_inc(full, 1)

            def down(p, w, full):
                for f in range(2):
                    for half in range(2):
                        mm = pe.matmul(psum[SB * half:SB * half + SB, 6 + p, :], hidden_T[:, p, f, :],
                                       w[:, f, 512 * half:512 * half + 512], start=(f == 0), stop=(f == 1),
                                       tile_position=(0, SB * half))
                mm.then_inc(full, 1)

            for name in ("logits", "logits_rows", "places", "tables"):
                banks.wait_drained(pe, name)
            pe.wait_ge(x_got[0], 16)
            x_transposes(0, xT_full)

            def pe_items(i, first):
                for k in range(4):
                    e, p = i * 4 + k, k % 2
                    pe.wait_ge(w_got[k], i * 16 + 16)
                    pe.wait_ge(xT_out, e + 1)
                    if not (first and k < 2):
                        pe.wait_ge(hidden_done, e - 1)
                    gate_up(p, w_gu[k], gu_full)
                    if not (first and k < 1):
                        pe.wait_ge(xT_out, e)
                    lone_wait(pe, x_got[1 - p], i * 32 + 16 * ((k + 1) // 2) + 16, pe_passed)
                    x_transposes(1 - p, xT_full)
                    if not (first and k < 2):
                        pe.wait_ge(hT_out, e - 1)
                    lone_wait(pe, hidden_done, e + 1, pe_passed)
                    hidden_transposes(p, hT_full)
                    pe.wait_ge(hT_out, e + 1)
                    if not (first and k < 2):
                        pe.wait_ge(y_out, e - 1)
                    down(p, w_dn[k], y_full)

            pe_items(0, True)
            with pe.Fori(1, NE // 4) as i:
                pe_items(i, False)

            pe.wait_ge(xT_out, NE + 1)
            pe.wait_ge(y_out, NE)
            pe.wait_ge(pe_passed, 2 * NE)
            total = pe.value_load(over_total[0:1, 0:1], min_val=0, max_val=N_OVER)
            with pe.Fori(0, N_OVER) as j:
                with pe.If(j < total):
                    lone_wait(pe, o_x, j * 16 + 16, o_pe_passed)
                    x_transposes(0, o_xT_full)
                    pe.wait_ge(o_w, j * 16 + 16)
                    pe.wait_ge(o_xT_out, j + 1)
                    gate_up(0, w_gu[0], o_gu)
                    lone_wait(pe, o_hidden, j + 1, o_pe_passed)
                    hidden_transposes(0, o_hT_full)
                    pe.wait_ge(o_hT_out, j + 1)
                    down(0, w_dn[0], o_y)
                    pe.wait_ge(o_pe_passed, j * 2 + 2)

        @block.sync
        def _(sp):
            sp.dma_start(const[:, :], io["consts"]).then_inc(const_in, 16)
            sp.dma_start(c_T[:, :, :], io["c_T"].rearrange("p (k n) -> p k n", k=KD)).then_inc(c_in, 16)
            for n, (name, size) in enumerate(STREAM):
                if n == 1:
                    sp.dma_start(bias1, io["b_ada"][0:4, :].partition_broadcast(P)).then_inc(bias_in, 16)
                    sp.dma_start(gain1, io["norm_mix_g"].partition_broadcast(P)).then_inc(bias_in, 16)
                if n == 2:
                    sp.dma_start(gains[:, :], io["head_gains"].partition_broadcast(P)).then_inc(bias_in, 16)
                if n >= RING:
                    banks.wait_full(sp, last_use[STREAM[n - RING][0]])
                sp.dma_start(ring[:, n % RING, 0:size], io["stream"][n, :, 0:size]).then_inc(ring_full[n % RING], 16)
            def expert_src(e):
                return io["experts"].rearrange("e p n -> (e p) n")[bass.ds(e * P, P), :]

            def load_w(k, e):
                sp.dma_start(expert_w[k], expert_src(e)).then_inc(w_got[k], 16)

            banks.wait_full(sp, last_use["O1"])
            load_w(0, 0)
            load_w(1, 1)
            sp.wait_ge(t2_ready, T5)
            load_w(2, 2)
            for t in range(T5):
                for j in range(2):
                    banks.wait_drained(sp, ("t2T", t, j))
            sp.wait_ge(t2_stored, 16 * T5)
            load_w(3, 3)
            sp.wait_ge(over_zeroed, 16)
            def store_item(e, p, done):
                for half in range(2):
                    dst = io["expert_rows"][bass.ds(e * SB, SB), 512 * half:512 * half + 512]
                    sp.dma_start(dst, y_rows[SB * half:SB * half + SB, p, :]).then_inc(done, 16)

            def sp_items(i, reload):
                for k in range(4):
                    e = i * 4 + k
                    if reload:
                        sp.wait_ge(y_full, e + 1)
                        load_w(k, e + 4)
                    sp.wait_ge(y_out, e + 1)
                    store_item(e, k % 2, y_stored[k % 2])

            sp_items(0, True)
            with sp.Fori(1, NE // 4 - 1) as i:
                sp_items(i, True)
            sp_items(NE // 4 - 1, False)
            for p in range(2):
                sp.wait_ge(y_stored[p], 16 * NE)
            total = sp.value_load(over_total[0:1, 0:1], min_val=0, max_val=N_OVER)
            sp.sem_inc(o_stored, 1)
            with sp.Fori(0, N_OVER) as j:
                with sp.If(j < total):
                    e = sp.value_load(over_expert[0:1, bass.ds(j, 1)], min_val=0, max_val=NE - 1)
                    sp.dma_start(expert_w[0], expert_src(e)).then_inc(o_w, 16)
                    sp.wait_ge(o_y_out, j + 1)
                    store_item(j + NE, 0, o_stored)
            sp.wait_ge(o_stored, total * 32 + 1)
            sp.sem_inc(experts_done, 1)
            for i, (_, n, t) in enumerate([(t, P if t < NT else NS, t) for t in range(T5)]):
                sp.wait_ge(y_ready, i + 1)
                dst = io["y_p"][t * P:(t + 1) * P, :] if t < NT else io["y_s"]
                sp.dma_start(dst, x2[0:n, t, :]).then_inc(y_outs, 16)
            sp.wait_ge(y_outs, 16 * T5)

        @block.gpsimd
        def _(pool):
            lane = Lane(pool, pool_lane)

            def rsqrt(n_asked, out, in_, width):
                pool.wait_ge(rstd_asked, n_asked)
                pool.tensor_tensor(out, in_, minus_half[:, 0:width], ALU.pow).then_inc(rstd_ready, 1)

            def store(dst, src):
                pool.dma_start(dst, src).then_inc(outs, 16)
                n_outs[0] += 1

            for t in range(NT):
                pool.dma_start(xbuf[:, t, :], io["x_prompt"][t * P:(t + 1) * P, :]).then_inc(x_in[t], 16)
            pool.dma_start(xbuf[0:NS, NT, :], io["x_sample"]).then_inc(x_in[NT], 16)
            pool.dma_start(page_rep, io["page_rep"]).then_inc(pages_in, 16)
            pool.dma_start(ln, io["ln"].partition_broadcast(P)).then_inc(ln_in, 16)
            pool.dma_start(wsT, io["ws_T"].rearrange("p (g t) -> p g t", g=GG)).then_inc(ws_in, 16)
            gm_b = io["gm_b"].rearrange("(j c) t -> c j t", c=2)
            for par in range(2):
                rows = slice(GD * par, GD * par + GD)
                pool.dma_start(bT[rows], gm_b[par].partition_broadcast(GD)).then_inc(gmlp_in, 16)
                pool.dma_start(gm_w0[rows], io["ws_00"][par].partition_broadcast(GD)).then_inc(gmlp_in, 16)
            pool.wait_ge(ws_in, 16)
            pool.affine_select(out=wsT, in_=wsT, pattern=[[0, GG], [1, CHUNK]], compare_op=ALU.is_ge, fill=0.0,
                               base=0, channel_multiplier=-1).then_inc(ws_masked, 1)
            pool.wait_ge(zeroed, 1)
            rsqrt(1, rstd, ssq, 5)

            pool.wait_ge(page_rows_ready, 1)
            banks.wait_drained(pool, ("hT", NT, 1))
            for b in range(NS):
                if b >= 2:
                    banks.wait_full(pool, ("kiT", b - 2, 1))
                pool.indirect_dma_start(ki_pages[:, b % 2, :], None, io["cache_ki"],
                                        bass.IndirectOffsetOnAxis(page_rows[:, b:b + 1], 0)).then_inc(ki_in[b % 2], 16)
                if b == 1:
                    rsqrt(2, ki_r, ki_ms, 5)
            pool.wait_ge(a_ready, 1)
            store(io["new_ki_p"].rearrange("(t p) d -> p t d", p=P), araw[:, 0:NT, KI:KI + ID])
            store(io["new_ki_s"], araw[0:NS, NT, KI:KI + ID])
            store(io["new_v_p"].rearrange("(t p) d -> p t d", p=P), araw[:, 0:NT, VV:VV + P])
            store(io["new_v_s"], araw[0:NS, NT, VV:VV + P])
            over_rows = io["expert_rows"][NE * SB:, :].rearrange("(p a) (b n) -> p (a b) n", p=P, n=256)
            pool.dma_start(over_rows, spread_dim(zeros[:, :], 1, over_rows.shape[1])).then_inc(over_zeroed, 16)
            rsqrt(3, q_r, q_ms, 40)
            rsqrt(4, k_r, k_ms, 10)
            pool.wait_ge(k_ready, 1)
            store(io["new_k_p"].rearrange("(t p) d -> p t d", p=P), kraw[:, 0:NT, :])
            store(io["new_k_s"], kraw[0:NS, NT, :])
            rsqrt(5, vg_r, mu_var[:, :, 1], 5)
            pool.wait_ge(vg_ready, 1)
            store(io["new_vg_s"], vg[0:NS, NT, :])
            pool.dma_start(pages_i, io["pages"].partition_broadcast(P)).then_inc(pages_all_in, 16)
            for qb in range(NT):
                banks.wait_drained(pool, ("att", qb))
            pool.wait_ge(sel_rows_ready, 1)
            for dst, src, got in ((k_sel, "cache_k", k_sel_in), (v_sel, "cache_v", v_sel_in)):
                for a in range(2 * NS):
                    pool.indirect_dma_start(dst[:, a, :], None, io[src], bass.IndirectOffsetOnAxis(sel_rows[:, a:a + 1], 0))\
                        .then_inc(got, 16)
            pool.wait_ge(merged, KD)
            pool.dma_start(bias2, io["b_ada"][4:12, :].partition_broadcast(P)).then_inc(late_in, 16)
            pool.dma_start(gain2, io["norm_ffn_g"].partition_broadcast(P)).then_inc(late_in, 16)
            for t in range(NT):
                pool.dma_start(x2[:, t, :], io["x_prompt"][t * P:(t + 1) * P, :]).then_inc(x2_in, 16)
            pool.dma_start(x2[0:NS, NT, :], io["x_sample"]).then_inc(x2_in, 16)
            pool.dma_start(w_router, io["w_router"].rearrange("p (k n) -> p k n", k=KD)).then_inc(router_in, 16)
            pool.dma_start(b_router, io["b_router"].partition_broadcast(P)).then_inc(router_in, 16)
            rsqrt(6, rstd, ssq, 5)
            pool.wait_ge(t2_stored, 16 * T5)
            pool.wait_ge(tables_ready, 1)
            for e in range(NE + 1):
                if e >= 2:
                    pool.wait_ge(xT_full, e - 1)
                pool.indirect_dma_start(x_rows[0:SB, e % 2, :], None, io["t2_rows"],
                                        bass.IndirectOffsetOnAxis(token_tab[0:SB, e:e + 1], 0)).then_inc(x_got[e % 2], 16)
            pool.wait_ge(xT_full, NE + 1)
            total = pool.value_load(over_total[0:1, 0:1], min_val=0, max_val=N_OVER)
            with pool.Fori(0, N_OVER) as j:
                with pool.If(j < total):
                    pool.tensor_copy(over_token[0:SB], token_tab[0:SB, bass.ds(j + NE, 1)]).then_inc(o_token, 1)
                    lone_wait(pool, o_token, j + 1, o_pool_passed)
                    pool.indirect_dma_start(x_rows[0:SB, 0, :], None, io["t2_rows"],
                                            bass.IndirectOffsetOnAxis(over_token[0:SB], 0)).then_inc(o_x, 16)
                    pool.wait_ge(o_pool_passed, j + 1)
                    pool.wait_ge(o_xT_full, j + 1)
            pool.wait_ge(experts_done, 1)
            pool.wait_ge(y_full, NE)
            for t in range(T5):
                n = P if t < NT else NS
                if t >= 2:
                    pool.wait_ge(picked_used, t - 1)
                for c in range(2):
                    a = c * T5 + t
                    pool.indirect_dma_start(picked[0:n, t % 2, c, :], None, io["expert_rows"],
                                            bass.IndirectOffsetOnAxis(rank_i[0:n, a:a + 1], 0)).then_inc(picked_in[t % 2], 16)
            pool.wait_ge(outs, 16 * n_outs[0])

        @block.scalar
        def _(act):
            lane = Lane(act, scalar_lane)
            act.wait_ge(c_in, 16)
            act.activation(c_T[:, :, :], c_T[:, :, :], ACT.Silu).then_inc(c_silu, 1)

            def evac(name, pairs, func=ACT.Copy, scale=1.0):
                banks.wait_full(act, name)
                for out, in_ in pairs:
                    ins = act.activation(out, in_, func, scale=scale)
                banks.drained(ins, name)

            def ada_out(c):
                if c >= 2:
                    banks.wait_full(act, ("adaS", c - 2))
                evac(("ada", c), [(G[:, c % 2, :], psum[:, c % 2, :])])

            act.wait_ge(zeroed, 1)
            for t in range(NT + 1):
                n = P if t < NT else NS
                act.wait_ge(x_in[t], 16)
                lane.wait()
                ins = act.activation(junk[0:n, :], xbuf[0:n, t, :], ACT.Square, accum_out=ssq[0:n, t:t + 1])
                lane.mark(ins) if t < NT else ins.then_inc(ssq_ready, 1)
            for c in range(4):
                ada_out(c)
            for t in range(NT):
                for j in range(2):
                    evac(("hT", t, j), [(hT[:, 4 * j:4 * j + 4, t * P:(t + 1) * P],
                                         psum[:, 6 + j, :].rearrange("p (k n) -> p k n", k=4))])
            for j in range(2):
                src = psum[:, 6 + j, 0:4 * NS].rearrange("p (k n) -> p k n", k=4)
                evac(("hT", NT, j), [(hT[:, 4 * j:4 * j + 4, SEQ:TOK], src), (hTs[:, 4 * j:4 * j + 4, 0:NS], src)])

            def rows_out(name, outs_of, gelu_from=None):
                def go(part, rows, t):
                    b = {"S": 3}.get(part, t % 2)
                    banks.wait_full(act, (name, part))
                    for dst, o, w, func in outs_of:
                        ins = act.activation(dst[0:rows, t, :], psum[0:rows, b, o:o + w], func)
                    banks.drained(ins, (name, part))
                width = sum(w for _, _, w, _ in outs_of)
                go(0, P, 0)
                evac((name, "s"), [(G[:, 1, 0:width], psum[:, 2, 0:width])])
                go(1, P, 1)
                go("S", NS, NT)
                go(2, P, 2)
                go(3, P, 3)

            banks.wait_full(act, ("adaS", 3))
            banks.wait_full(act, ("adaS", 2))
            act.wait_ge(zeroed, 2)
            rows_out("A", [(araw, 0, NA, ACT.Copy)])
            for t in range(NT):
                b = 4 + t % 2
                evac(("qkiT", t), [
                    (qiT[:, :, t * P:(t + 1) * P], psum[:, b, 0:2 * P].rearrange("p (j n) -> p j n", j=2)),
                    (kiT[:, t * P:(t + 1) * P], psum[:, b, 2 * P:3 * P])])
            src = psum[:, 4, 0:IH * NS].rearrange("p (h b) -> p b h", h=IH)
            act.wait_ge(qi_lhs_ready, 1)
            evac("qi_sample", [(qi_lhs[0:ID, :, 0:IH], src[0:ID]), (qi_lhs[ID:P, :, IH:2 * IH], src[ID:P])])
            evac("wi_sample", [(wi_lhs, psum[:, 5, 0:4 * NS].rearrange("p (c b) -> p c b", c=4))])
            index_scale = ID ** -0.5 * IH ** -0.5
            for qb in range(1, NT):
                L = (qb + 1) * P
                if qb > 1:
                    act.wait_ge(relu_p_read, qb - 1)
                evac(("dots", qb), [(relu_p[:, :, 0:L], psum[:, 0:4, 0:L])], ACT.Relu, index_scale)
            for b in range(NS):
                if b >= 2 and (b - 2) % 4 == 3:
                    banks.wait_full(act, ("dotsS", (b - 2) // 4))
                elif b >= 2:
                    act.wait_ge(ki_used, (b - 1) - (b - 1) // 4)
                for j in range(2):
                    evac(("kiT", b, j), [(ki_T[:, b % 2, j * 512:(j + 1) * 512], psum[:, 4 + j, :])])
                if b % 4 == 3:
                    g = b // 4
                    evac(("dotsS", g), [(relu_s[:, g, :].rearrange("p (j n) -> p j n", j=2), psum[:, 2 * g:2 * g + 2, :])],
                         ACT.Relu, index_scale)
            banks.wait_full(act, "scoresS")
            view = scores[0:NS, 0:PAST].rearrange("s (n r e) -> s e r n", r=8, e=2)
            for par in range(2):
                ins = act.activation(view[:, par], psum[0:NS, 2 * par:2 * par + 2, :].rearrange("s j (r n) -> s (j r) n", r=4),
                                     ACT.Copy)
            banks.drained(ins, "scoresS")
            rows_out("B", [(qraw, 0, NB, ACT.Copy)])
            rows_out("C", [(kraw, 0, NKV * HD, ACT.Copy), (vg[:, :, 0:VG0], NKV * HD, VG0, ACT.Gelu_apprx_tanh)])
            rows_out("D", [(vg[:, :, VG0:GM], 0, ND, ACT.Gelu_apprx_tanh)])
            for f in range(4):
                b = 2 * (f % 2)
                evac(("U", f), [(halves(uT[:, f, :]), pair(b))], ACT.Gelu_apprx_tanh)
            for t in range(NT):
                if t == 0:
                    banks.wait_drained(act, "scoresS")
                evac(("qT", t), [(qT[:, :, t * P:(t + 1) * P], psum[:, 4 + t % 2, :].rearrange("p (j n) -> p j n", j=4))])
            evac("kT", [(kT[:, 0:SEQ], psum[:, 6, :])])
            evac("qkT_s", [(qT[:, :, SEQ:TOK], psum[:, 7, 0:4 * NS].rearrange("p (j n) -> p j n", j=4)),
                           (kT[:, SEQ:TOK], psum[:, 7, 4 * NS:5 * NS])])
            for g, (qb, kv) in enumerate([(qb, kv) for qb in range(NT) for kv in range(NKV)]):
                L = (qb + 1) * P
                act.wait_ge(max_ready, g + 1)
                for j in range(4):
                    s_j = soft[g % 2][:, j, 0:L]
                    ins = act.activation(s_j, s_j, ACT.Exp, bias=mx4[g % 2][:, j:j + 1], accum_out=sum4[g % 2][:, j:j + 1])
                ins.then_inc(exp_ready, 1)
                for c in range(qb + 1):
                    if g and kv == 1:
                        act.wait_ge(values_done, qb + 1)
                    elif g:
                        banks.wait_full(act, ("att", qb - 1))
                    evac(("probsT", g, c), [(probsT[:, c, :], psum[:, 4 + c % 2, :])])
                if kv == 1:
                    evac(("att", qb), [(attT[:, :, qb * P:(qb + 1) * P],
                                        psum[:, 6 + qb % 2, :].rearrange("p (j n) -> p j n", j=4))])
            act.wait_ge(vg_ready, 1)
            for c in range(4):
                for f in range(4):
                    to = 2 * c + f if f < 2 else KD + 2 * c + f - 2
                    evac((f"G{c}", f), [(halves(gates[:, to, :]), pair(2 * (f % 2)))], ACT.Sigmoid)
            for b in range(NS):
                if b == 0:
                    act.wait_ge(probs_ready, 8)
                evac(("k_selT", b), [(k_selT[:, b, :], psum[:, 6 + b % 2, 0:2 * P])])
            act.wait_ge(max_s_ready, 1)
            for g in range(2):
                ins = act.activation(soft_s[:, g, :], psum[:, g, 0:TOPK_S + 1], ACT.Exp, bias=mx2[:, g:g + 1],
                                     scale=HD ** -0.5, accum_out=sum2[:, g:g + 1])
                banks.drained(ins, ("att_ss", g))
            evac("probsT_s", [(probsT_s, psum[:, 2, :].rearrange("p (a n) -> p a n", n=P))])
            src = psum[:, 4, 0:NS * NH].rearrange("p (b v j) -> p v j b", b=NS, v=NKV)
            evac("att_samples", [(attT[0:HD, :, SEQ:TOK], src[0:HD, 0]), (attT[HD:P, :, SEQ:TOK], src[HD:P, 1])])
            banks.wait_full(act, ("WG", KD - 1))
            for c in range(4, 12):
                ada_out(c) if c >= 6 else evac(("ada", c), [(G[:, c % 2, :], psum[:, c % 2, :])])
            for name in ("O0", "O1"):
                if name == "O0":
                    banks.wait_full(act, ("adaS", 10))
                    banks.wait_full(act, ("adaS", 11))
                else:
                    banks.wait_full(act, ("O0", "S"))
                evac((name, "s"), [(G[:, 1, :], psum[:, 2, :])])
            for i, (_, n, t) in enumerate(ORDER):
                act.wait_ge(x2_ready, i + 1)
                lane.wait()
                ins = act.activation(junk2[0:n, :], x2[0:n, t, :], ACT.Square, accum_out=ssq[0:n, t:t + 1])
                lane.mark(ins) if i < NT else ins.then_inc(ssq2_ready, 1)
            banks.wait_full(act, ("O1", 3))
            for i, (_, n, t) in enumerate(ORDER):
                cols = slice(t * P, t * P + n)
                for j in range(2):
                    evac(("t2T", t, j), [(hT[:, 4 * j:4 * j + 4, cols],
                                          psum[:, 4 + j, 0:4 * n].rearrange("p (k n) -> p k n", k=4))])
                dst = io["t2_rows"][t * P:t * P + n, :]
                act.dma_start(dst, t2[0:n, t, :]).then_inc(t2_stored, 16)
            evac("logits", [(halves(logits_T[0:NEG + NE]), psum[0:NEG + NE, 0:2, 0:HALF])])
            act.wait_ge(g_diff_ready, 1)
            act.activation(g_exp, g_tmp, ACT.Exp).then_inc(g_exp_ready, 1)
            act.wait_ge(e_diff_ready, 1)
            act.activation(e_ratio, e_ratio, ACT.Exp).then_inc(e_exp_ready, 1)

            def x_out(p, done):
                act.activation(x_T[:, p], psum[:, p, :].rearrange("p (k n) -> p k n", k=KD), ACT.Copy).then_inc(done, 1)

            def silu(p, done):
                act.activation(silu_g[0:SB, p, :], psum[SB:2 * SB, 2 + p, 0:DE], ACT.Silu).then_inc(done, 1)

            act.wait_ge(tables_ready, 1)
            act.wait_ge(xT_full, 1)
            x_out(0, xT_out)

            def act_items(i, first):
                for k in range(4):
                    e, p = i * 4 + k, k % 2
                    act.wait_ge(gu_full, e + 1)
                    if not (first and k < 2):
                        act.wait_ge(hidden_done, e - 1)
                    silu(p, silu_done)
                    act.wait_ge(xT_full, e + 2)
                    if not (first and k < 1):
                        act.wait_ge(gu_full, e)
                    x_out(1 - p, xT_out)

            act_items(0, True)
            with act.Fori(1, NE // 4) as i:
                act_items(i, False)
            act.wait_ge(gu_full, NE)
            total = act.value_load(over_total[0:1, 0:1], min_val=0, max_val=N_OVER)
            with act.Fori(0, N_OVER) as j:
                with act.If(j < total):
                    act.wait_ge(o_xT_full, j + 1)
                    x_out(0, o_xT_out)
                    act.wait_ge(o_gu, j + 1)
                    silu(0, o_silu)

        @block.vector
        def _(dve):
            lane = Lane(dve, vector_lane)
            asked = [0]

            def rsqrt_of(ms, sums, count, wait=True):
                asked[0] += 1
                dve.tensor_scalar(ms, sums, 1.0 / count, EPS, ALU.mult, ALU.add).then_inc(rstd_asked, 1)
                if wait:
                    dve.wait_ge(rstd_ready, asked[0])

            def rope(rope_tmp, view, heads):
                nt = view.shape[1]
                t1 = rope_tmp[:, 0:nt * heads * ROT].rearrange("p (t h r) -> p t h r", t=nt, h=heads)
                t2 = rope_tmp[:, nt * heads * ROT:2 * nt * heads * ROT].rearrange("p (t h r) -> p t h r", t=nt, h=heads)
                cos = spread_dim(C("cos").rearrange("p (t r) -> p t r", r=ROT), 2, heads)
                sin = spread_dim(C("sin").rearrange("p (t r) -> p t r", r=ROT), 2, heads)
                half = ROT // 2
                dve.tensor_tensor(t1, view[:, :, :, 0:ROT], cos, ALU.mult)
                dve.tensor_tensor(t2[:, :, :, 0:half], view[:, :, :, half:ROT], sin[:, :, :, 0:half], ALU.mult)
                lane.then(dve.tensor_tensor(t2[:, :, :, half:ROT], view[:, :, :, 0:half], sin[:, :, :, half:ROT], ALU.mult))
                return dve.tensor_tensor(view[:, :, :, 0:ROT], t1, t2, ALU.add)

            lane.then(dve.memset(stat[:, 16:212], 0.0))
            dve.memset(minus_half, -0.5).then_inc(zeroed, 1)
            dve.memset(hTs[:, :, :], 0.0)
            dve.memset(zeros[:, :], 0.0)
            dve.memset(araw[:, NT, :], 0.0)
            dve.memset(kraw[:, NT, :], 0.0)
            dve.memset(qi_lhs, 0.0).then_inc(qi_lhs_ready, 1)
            dve.wait_ge(pages_in, 16)
            dve.wait_ge(const_in, 16)
            dve.tensor_scalar(page_rows, page_rep, float(PAGE // 16), C("page_seg"), ALU.mult, ALU.add)\
               .then_inc(page_rows_ready, 1)
            dve.wait_ge(ssq_ready, 1)
            rsqrt_of(ssq, ssq, D, wait=False)
            dve.wait_ge(bias_in, 48)
            for c in range(4):
                m, half = c // 2, slice(512 * (c % 2), 512 * (c % 2) + 512)
                for g, name, b, rows in ((0, "adaP", 2 + c % 2, P), (1, "adaS", 4 + c % 2, NS)):
                    banks.wait_full(dve, (name, c))
                    out = mod1[0:rows, g, m, half]
                    if m == 0:
                        banks.drained(dve.tensor_tensor(out, psum[0:rows, b, :], bias1[0:rows, c, :], ALU.add), (name, c))
                    else:
                        banks.drained(dve.scalar_tensor_tensor(out, psum[0:rows, b, :], 1.0, bias1[0:rows, c, :],
                                                               ALU.add, ALU.add), (name, c))
                        banks.wait_drained(dve, (name, c))
                        lane.mark(dve.tensor_tensor(out, out, gain1[0:rows, half], ALU.mult))
            lane.wait()
            dve.wait_ge(rstd_ready, 1)
            for t in range(NT + 1):
                rows, g = (P, 0) if t < NT else (NS, 1)
                xt = xbuf[0:rows, t, :]
                lane.then(dve.scalar_tensor_tensor(xt, xt, rstd[0:rows, t:t + 1], mod1[0:rows, g, 1, :], ALU.mult, ALU.mult))
                dve.tensor_tensor(xt, xt, mod1[0:rows, g, 0, :], ALU.add).then_inc(h_ready, 1)
            dve.memset(vg[:, NT, :], 0.0)
            dve.memset(qraw[:, NT, :], 0.0).then_inc(zeroed, 1)

            for part in (0, 1, "S", 2, 3):
                banks.wait_drained(dve, ("A", part))
            ki = araw[:, :, KI:KI + ID]
            sq = ki_twice[:, :, 0:ID]
            lane.then(dve.tensor_tensor(sq, ki, ki, ALU.mult))
            lane.then(dve.tensor_reduce(ki_ms, sq, AX_X, ALU.add))
            rsqrt_of(ki_ms, ki_ms, ID)
            lane.then(dve.tensor_tensor(ki, ki, spread_dim(ki_r, 2, ID), ALU.mult))
            lane.then(dve.tensor_tensor(ki, ki, spread_dim(gains[:, 2 * HD:3 * HD], 1, NT + 1), ALU.mult))
            lane.then(rope(work, araw[:, :, 0:WI].rearrange("p t (h d) -> p t h d", d=ID), IH + 1))
            dve.tensor_copy(ki_twice.rearrange("p t (c d) -> p t c d", c=2), spread_dim(ki, 2, 2)).then_inc(a_ready, 1)
            qi_s = araw[0:NS, NT, QI:KI].rearrange("p (h d) -> p h d", h=IH)
            wi_s = araw[0:NS, NT, WI:VV]
            dve.tensor_copy(qi_twice[0:NS], spread_dim(qi_s, 2, 2))
            dve.tensor_tensor(wi_place[0:NS].rearrange("p (c h) -> p c h", h=IH),
                              C("place")[0:NS].rearrange("p (c h) -> p c h", h=IH), spread_dim(wi_s, 1, P), ALU.mult)\
               .then_inc(qi_dup_ready, 1)

            prod = work[0:NS, 0:IH * ID].rearrange("p (h d) -> p h d", h=IH)
            nd = new_dots[0:NS]
            lane.then(dve.tensor_tensor(prod, qi_s, spread_dim(araw[0:NS, NT, KI:KI + ID], 1, IH), ALU.mult))
            lane.then(dve.tensor_reduce(nd, prod, AX_X, ALU.add))
            lane.then(dve.tensor_scalar(nd, nd, ID ** -0.5 * IH ** -0.5, 0.0, ALU.mult, ALU.max))
            lane.then(dve.tensor_tensor(nd, nd, wi_s, ALU.mult))
            lane.then(dve.tensor_reduce(scores[0:NS, PAST:PAST + 1], nd, AX_X, ALU.add))

            w_at = {1: 0, 2: 256, 3: 640}
            for qb in range(1, NT):
                L = (qb + 1) * P
                s = work[:, w_at[qb]:w_at[qb] + L]
                banks.wait_drained(dve, ("dots", qb))
                lane.then(dve.tensor_scalar(s, relu_p[:, 0, 0:L], araw[:, qb, WI:WI + 1], None, ALU.mult))
                for h in range(1, IH):
                    ins = dve.scalar_tensor_tensor(s, relu_p[:, h, 0:L], araw[:, qb, WI + h:WI + h + 1], s,
                                                   ALU.mult, ALU.add)
                    if h < IH - 1:
                        lane.then(ins)
                ins.then_inc(relu_p_read, 1)
                dve.wait_ge(relu_p_read, qb)
                lane.mark(dve.tensor_tensor(s[:, L - P:L], s[:, L - P:L], C("causal"), ALU.add))
            lane.wait()
            for _ in range(TOPK_P // 8):
                for qb in range(1, NT):
                    lane.mark(dve.max(top8[:, 8 * (qb - 1):8 * qb], work[:, w_at[qb]:w_at[qb] + (qb + 1) * P]))
                lane.wait()
                for qb in range(1, NT):
                    s = work[:, w_at[qb]:w_at[qb] + (qb + 1) * P]
                    lane.mark(dve.match_replace(s, top8[:, 8 * (qb - 1):8 * qb], s, TAKEN))
                lane.wait()
            lane.then(dve.tensor_scalar(work, work, TAKEN / 2, -BIG, ALU.is_gt, ALU.mult))

            def norm_heads(raw, heads, ms, r, gain):
                view = raw.rearrange("p t (h d) -> p (t h) d", d=HD)
                sq = norm_tmp[:, 0:(NT + 1) * heads * HD].rearrange("p (a d) -> p a d", d=HD)
                lane.then(dve.tensor_tensor(sq, view, view, ALU.mult))
                lane.then(dve.tensor_reduce(ms, sq, AX_X, ALU.add))
                rsqrt_of(ms, ms, HD)
                lane.then(dve.tensor_tensor(view, view, spread_dim(r, 2, HD), ALU.mult))
                lane.then(dve.tensor_tensor(view, view, spread_dim(gain, 1, (NT + 1) * heads), ALU.mult))
                return rope(norm_tmp, raw.rearrange("p t (h d) -> p t h d", d=HD), heads)

            banks.wait_drained(dve, "scoresS")
            for part in (0, 1, "S", 2, 3):
                banks.wait_drained(dve, ("B", part))
            norm_heads(qraw, NH, q_ms, q_r, gains[:, 0:HD]).then_inc(q_ready, 1)
            for part in (0, 1, "S", 2, 3):
                banks.wait_drained(dve, ("C", part))
            dve.wait_ge(q_ready, 1)
            norm_heads(kraw, NKV, k_ms, k_r, gains[:, HD:2 * HD]).then_inc(k_ready, 1)
            for part in (0, 1, "S", 2, 3):
                banks.wait_drained(dve, ("D", part))
            dve.wait_ge(ln_in, 16)
            for t in range(NT + 1):
                lane.mark(dve.bn_stats(bn[:, t, :], vg[:, t, :]))
            lane.wait()
            for t in range(NT + 1):
                lane.mark(dve.bn_aggr(mu_var[:, t, :], bn[:, t, :]))
            lane.wait()
            rsqrt_of(mu_var[:, :, 1], mu_var[:, :, 1], 1)
            for t in range(NT + 1):
                lane.mark(dve.tensor_scalar(vg[:, t, :], vg[:, t, :], mu_var[:, t, 0:1], vg_r[:, t:t + 1],
                                            ALU.subtract, ALU.mult))
            lane.wait()
            lane.then(dve.tensor_tensor(vg, vg, spread_dim(ln[:, 0, :], 1, NT + 1), ALU.mult))
            dve.tensor_tensor(vg, vg, spread_dim(ln[:, 1, :], 1, NT + 1), ALU.add).then_inc(vg_ready, 1)
            def sample_rounds(n, first):
                s = scores[0:NS, 0:PAST + 1]
                for r in range(first, first + n):
                    lane.then(dve.max(top8_s[0:NS], s))
                    lane.mark(dve.max_index(idx_u[0:NS, 8 * r:8 * r + 8], top8_s[0:NS], s))
                    lane.then(dve.match_replace(s, top8_s[0:NS], s, TAKEN))

            dve.wait_ge(gmlp_in, 64)
            for j in range(4):
                banks.wait_drained(dve, ("U", j))
            mixed = norm_tmp[:, 0:SEQ]
            for j in range(4):
                banks.wait_full(dve, ("mix", j))
                banks.drained(dve.tensor_tensor(
                    mixed.rearrange("p (c t) -> p c t", t=P), psum[:, 4 + j % 2, :].rearrange("p (c t) -> p c t", t=P),
                    spread_dim(bT[:, j, :], 1, NT), ALU.add), ("mix", j))
                banks.wait_drained(dve, ("mix", j))
                dve.tensor_tensor(uT[:, j, 0:SEQ], uT[:, j, 0:SEQ], mixed, ALU.mult).then_inc(gm_tile, 1)
                dve.wait_ge(gm_tile, j + 1)
            banks.wait_full(dve, "vgT_s")
            ms = norm_tmp[:, 0:4 * NS].rearrange("p (j s) -> p j s", j=4)
            banks.drained(dve.tensor_tensor(ms, psum[:, 6, 0:4 * NS].rearrange("p (j s) -> p j s", j=4),
                                            spread_dim(gm_w0, 2, NS), ALU.mult), "vgT_s")
            banks.wait_drained(dve, "vgT_s")
            lane.then(dve.tensor_tensor(ms, ms, spread_dim(bT[:, :, 0], 2, NS), ALU.add))
            dve.tensor_tensor(uT[:, :, SEQ:TOK], uT[:, :, SEQ:TOK], ms, ALU.mult).then_inc(gm_ready, 1)
            dve.wait_ge(gm_ready, 1)

            for g, (qb, kv) in enumerate([(qb, kv) for qb in range(NT) for kv in range(NKV)]):
                L = (qb + 1) * P
                s, mx, su, inv = soft[g % 2][:, :, 0:L], mx4[g % 2], sum4[g % 2], inv4[g % 2]
                mask = C("causal") if qb == 0 else work[:, w_at[qb]:w_at[qb] + L]
                if g >= 2:
                    banks.wait_full(dve, ("probsT", g - 2, (g - 2) // NKV))
                banks.wait_full(dve, ("att_s", g))
                if g == 0:
                    for t in range(NT):
                        banks.wait_drained(dve, ("qT", t))
                    banks.wait_full(dve, "qkT_s")
                banks.drained(dve.scalar_tensor_tensor(s, psum[:, 0:4, 0:L], HD ** -0.5, spread_dim(mask, 1, 4),
                                                       ALU.mult, ALU.add), ("att_s", g))
                banks.wait_drained(dve, ("att_s", g))
                lane.then(dve.tensor_reduce(mx, s, AX_X, ALU.max))
                dve.tensor_scalar(mx, mx, -1.0, None, ALU.mult).then_inc(max_ready, 1)
                dve.wait_ge(exp_ready, g + 1)
                lane.then(dve.reciprocal(inv, su))
                dve.tensor_tensor(s, s, spread_dim(inv, 2, L), ALU.mult).then_inc(probs_ready, 1)
            sample_rounds(TOPK_S // 8, 0)

            lane.then(dve.tensor_copy(idx_f[0:NS], idx_u[0:NS]))
            dve.tensor_scalar(key_bias[0:NS, 0:TOPK_S], idx_f[0:NS], float(PAST), -BIG, ALU.is_equal, ALU.mult)\
               .then_inc(idx_ready, 1)
            lane.then(dve.tensor_reduce(idx_max[0:NS], idx_f[0:NS], AX_X, ALU.max))
            dve.tensor_scalar(key_bias[0:NS, TOPK_S:TOPK_S + 1], idx_max[0:NS], float(PAST), -BIG, ALU.is_lt, ALU.mult)\
               .then_inc(key_bias_ready, 1)
            dve.wait_ge(pages_all_in, 16)
            lane.then(dve.tensor_copy(pages_f, pages_i))
            banks.wait_full(dve, "idxT")
            banks.drained(dve.tensor_copy(slot_i, psum[:, 4, 0:2 * NS]), "idxT")
            banks.wait_drained(dve, "idxT")
            lane.mark(dve.tensor_scalar(off_i, slot_i, PAGE - 1, None, ALU.bitwise_and))
            lane.then(dve.tensor_scalar(slot_i, slot_i, 7, None, ALU.logical_shift_right))
            lane.mark(dve.tensor_copy(page_f, slot_i))
            lane.then(dve.tensor_copy(off_f, off_i))
            lane.then(dve.tensor_tensor(page_hot, spread_dim(C("iota")[:, 0:N_PAGES], 1, 2 * NS),
                                        spread_dim(page_f, 2, N_PAGES), ALU.is_equal))
            hot = page_hot.rearrange("p (h b) n -> p h (b n)", h=2)
            lane.then(dve.tensor_tensor(hot, hot, spread_dim(pages_f, 1, 2), ALU.mult))
            lane.then(dve.tensor_reduce(slot_f, page_hot, AX_X, ALU.add))
            dve.scalar_tensor_tensor(sel_rows, slot_f, float(PAGE), off_f, ALU.mult, ALU.add).then_inc(sel_rows_ready, 1)
            lane.then(dve.memset(q_lhs, 0.0))
            banks.wait_drained(dve, "qkT_s")
            for v in range(NKV):
                o = HD * v
                dve.tensor_copy(q_lhs[o:o + HD, :, 4 * v:4 * v + 4], qT[o:o + HD, :, SEQ:TOK].rearrange("p j b -> p b j"))\
                   .then_inc(q_lhs_ready, 1)
            for g in range(2):
                banks.wait_full(dve, ("att_ss", g))
            lane.then(dve.tensor_reduce(mx2, psum[:, 0:2, 0:TOPK_S + 1], AX_X, ALU.max))
            dve.tensor_scalar(mx2, mx2, -HD ** -0.5, None, ALU.mult).then_inc(max_s_ready, 1)
            for g in range(2):
                banks.wait_drained(dve, ("att_ss", g))
            lane.then(dve.reciprocal(inv2, sum2))
            lane.then(dve.tensor_tensor(soft_s, soft_s, spread_dim(inv2, 2, TOPK_S + 1), ALU.mult))
            lane.mark(dve.tensor_scalar(new_probs[:, 0, :], C("head"), soft_s[:, 0, TOPK_S:TOPK_S + 1], None, ALU.mult))
            dve.tensor_scalar(new_probs[:, 1, :], C("head"), soft_s[:, 1, TOPK_S:TOPK_S + 1], None, ALU.mult)\
               .then_inc(probs_s_ready, 1)
            banks.wait_full(dve, "new_probs")
            banks.drained(dve.tensor_copy(sstat[0:NS, 52:60], psum[0:NS, 3, 0:NH]), "new_probs")
            banks.wait_drained(dve, "new_probs")
            dve.tensor_tensor(new_spread[0:NS].rearrange("p (b h) -> p b h", b=NS),
                              C("own")[0:NS].rearrange("p (b h) -> p b h", b=NS),
                              spread_dim(sstat[0:NS, 52:60], 1, NS), ALU.mult).then_inc(new_spread_ready, 1)

            for f in range(KD):
                o = 4 * (f % 2)
                for name, b, g in (("WA", o, f), ("WG", o + 2, KD + f)):
                    banks.wait_full(dve, (name, f))
                    banks.drained(dve.tensor_tensor(halves(gates[:, g, :]), halves(gates[:, g, :]), pair(b), ALU.mult),
                                  (name, f))
                banks.wait_drained(dve, ("WG", f))
                lane.mark(dve.tensor_tensor(hT[:, f, :], gates[:, f, :], gates[:, KD + f, :], ALU.add))
                lane.wait()
                dve.tensor_copy(hTs[:, f, 0:NS], hT[:, f, SEQ:TOK]).then_inc(merged, 1)
            dve.wait_ge(late_in, 32)
            for c in range(4, 12):
                m, half = ("gate1", "shift2", "scale2", "gate2")[c // 2 - 2], slice(512 * (c % 2), 512 * (c % 2) + 512)
                for g, name, b, rows in ((0, "adaP", 2 + c % 2, P), (1, "adaS", 4 + c % 2, NS)):
                    banks.wait_full(dve, (name, c))
                    out, bias = mod2[m][0:rows, g, half], bias2[0:rows, c - 4, :]
                    if m != "scale2":
                        banks.drained(dve.tensor_tensor(out, psum[0:rows, b, :], bias, ALU.add), (name, c))
                    else:
                        banks.drained(dve.scalar_tensor_tensor(out, psum[0:rows, b, :], 1.0, bias, ALU.add, ALU.add),
                                      (name, c))
                        banks.wait_drained(dve, (name, c))
                        lane.mark(dve.tensor_tensor(out, out, gain2[0:rows, half], ALU.mult))
            dve.wait_ge(x2_in, 16 * T5)
            for c in range(2):
                half = slice(512 * c, 512 * c + 512)
                for i, (part, rows, t) in enumerate(ORDER):
                    b = 3 if part == "S" else t % 2
                    banks.wait_full(dve, (f"O{c}", part))
                    tmp = w_tmp[0:rows, i % 2, :]
                    g = 1 if part == "S" else 0
                    if c + i:
                        dve.wait_ge(x2_half if c == 0 or i == 0 else x2_ready, 5 if c and i == 0 else i)
                    banks.drained(dve.tensor_tensor(tmp, psum[0:rows, b, :], mod2["gate1"][0:rows, g, half], ALU.mult),
                                  (f"O{c}", part))
                    banks.wait_drained(dve, (f"O{c}", part))
                    dve.tensor_tensor(x2[0:rows, t, half], x2[0:rows, t, half], tmp, ALU.add)\
                       .then_inc(x2_ready if c else x2_half, 1)
            dve.wait_ge(ssq2_ready, 1)
            rsqrt_of(ssq, ssq, D)
            for _, rows, t in ORDER:
                g = 0 if t < NT else 1
                out = t2[0:rows, t, :]
                lane.then(dve.scalar_tensor_tensor(out, x2[0:rows, t, :], rstd[0:rows, t:t + 1],
                                                   mod2["scale2"][0:rows, g, :], ALU.mult, ALU.mult))
                dve.tensor_tensor(out, out, mod2["shift2"][0:rows, g, :], ALU.add).then_inc(t2_ready, 1)

            lane.then(dve.memset(logits, 0.0))
            banks.wait_full(dve, "logits_rows")
            n36 = NEG + NE
            lane.mark(dve.tensor_tensor(logits[:, 0:NT, :], psum[:, 2, 0:NT * n36].rearrange("p (t n) -> p t n", t=NT),
                                        spread_dim(b_router, 1, NT), ALU.add))
            banks.drained(dve.tensor_tensor(logits[0:NS, NT, :], psum[0:NS, 2, NT * n36:T5 * n36], b_router[0:NS], ALU.add),
                          "logits_rows")
            banks.wait_drained(dve, "logits_rows")

            def first_best(hot, values, best, rev, tmp, width):
                lane.then(dve.tensor_reduce(best, values, AX_X, ALU.max))
                lane.then(dve.tensor_tensor(tmp, values, spread_dim(best, 2, width), ALU.is_equal))
                lane.then(dve.tensor_tensor(tmp, tmp, spread_dim(C(rev), 1, T5), ALU.mult))
                lane.then(dve.tensor_reduce(w_max, tmp, AX_X, ALU.max))
                lane.then(dve.tensor_tensor(hot, tmp, spread_dim(w_max, 2, width), ALU.is_equal))

            g_logits = logits[:, :, 0:NEG]
            first_best(g_exp, g_logits, g_max, "rev4", g_tmp, NEG)
            lane.then(dve.tensor_scalar(g_exp, g_exp, -1.0, BIG, ALU.add, ALU.mult))
            lane.mark(dve.tensor_tensor(e_logits.rearrange("p t (g e) -> p t g e", g=NEG),
                                        logits[:, :, NEG:n36].rearrange("p t (g e) -> p t g e", g=NEG),
                                        spread_dim(g_exp, 3, EPG), ALU.add))
            lane.wait()
            dve.tensor_tensor(g_tmp, g_logits, spread_dim(g_max, 2, NEG), ALU.subtract).then_inc(g_diff_ready, 1)
            first_best(hot1, e_logits, e_max1, "rev32", e_tmp, NE)
            lane.then(dve.scalar_tensor_tensor(e_logits, hot1, -BIG, e_logits, ALU.mult, ALU.add))
            first_best(hot2, e_logits, e_max2, "rev32", e_tmp, NE)
            dve.tensor_tensor(e_ratio, e_max2, e_max1, ALU.subtract).then_inc(e_diff_ready, 1)
            lane.then(dve.tensor_tensor(chosen, hot1, hot2, ALU.add))
            lane.mark(dve.tensor_tensor(chosen, chosen, spread_dim(C("valid"), 2, NE), ALU.mult))
            lane.then(dve.memset(before_sum[:, 0, :], 0.0))
            for t in range(T5):
                ins = dve.tensor_tensor(before_sum[:, t + 1, :], before_sum[:, t, :], chosen[:, t, :], ALU.add)
                lane.then(ins) if t < NT else ins.then_inc(chosen_ready, 1)
            dve.wait_ge(g_exp_ready, 1)
            lane.then(dve.tensor_reduce(g_sum, g_exp, AX_X, ALU.add))
            dve.wait_ge(e_exp_ready, 1)
            lane.then(dve.tensor_scalar(p_first, e_ratio, 1.0, None, ALU.add))
            lane.then(dve.tensor_tensor(p_first, p_first, g_sum, ALU.mult))
            lane.then(dve.reciprocal(gate_of[:, 0, :], p_first))
            lane.mark(dve.tensor_tensor(gate_of[:, 1, :], gate_of[:, 0, :], e_ratio, ALU.mult))
            lane.mark(dve.tensor_copy(token_of, spread_dim(C("tok"), 1, 2)))

            banks.wait_full(dve, "places")
            lane.mark(dve.tensor_copy(place, psum[:, 3, 0:T5 * NE].rearrange("p (t n) -> p t n", t=T5)))
            banks.drained(dve.tensor_copy(counts, psum[:, 3, T5 * NE:(T5 + 1) * NE]), "places")
            banks.wait_drained(dve, "places")
            lane.then(dve.tensor_tensor(over_cmp, spread_dim(counts, 2, 8), spread_dim(C("over"), 1, NE), ALU.is_gt))
            lane.then(dve.tensor_reduce(n_over, over_cmp, AX_X, ALU.add))
            lane.then(dve.tensor_tensor_scan(over_end, C("ones")[:, 0:NE], n_over, 0.0, ALU.mult, ALU.add))
            lane.then(dve.tensor_tensor(over_shift, over_end, n_over, ALU.subtract))
            lane.then(dve.tensor_scalar(over_shift, over_shift, float(SB), float(SB * (NE - 1)), ALU.mult, ALU.add))
            lane.then(dve.tensor_tensor(over_shift, over_shift, C("first_slot"), ALU.subtract))
            lane.then(dve.tensor_scalar(e_tmp, place, float(SB), None, ALU.is_ge))
            lane.then(dve.tensor_tensor(e_tmp, e_tmp, spread_dim(over_shift, 1, T5), ALU.mult))
            lane.then(dve.tensor_tensor(place, place, e_tmp, ALU.add))
            lane.then(dve.tensor_tensor(place, place, spread_dim(C("first_slot"), 1, T5), ALU.add))
            for c, hot in enumerate((hot1, hot2)):
                lane.then(dve.tensor_tensor(e_tmp, hot, place, ALU.mult))
                lane.then(dve.tensor_reduce(rank[:, c, :], e_tmp, AX_X, ALU.add))
            flat = lambda a: a.rearrange("p c t -> p (c t)")
            lane.then(dve.tensor_copy(rank_i, flat(rank)))
            lane.mark(dve.tensor_scalar(slot_of_i, rank_i, SB - 1, None, ALU.bitwise_and))
            lane.then(dve.tensor_scalar(item_of_i, rank_i, 6, None, ALU.logical_shift_right))
            lane.mark(dve.tensor_copy(slot_of, slot_of_i))
            lane.then(dve.tensor_copy(item_of, item_of_i))
            item2 = item_of.rearrange("p (c t) -> p c t", c=2)
            valid2 = spread_dim(C("valid"), 1, 2)
            lane.then(dve.tensor_scalar(item_of, item_of, 1.0, None, ALU.add))
            lane.then(dve.tensor_tensor(item2, item2, valid2, ALU.mult))
            lane.then(dve.tensor_scalar(item_of, item_of, -1.0, None, ALU.add))
            for half in range(2):
                lane.mark(dve.tensor_tensor(slot_hot[:, :, SB * half:SB * half + SB],
                                            spread_dim(C("iota")[:, 0:SB], 1, 2 * T5), spread_dim(slot_of, 2, SB),
                                            ALU.is_equal))
            gate_cols = item_hot[:, :, N_ITEMS:2 * N_ITEMS]
            token_cols = item_hot[:, :, 0:N_ITEMS]
            lane.then(dve.tensor_tensor(gate_cols, spread_dim(C("iota")[:, 0:N_ITEMS], 1, 2 * T5),
                                        spread_dim(item_of, 2, N_ITEMS), ALU.is_equal))
            lane.then(dve.tensor_tensor(token_cols, gate_cols, spread_dim(flat(token_of), 2, N_ITEMS), ALU.mult))
            dve.tensor_tensor(gate_cols, gate_cols, spread_dim(flat(gate_of), 2, N_ITEMS), ALU.mult)\
               .then_inc(tables_hot_ready, 1)
            lane.then(dve.tensor_tensor(over_hot[0:1], spread_dim(over_end[0:1], 1, N_OVER),
                                        spread_dim(C("iota")[0:1, 0:N_OVER], 2, NE), ALU.is_le))
            lane.then(dve.tensor_reduce(over_expert_f[0:1], over_hot[0:1], AX_X, ALU.add))
            lane.mark(dve.tensor_scalar(over_expert[0:1], over_expert_f[0:1], float(NE - 1), None, ALU.min))
            lane.mark(dve.tensor_copy(over_total[0:1], over_end[0:1, NE - 1:NE]))
            banks.wait_full(dve, "tables")
            banks.drained(dve.tensor_copy(gate_tab, psum[:, 4, N_ITEMS:2 * N_ITEMS]), "tables")
            dve.tensor_copy(token_tab, psum[:, 4, 0:N_ITEMS]).then_inc(tables_ready, 1)

            def hidden_of(p, done):
                dve.tensor_tensor(hidden[0:SB, p, :], silu_g[0:SB, p, :], psum[0:SB, 2 + p, 0:DE], ALU.mult).then_inc(done, 1)

            def hidden_out(p, done):
                dve.tensor_copy(hidden_T[:, p], psum[:, 4 + p, 0:2 * SB].rearrange("p (f n) -> p f n", f=2)).then_inc(done, 1)

            def y_scaled(p, gate, done):
                dve.tensor_scalar(y_rows[:, p, :], psum[:, 6 + p, :], gate, None, ALU.mult).then_inc(done, 1)

            def dve_items(i, first):
                for k in range(4):
                    e, p = i * 4 + k, k % 2
                    dve.wait_ge(silu_done, e + 1)
                    if not (first and k < 2):
                        dve.wait_ge(hT_full, e - 1)
                    hidden_of(p, hidden_done)
                    dve.wait_ge(hT_full, e + 1)
                    if not (first and k < 2):
                        dve.wait_ge(y_full, e - 1)
                    hidden_out(p, hT_out)
                    dve.wait_ge(y_full, e + 1)
                    if not (first and k < 2):
                        dve.wait_ge(y_stored[p], i * 64 + 32 * (k // 2))
                    gate = gate_tab[:, e:e + 1] if first else gate_tab[:, bass.ds(e, 1)]
                    y_scaled(p, gate, y_out)

            dve.wait_ge(tables_ready, 1)
            dve_items(0, True)
            with dve.Fori(1, NE // 4) as i:
                dve_items(i, False)
            total = dve.value_load(over_total[0:1, 0:1], min_val=0, max_val=N_OVER)
            for p in range(2):
                dve.wait_ge(y_stored[p], 16 * NE)
            with dve.Fori(0, N_OVER) as j:
                with dve.If(j < total):
                    dve.wait_ge(o_silu, j + 1)
                    hidden_of(0, o_hidden)
                    dve.wait_ge(o_hT_full, j + 1)
                    hidden_out(0, o_hT_out)
                    dve.wait_ge(o_y, j + 1)
                    dve.wait_ge(o_stored, j * 32 + 1)
                    y_scaled(0, gate_tab[:, bass.ds(j + NE, 1)], o_y_out)

            for t in range(T5):
                rows, g = (P, 0) if t < NT else (NS, 1)
                dve.wait_ge(picked_in[t % 2], 32 * (t // 2 + 1))
                a, b = picked[0:rows, t % 2, 0, :], picked[0:rows, t % 2, 1, :]
                lane.then(dve.tensor_tensor(a, a, b, ALU.add))
                lane.then(dve.tensor_tensor(a, a, mod2["gate2"][0:rows, g, :], ALU.mult))
                dve.tensor_tensor(x2[0:rows, t, :], x2[0:rows, t, :], a, ALU.add).then_inc(y_ready, 1)
                if t < T5 - 1:
                    dve.wait_ge(y_ready, t + 1)
                    dve.sem_inc(picked_used, 1)


def _tiles(w, width):
    k = w.shape[0] // P
    return w.reshape(k, P, width).transpose(1, 0, 2).reshape(P, k * width)


def _stream(inputs):
    w_in, w_ada = inputs["w_in"][0], inputs["w_ada"][0]
    o = np.cumsum([0, NH * HD, NKV * HD, NKV * HD, IH * ID, ID, IH, GM, GM, 2 * D])
    q, k, v, qi, ki, wi, u, vg, gates = (w_in[:, o[i]:o[i + 1]] for i in range(9))
    q = q.reshape(D, NH, HD)[:, HEAD_ORDER].reshape(D, NH * HD)
    wa = inputs["w_proj_attn"][0].reshape(NH, HD, D)[HEAD_ORDER].reshape(NH * HD, D)
    parts = {f"ada{c}": w_ada[:, 512 * c:512 * c + 512] for c in range(12)}
    parts |= {"A": np.concatenate([qi, ki, wi, v], 1), "B": q, "C": np.concatenate([k, vg[:, :VG0]], 1),
              "D": vg[:, VG0:], "U": u}
    parts |= {f"G{c}": np.concatenate([gates[:, 256 * c:256 * c + 256], gates[:, D + 256 * c:D + 256 * c + 256]], 1)
              for c in range(4)}
    parts |= {"WA": wa, "WG": inputs["w_proj_gmlp"][0]}
    parts |= {f"O{c}": inputs["w_out"][0][:, 512 * c:512 * c + 512] for c in range(2)}
    out = np.zeros((len(STREAM), P, KD * 512), np.float32)
    for n, (name, size) in enumerate(STREAM):
        w = parts[name]
        out[n, :, :size] = _tiles(w, w.shape[1])
    return out


def _layout(inputs):
    x = {k: np.asarray(v) for k, v in inputs.items()}
    c = np.concatenate([x["c_sample"], x["c_prompt"]], 0)
    c_T = np.zeros((P, KD, 32), np.float32)
    c_T[:, :, :NS + 1] = c.reshape(NS + 1, KD, P).transpose(2, 1, 0)
    a = {
        "consts": np.concatenate(list(CONSTS.values()), 1),
        "stream": _stream(x),
        "c_T": c_T.reshape(P, -1),
        "b_ada": x["b_ada"].reshape(12, 512),
        "norm_mix_g": x["norm_mix_g"][0],
        "norm_ffn_g": x["norm_ffn_g"][0],
        "head_gains": np.concatenate([x["q_norm_g"][0], x["k_norm_g"][0], x["kidx_norm_g"][0]]),
        "ln": np.concatenate([x["gm_ln_g"], x["gm_ln_b"]], 0),
        "x_prompt": x["x_prompt"][0],
        "x_sample": x["x_sample"][:, 0],
        "page_rep": np.repeat(x["page_table"].T, 8, axis=0),
        "pages": x["page_table"].reshape(-1),
        "cache_ki": x["cache_kidx"].reshape(POOL_PAGES * 8, 16 * ID),
        "cache_k": x["cache_k"].reshape(POOL_PAGES * PAGE, NKV * HD),
        "cache_v": x["cache_v"].reshape(POOL_PAGES * PAGE, NKV * HD),
        "ws_T": x["gm_spatial_w"][0].transpose(2, 0, 1).reshape(P, GG * CHUNK),
        "ws_00": x["gm_spatial_w"][0][:, 0, 0].reshape(4, 2).T,
        "gm_b": x["gm_spatial_b"][0],
        "w_router": _tiles(np.concatenate([x["w_router_group"][0], x["w_router_expert"][0]], 1), NEG + NE),
        "b_router": np.concatenate([x["b_router_group"][0], x["b_router_expert"][0]]),
        "experts": np.concatenate([
            np.concatenate([x["w_expert_gate"][0], x["w_expert_up"][0]], 2)
            .reshape(NE, KD, P, 2 * DE).transpose(0, 2, 1, 3).reshape(NE, P, KD * 2 * DE),
            x["w_expert_down"][0].reshape(NE, 2, P, D).transpose(0, 2, 1, 3).reshape(NE, P, 2 * D)], 2),
    }
    return {k: np.ascontiguousarray(v) for k, v in a.items()}


OUTS = {
    "y_p": (SEQ, D), "y_s": (NS, D),
    "new_k_p": (SEQ, NKV * HD), "new_v_p": (SEQ, NKV * HD), "new_ki_p": (SEQ, ID),
    "new_k_s": (NS, NKV * HD), "new_v_s": (NS, NKV * HD), "new_ki_s": (NS, ID), "new_vg_s": (NS, GM),
}
SCRATCH = {"t2_rows": (TOK, D), "expert_rows": (N_ITEMS * SB, D)}


def kernel(**inputs):
    import concourse.bacc as bacc
    from concourse.bass_utils import run_bass_kernel_spmd

    arrays = _layout(inputs)
    nc = bacc.Bacc("TRN2", target_bir_lowering=False, num_devices=1)
    io = {k: nc.dram_tensor(f"in_{k}", a.shape, mybir.dt.from_np(a.dtype), kind="ExternalInput").ap()
          for k, a in arrays.items()}
    io |= {k: nc.dram_tensor(f"out_{k}", s, F32, kind="ExternalOutput").ap() for k, s in OUTS.items()}
    io |= {k: nc.dram_tensor(k, s, F32, kind="Internal").ap() for k, s in SCRATCH.items()}
    decoder_step(nc, io)
    run = run_bass_kernel_spmd(nc, [{f"in_{k}": a for k, a in arrays.items()}], core_ids=[0])
    got = {k: run.results[0][f"out_{k}"] for k in OUTS}
    return (
        got["y_p"].reshape(1, SEQ, D), got["y_s"].reshape(NS, 1, D),
        got["new_k_p"].reshape(1, 1, SEQ, NKV, HD), got["new_v_p"].reshape(1, 1, SEQ, NKV, HD),
        got["new_ki_p"].reshape(1, 1, SEQ, ID),
        got["new_k_s"].reshape(1, NS, 1, NKV, HD), got["new_v_s"].reshape(1, NS, 1, NKV, HD),
        got["new_ki_s"].reshape(1, NS, 1, ID), got["new_vg_s"].reshape(1, NS, 1, GM),
    )
```

```python
from contextlib import ExitStack

import numpy as np

import concourse.bass as bass
from concourse import mybir

F32 = mybir.dt.float32
I32 = mybir.dt.int32
U32 = mybir.dt.uint32
ALU = mybir.AluOpType
ACT = mybir.ActivationFunctionType
AX_X = mybir.AxisListType.X

P = 128
D = 1024
KD = D // P
SEQ = 512
NT = SEQ // P
NS = 8
TOK = SEQ + NS
HALF = TOK // 2
PAST = 2048
PAGE = 128
N_PAGES = PAST // PAGE
POOL_PAGES = 160
NH, HD, NKV = 8, 64, 2
ROT = HD // 4
THETA = 500000.0
IH, ID = 4, 64
TOPK_P = min(256, SEQ // 4)
TOPK_S = min(256, (PAST + 1) // 4)
GM, GG, GD = 512, 8, 64
CHUNK = 128
NEG, EPG = 4, 8
NE = NEG * EPG
DE = D // 4
EPS = 1e-6
BIG = 1e30
TAKEN = -3e38

QI, KI, WI, VV = 0, 256, 320, 324
NA = VV + NKV * HD
NB = NH * HD
VG0 = 192
NC = NKV * HD + VG0
ND = GM - VG0
HEAD_ORDER = [h for j in range(4) for h in (j, j + 4)]

STREAM = ([(f"ada{c}", KD * 512) for c in range(4)] + [("A", KD * NA), ("B", KD * NB), ("C", KD * NC), ("D", KD * ND)]
          + [("U", KD * 512)]
          + [(name, KD * 512) for c in range(4) for name in (f"G{c}", f"ada{4 + 2 * c}", f"ada{5 + 2 * c}")]
          + [("WG", 4 * D), ("WA", 4 * D), ("O0", KD * 512), ("O1", KD * 512)])
SLOT_OF = {name: n for n, (name, _) in enumerate(STREAM)}
RING = 3

ROUNDS = (4, 3, 5, 2, 1)

SB = 64
ASSIGNED = 2 * TOK
N_OVER = ASSIGNED // (SB + 1)
N_ITEMS = NE + N_OVER

O_GATES, O_QT, O_ATT, O_U, O_KT, O_QIT, O_KIT = 0, 8320, 10400, 12480, 14560, 15080, 16120
O_VG, O_QR, O_KR, O_AR, O_WS, O_BT, O_S, O_PT, O_WORK, O_SC = (
    16640, 19200, 21760, 22400, 24660, 25684, 26196, 28244, 29268, 30420)
ARENA = 33024


def constant_fields():
    eye = np.eye(P, dtype=np.float32)
    row = np.arange(P)
    f = {}
    f["ident"] = eye
    sel_p = np.zeros((P, P)); sel_p[8::32, :] = 1.0
    f["sel_p"] = sel_p
    sel_s = np.zeros((P, NS))
    for i in range(NS):
        sel_s[i::32, i] = 1.0
    f["sel_s"] = sel_s
    f["before"] = (row[:, None] < row[None, :]).astype(np.float32)
    f["ones"] = np.ones((P, P))
    f["causal"] = np.where(row[None, :] <= row[:, None], 0.0, -BIG)
    pos = np.zeros((P, NT + 1), np.float32)
    for t in range(NT):
        pos[:, t] = t * P + row
    pos[:, NT] = PAST
    half = ROT // 2
    inv = np.float32(THETA) ** (-np.arange(half, dtype=np.float32) / np.float32(half))
    ang = (pos[:, :, None] * inv[None, None, :].astype(np.float32)).astype(np.float32)
    cos, sin = np.cos(ang), np.sin(ang)
    f["cos"] = np.concatenate([cos, cos], -1).reshape(P, -1)
    f["sin"] = np.concatenate([-sin, sin], -1).reshape(P, -1)
    f["iota"] = np.tile(np.arange(P, dtype=np.float32), (P, 1))
    tok = np.zeros((P, NT + 1)); valid = np.zeros((P, NT + 1))
    for t in range(NT):
        tok[:, t] = t * P + row; valid[:, t] = 1.0
    tok[:NS, NT] = SEQ + row[:NS]; valid[:NS, NT] = 1.0
    f["tok"] = tok
    f["valid"] = valid
    f["page_seg"] = (row % 8)[:, None]
    place = np.zeros((P, 2, 2, 4, 8, 4))
    for b in range(NS):
        for par in range(2):
            place[b, b // 4, par, b % 4, par, :] = 1.0
    f["place"] = place.reshape(P, -1)
    spread = np.zeros((P, 2, P)); gather = np.zeros((P, 2, NS))
    for b in range(NS):
        spread[b, b // 4, 32 * (b % 4):32 * (b % 4) + NH] = 1.0
        gather[32 * (b % 4):32 * (b % 4) + NH, b // 4, b] = 1.0
    f["spread"] = spread.reshape(P, -1)
    f["gather"] = gather.reshape(P, -1)
    f["head"] = (row[:, None] % 32 == np.arange(NH)[None, :])
    f["own"] = np.repeat(np.eye(NS), NH, axis=1) if False else np.concatenate(
        [np.repeat(np.eye(NS), NH, axis=1), np.zeros((P - NS, NS * NH))])
    f["rev4"] = np.tile(4.0 - np.arange(4), (P, 1))
    f["rev32"] = np.tile(32.0 - np.arange(32), (P, 1))
    f["first_slot"] = np.tile(SB * np.arange(NE), (P, 1))
    f["over"] = np.tile(SB * np.arange(1, 9), (P, 1))
    f["one"] = np.ones((P, 1))
    return {k: np.ascontiguousarray(v, dtype=np.float32) for k, v in f.items()}


CONSTS = constant_fields()
CONST_AT = {}
_n = 0
for _k, _v in CONSTS.items():
    CONST_AT[_k] = (_n, _v.shape[1])
    _n += _v.shape[1]
N_CONST = _n


class Lane:

    def __init__(self, engine, semaphore):
        self.engine, self.semaphore, self.count = engine, semaphore, 0

    def mark(self, instruction):
        instruction.then_inc(self.semaphore, 1)
        self.count += 1

    def wait(self):
        if self.count:
            self.engine.wait_ge(self.semaphore, self.count)

    def then(self, instruction):
        self.mark(instruction)
        self.wait()


class Banks:

    def __init__(self, full, free):
        self.full, self.free = full, free
        self.count = [0] * 8
        self.last = [None] * 8
        self.at = {}

    def begin(self, pe, name, *banks):
        before = {self.at[self.last[b]] for b in banks if self.last[b] is not None}
        lead = banks[0]
        self.at[name] = (lead, self.count[lead])
        self.count[lead] += 1
        for b in banks:
            self.last[b] = name
        for b, n in sorted(before):
            pe.wait_ge(self.free[b], n + 1)

    def filled(self, instruction, name):
        instruction.then_inc(self.full[self.at[name][0]], 1)

    def wait_full(self, engine, name):
        b, n = self.at[name]
        engine.wait_ge(self.full[b], n + 1)

    def drained(self, instruction, name):
        instruction.then_inc(self.free[self.at[name][0]], 1)

    def wait_drained(self, engine, name):
        b, n = self.at[name]
        engine.wait_ge(self.free[b], n + 1)


def spread_dim(ap, axis, n):
    wide = ap.unsqueeze(axis)
    shape = list(wide.shape)
    shape[axis] = n
    return wide.broadcast_to(shape)


def decoder_step(nc, io):
    ctx = ExitStack()
    with ctx:
        def sb(name, shape, dt=F32):
            return ctx.enter_context(nc.sbuf_tensor(name, shape, dt))

        def sem(name):
            return ctx.enter_context(nc.semaphore(name))

        ring = sb("ring", [P, RING, KD * 512])
        hT = sb("hT", [P, KD, TOK])
        hTs = sb("hTs", [P, KD, 32])
        c_T = sb("c_T", [P, KD, 32])
        bn = sb("bn", [P, NT + 1, 6])
        zeros = sb("zeros", [P, 256])
        arena = sb("arena", [P, ARENA])
        const = sb("const", [P, N_CONST])
        gains = sb("gains", [P, 3 * HD])
        stat = sb("stat", [P, 256])
        psum = ctx.enter_context(nc.psum_tensor("psum", [P, 8, 512], F32))

        def at(offset, size):
            return arena[:, offset:offset + size]

        def C(name):
            o, n = CONST_AT[name]
            return const[:, o:o + n]

        ident = C("ident")
        early = O_GATES
        mod1 = at(early, 4096).rearrange("p (g m n) -> p g m n", g=2, m=2)
        ln = at(early + 4096, 2 * GM).rearrange("p (m n) -> p m n", m=2)
        xbuf = at(early + 5120, (NT + 1) * D).rearrange("p (t n) -> p t n", n=D)
        relu_p = at(early, 4 * 512).rearrange("p (h n) -> p h n", h=4)
        ki_pages = at(early + 2048, 2 * D).rearrange("p (b n) -> p b n", b=2)
        ki_T = at(early + 5120, 2 * D).rearrange("p (b n) -> p b n", b=2)
        relu_s = at(early + 5120 + 2 * D, 2 * D).rearrange("p (b n) -> p b n", b=2)
        gain1 = at(O_QR, D)
        junk = at(O_QR + D, D)
        G = at(O_PT, 2 * 512).rearrange("p (b n) -> p b n", b=2)
        late_G = [at(o, 512) for o in (O_QIT, O_QIT + 512, O_QIT + 1024, O_WS, O_WS + 512, O_WS + 1024,
                                       O_VG + NT * GM, O_QR + NT * NB)]
        ada_bias = at(O_SC + 1540, 512)
        gates = at(O_GATES, 16 * TOK).rearrange("p (f n) -> p f n", f=16)
        qT = at(O_QT, 4 * TOK).rearrange("p (j n) -> p j n", j=4)
        attT = at(O_ATT, 4 * TOK).rearrange("p (j n) -> p j n", j=4)
        uT = at(O_U, 4 * TOK).rearrange("p (j n) -> p j n", j=4)
        kT = at(O_KT, TOK)
        qiT = at(O_QIT, 2 * TOK).rearrange("p (j n) -> p j n", j=2)
        kiT = at(O_KIT, TOK)
        vg = at(O_VG, (NT + 1) * GM).rearrange("p (t n) -> p t n", n=GM)
        qraw = at(O_QR, (NT + 1) * NB).rearrange("p (t n) -> p t n", n=NB)
        kraw = at(O_KR, (NT + 1) * NKV * HD).rearrange("p (t n) -> p t n", n=NKV * HD)
        araw = at(O_AR, (NT + 1) * NA).rearrange("p (t n) -> p t n", n=NA)
        wsT = at(O_WS, GG * CHUNK).rearrange("p (g n) -> p g n", g=GG)
        bT = at(O_BT, 4 * CHUNK).rearrange("p (j n) -> p j n", j=4)
        ki_twice = at(O_S, (NT + 1) * P).rearrange("p (t n) -> p t n", n=P)
        qi_twice = at(O_S + 640, IH * P).rearrange("p (h c d) -> p h c d", h=IH, c=2)
        qi_lhs = at(O_S + 1152, NS * 32).rearrange("p (b m) -> p b m", b=NS)
        wi_lhs = at(O_S + 1408, 4 * NS).rearrange("p (c b) -> p c b", c=4)
        wi_place = at(O_S + 1440, 512)
        work = at(O_WORK, 1152)
        norm_tmp = at(O_S, 2560)
        scores = at(O_SC, PAST // 2 + 1)
        top_values = at(O_SC + 1028, TOPK_S)
        idx = at(O_SC + 1284, TOPK_S)
        second_values = at(O_WORK, TOPK_S)
        half_idx = at(O_WORK + 256, TOPK_S)
        second_idx = at(O_WORK + 512, TOPK_S)
        page_rows = stat[:, 0:NS].bitcast(I32)
        page_rep = stat[:, NS:2 * NS].bitcast(I32)
        ssq = stat[:, 16:21]
        rstd = stat[:, 24:29]
        ki_ms = stat[:, 32:37]
        ki_r = stat[:, 40:45]
        k_ms = stat[:, 48:58]
        k_r = stat[:, 60:70]
        q_ms = stat[:, 72:112]
        q_r = stat[:, 112:152]
        new_dots = stat[:, 152:156]
        top8 = stat[:, 160:192]
        mu_var = stat[:, 192:202].rearrange("p (t m) -> p t m", m=2)
        vg_r = stat[:, 204:209]
        minus_half = stat[:, 212:252]

        norm_tmp2 = at(O_S, 2048).rearrange("p (h n) -> p h n", h=4)
        soft = [norm_tmp2, at(O_QR, 2048).rearrange("p (h n) -> p h n", h=4)]
        probsT = at(O_VG, 4 * 512).rearrange("p (c n) -> p c n", c=4)
        gm_w0 = stat[:, 252:256]
        pages_i = at(O_SC + 2312, N_PAGES * NS).bitcast(I32)
        pages_f = at(O_SC + 2440, N_PAGES * NS)
        k_sel = at(O_QR, 2048).rearrange("p (a n) -> p a n", n=P)
        v_sel = at(O_VG, 2048).rearrange("p (a n) -> p a n", n=P)
        k_selT = at(O_S, 2048).rearrange("p (b n) -> p b n", b=NS)
        soft_s = at(O_PT, 2 * 257).rearrange("p (g n) -> p g n", g=2)
        page_hot = at(O_WORK, 256).rearrange("p (a n) -> p a n", n=N_PAGES)
        q_lhs = at(O_WORK + 256, 256).rearrange("p (b m) -> p b m", b=NS)
        probsT_s = at(O_WORK + 512, 512).rearrange("p (a n) -> p a n", n=P)
        sel_tmp = at(O_WORK + 1024, 128)
        new_probs = sel_tmp[:, 0:2 * NH].rearrange("p (g h) -> p g h", g=2)
        new_spread = sel_tmp[:, 16:16 + NS * NH]
        slot_f = at(O_PT + 520, 16)
        slot_i = at(O_PT + 540, 16).bitcast(I32)
        off_i = at(O_PT + 560, 16).bitcast(I32)
        page_f = at(O_PT + 580, 16)
        off_f = at(O_PT + 600, 16)
        sel_rows = at(O_PT + 620, 16).bitcast(I32)
        idx_u = idx.bitcast(U32)
        key_bias = scores[:, 0:TOPK_S + 1]
        idx_f = scores[:, 512:512 + TOPK_S]
        sstat = sb("sstat", [P, 64])
        mx4 = [sstat[:, 0:4], sstat[:, 4:8]]
        sum4 = [sstat[:, 8:12], sstat[:, 12:16]]
        inv4 = [sstat[:, 16:20], sstat[:, 20:24]]
        mx2, sum2, inv2 = sstat[:, 24:26], sstat[:, 26:28], sstat[:, 28:30]
        idx_max = sstat[:, 48:49]

        x2 = at(0, (NT + 1) * D).rearrange("p (t n) -> p t n", n=D)
        mod2 = {m: at(o, 2 * D).rearrange("p (g n) -> p g n", g=2)
                for m, o in (("gate2", 5120), ("gate1", 7168), ("shift2", 9216), ("scale2", 11264))}
        t2 = at(13312, (NT + 1) * D).rearrange("p (t n) -> p t n", n=D)
        gain2 = at(23552, D)
        w_tmp = at(25600, 1024).rearrange("p (b n) -> p b n", b=2)
        w_router = at(26624, KD * (NEG + NE)).rearrange("p (k n) -> p k n", k=KD)
        b_router = at(26912, NEG + NE)
        junk2 = at(19456, D)
        router_at = [27648]

        def rt(n):
            router_at[0] += n
            assert router_at[0] <= ARENA
            return at(router_at[0] - n, n)

        T5 = NT + 1
        logits_T = rt(TOK)
        logits = rt(T5 * (NEG + NE)).rearrange("p (t n) -> p t n", t=T5)
        e_logits, hot1, hot2, e_tmp, chosen, place = (rt(T5 * NE).rearrange("p (t n) -> p t n", t=T5) for _ in range(6))
        before_sum = rt((T5 + 1) * NE).rearrange("p (t n) -> p t n", n=NE)
        g_tmp = rt(T5 * NEG).rearrange("p (t n) -> p t n", t=T5)
        g_exp = rt(T5 * NEG).rearrange("p (t n) -> p t n", t=T5)
        slot_hot = rt(2 * T5 * P).rearrange("p (a n) -> p a n", n=P)
        item_hot = rt(2 * T5 * 2 * N_ITEMS).rearrange("p (a n) -> p a n", n=2 * N_ITEMS)
        over_cmp = at(26960, NE * 8).rearrange("p (e m) -> p e m", m=8)
        over_hot = at(26960, N_OVER * NE).rearrange("p (j e) -> p j e", e=NE)
        r = sb("router", [P, 400])
        g_max, e_max1, e_max2, w_max, g_sum, p_first, e_ratio = (r[:, 5 * i:5 * i + 5] for i in range(7))
        rank = r[:, 40:50].rearrange("p (c t) -> p c t", c=2)
        gate_of = r[:, 50:60].rearrange("p (c t) -> p c t", c=2)
        token_of = r[:, 60:70].rearrange("p (c t) -> p c t", c=2)
        rank_i = r[:, 70:80].bitcast(I32)
        slot_of_i, item_of_i = r[:, 80:90].bitcast(I32), r[:, 90:100].bitcast(I32)
        slot_of, item_of = r[:, 100:110], r[:, 110:120]
        n_over, over_end, over_shift, counts = (r[:, 120 + 32 * i:152 + 32 * i] for i in range(4))
        over_expert_f, over_expert = r[:, 248:264], r[:, 264:284].bitcast(I32)
        item_counts = r[:, 284:287].bitcast(I32)
        gate_tab = r[:, 288:288 + N_ITEMS]
        token_tab = r[:, 336:337 + N_ITEMS].bitcast(I32)

        flat_ring = ring.rearrange("p r n -> p (r n)")
        EW = KD * 2 * DE + 2 * D
        expert_w = [flat_ring[:, 0:EW], flat_ring[:, EW:2 * EW], at(7168, EW), at(13312, EW)]
        w_gu = [w[:, 0:KD * 2 * DE].rearrange("p (k n) -> p k n", k=KD) for w in expert_w]
        w_dn = [w[:, KD * 2 * DE:EW].rearrange("p (f n) -> p f n", f=2) for w in expert_w]
        x_rows = at(19456, 2 * D).rearrange("p (b n) -> p b n", b=2)
        y_rows = at(21504, 1024).rearrange("p (b n) -> p b n", b=2)
        silu_g = at(22528, 2 * DE).rearrange("p (b n) -> p b n", b=2)
        hidden = at(23040, 2 * DE).rearrange("p (b n) -> p b n", b=2)
        x_T = at(23552, 2 * KD * SB).rearrange("p (b k n) -> p b k n", b=2, k=KD)
        hidden_T = at(24576, 4 * SB).rearrange("p (b f n) -> p b f n", b=2, f=2)
        next_token = at(24832, 2).bitcast(I32)
        picked = flat_ring[:, 0:2 * T5 * D].rearrange("p (t c n) -> p t c n", t=T5, c=2)

        bank_full = [sem(f"bank_full{b}") for b in range(8)]
        bank_free = [sem(f"bank_free{b}") for b in range(8)]
        banks = Banks(bank_full, bank_free)
        ring_full = [sem(f"ring_full{i}") for i in range(RING)]
        const_in = sem("const_in")
        c_in = sem("c_in")
        bias_in = sem("bias_in")
        ada_bias_in = sem("ada_bias_in")
        vg_s_stored = sem("vg_s_stored")
        ln_in = sem("ln_in")
        gmlp_in, ws_in = sem("gmlp_in"), sem("ws_in")
        x_in = [sem(f"x_in{t}") for t in range(NT + 1)]
        pages_in = sem("pages_in")
        c_silu = sem("c_silu")
        zeroed = sem("zeroed")
        ssq_ready = sem("ssq_ready")
        rstd_asked, rstd_ready = sem("rstd_asked"), sem("rstd_ready")
        h_ready = sem("h_ready")
        a_ready = sem("a_ready")
        k_ready = sem("k_ready")
        q_ready = sem("q_ready")
        vg_ready = sem("vg_ready")
        qi_dup_ready = sem("qi_dup_ready")
        qi_lhs_ready = sem("qi_lhs_ready")
        relu_p_read = sem("relu_p_read")
        page_rows_ready = sem("page_rows_ready")
        ki_in = [sem(f"ki_in{i}") for i in range(2)]
        ki_used = sem("ki_used")
        scores_ready = sem("scores_ready")
        outs, y_outs = sem("outs"), sem("y_outs")
        late_in = sem("late_in")
        over_zeroed = sem("over_zeroed")
        x2_in = sem("x2_in")
        router_in = sem("router_in")
        x2_half, x2_ready = sem("x2_half"), sem("x2_ready")
        ssq2_ready = sem("ssq2_ready")
        t2_ready = sem("t2_ready")
        t2_stored = sem("t2_stored")
        g_diff_ready, g_exp_ready = sem("g_diff_ready"), sem("g_exp_ready")
        e_diff_ready, e_exp_ready = sem("e_diff_ready"), sem("e_exp_ready")
        chosen_ready = sem("chosen_ready")
        tables_hot_ready, tables_ready = sem("tables_hot_ready"), sem("tables_ready")
        w_got = [sem(f"w_got{i}") for i in range(4)]
        x_got = [sem(f"x_got{i}") for i in range(2)]
        y_stored = [sem(f"y_stored{i}") for i in range(2)]
        (xT_full, xT_out, gu_full, silu_done, hidden_done, hT_full, hT_out, y_full, y_out) = (
            sem(n) for n in ("xT_full", "xT_out", "gu_full", "silu_done", "hidden_done", "hT_full", "hT_out", "y_full",
                             "y_out"))
        token_copied = sem("token_copied")
        experts_done = sem("experts_done")
        pe_passed, pool_passed, pe_finished, pool_finished = (
            sem(n) for n in ("pe_passed", "pool_passed", "pe_finished", "pool_finished"))
        picked_in = [sem(f"picked_in{t}") for t in range(T5)]
        y_ready = sem("y_ready")
        ws_masked = sem("ws_masked")
        gm_ready, gm_tile = sem("gm_ready"), sem("gm_tile")
        max_ready, exp_ready, probs_ready = sem("max_ready"), sem("exp_ready"), sem("probs_ready")
        idx_ready = sem("idx_ready")
        pages_all_in = sem("pages_all_in")
        sel_rows_ready = sem("sel_rows_ready")
        k_sel_in, v_sel_in = sem("k_sel_in"), sem("v_sel_in")
        key_bias_ready = sem("key_bias_ready")
        q_lhs_ready = sem("q_lhs_ready")
        max_s_ready, exp_s_ready, probs_s_ready = sem("max_s_ready"), sem("exp_s_ready"), sem("probs_s_ready")
        new_spread_ready = sem("new_spread_ready")
        merged = sem("merged")
        values_done = sem("values_done")
        vector_lane, scalar_lane, pool_lane = sem("vector_lane"), sem("scalar_lane"), sem("pool_lane")
        n_outs = [0]
        last_use = {}
        ORDER = [(0, P, 0), (1, P, 1), ("S", NS, NT), (2, P, 2), (3, P, 3)]

        def lone_wait(engine, semaphore, value, passed):
            engine.wait_ge(semaphore, value)
            engine.sem_inc(passed, 1)

        def load_n_items(engine, which=0):
            least, most = (NE, N_ITEMS) if which == 0 else (16 * NE, 16 * N_ITEMS)
            return engine.value_load(item_counts[0:1, which:which + 1], min_val=least, max_val=most)

        def each_item(engine, item):
            for k in range(4):
                item(0, k, True)
            with engine.Fori(1, NE // 4) as i:
                for k in range(4):
                    item(i, k, False)
            n_items = load_n_items(engine)
            with engine.Fori(NE // 4, N_ITEMS // 4) as i:
                for k in range(4):
                    with engine.If(i * 4 + k < n_items):
                        item(i, k, False)
            return n_items

        def ring_wait(pe, name):
            n = SLOT_OF[name]
            pe.wait_ge(ring_full[n % RING], 16 * (n // RING + 1))

        def ring_at(name, width):
            kk = STREAM[SLOT_OF[name]][1] // width
            return ring[:, SLOT_OF[name] % RING, 0:kk * width].rearrange("p (k n) -> p k n", k=kk)

        def pair(b0):
            return psum[:, b0:b0 + 2, 0:HALF]

        def halves(ap):
            return ap.rearrange("p (s n) -> p s n", s=2)

        block = ctx.enter_context(nc.Block())

        @block.tensor
        def _(pe):
            def grouped(name, b, width, weights, lhs, bias=None):
                banks.begin(pe, name, b)
                if bias is not None:
                    pe.matmul(psum[0:32, b, 0:width], ident[0:12, bias:bias + 1].broadcast_to([12, 32]),
                              ada_bias[0:12, :], start=True, stop=False, tile_position=(0, 0))
                for k in range(KD):
                    j = k % 4
                    mm = pe.matmul(psum[32 * j:32 * j + 32, b, 0:width], lhs[:, k, :], weights[:, k, :],
                                   start=(k < 4 and (j > 0 or bias is None)), stop=(k >= 4),
                                   tile_position=(0, 32 * j))
                banks.filled(mm, name)

            def ada_product(c, b):
                ring_wait(pe, f"ada{c}")
                grouped(("ada", c), b, 512, ring_at(f"ada{c}", 512), c_T, bias=c)
                last_use[f"ada{c}"] = ("ada", c)

            def ada_spread(c):
                banks.wait_drained(pe, ("ada", c))
                for name, sel, b, rows in (("adaP", "sel_p", 2 + c % 2, P), ("adaS", "sel_s", 4 + c % 2, NS)):
                    banks.begin(pe, (name, c), b)
                    part = G[:, c % 2, :] if c < 4 else late_G[c - 4]
                    mm = pe.matmul(psum[0:rows, b, :], C(sel), part, start=True, stop=True)
                    banks.filled(mm, (name, c))

            pe.wait_ge(const_in, 16)
            pe.wait_ge(c_silu, 1)
            for c in range(5):
                if c == 0:
                    pe.wait_ge(ada_bias_in, 16)
                if c < 4:
                    ada_product(c, c % 2)
                if c >= 1:
                    ada_spread(c - 1)

            for t in range(NT + 1):
                n = P if t < NT else NS
                pe.wait_ge(h_ready, t + 1)
                for j in range(2):
                    b = 6 + j
                    banks.begin(pe, ("hT", t, j), b)
                    for k in range(4):
                        mm = pe.transpose(psum[:, b, k * n:(k + 1) * n], xbuf[0:n, t, (4 * j + k) * P:(4 * j + k + 1) * P],
                                          ident[0:n, 0:n])
                    banks.filled(mm, ("hT", t, j))

            def rows_slice(name, width):
                ring_wait(pe, name)
                w = ring_at(name, width)
                for t in range(NT):
                    if name == "A":
                        for j in range(2):
                            banks.wait_drained(pe, ("hT", t, j))
                    b = t % 2
                    banks.begin(pe, (name, t), b)
                    for k in range(KD):
                        mm = pe.matmul(psum[:, b, 0:width], hT[:, k, t * P:(t + 1) * P], w[:, k, :],
                                       start=(k == 0), stop=(k == KD - 1))
                    banks.filled(mm, (name, t))
                    if t == 0:
                        if name == "A":
                            for j in range(2):
                                banks.wait_drained(pe, ("hT", NT, j))
                        grouped((name, "s"), 2, width, w, hTs)
                    if t == 1:
                        banks.wait_drained(pe, (name, "s"))
                        banks.begin(pe, (name, "S"), 3)
                        mm = pe.matmul(psum[0:NS, 3, 0:width], C("sel_s"), G[:, 1, 0:width], start=True, stop=True)
                        banks.filled(mm, (name, "S"))
                last_use[name] = (name, NT - 1)

            def feature_block(name, w, rhs, b0, f, first=True, last=True):
                kk = w.shape[1]
                for k in range(kk):
                    for s in range(2):
                        mm = pe.matmul(psum[:, b0 + s, 0:HALF], w[:, k, f * P:(f + 1) * P],
                                       rhs[:, k, s * HALF:(s + 1) * HALF],
                                       start=(first and k == 0), stop=(last and k == kk - 1))
                return mm

            rows_slice("A", NA)

            pe.wait_ge(a_ready, 1)
            for t in range(NT):
                b = 4 + t % 2
                banks.begin(pe, ("qkiT", t), b)
                for j in range(3):
                    src = araw[:, t, j * P:(j + 1) * P] if j < 2 else ki_twice[:, t, :]
                    mm = pe.transpose(psum[:, b, j * P:(j + 1) * P], src, ident)
                banks.filled(mm, ("qkiT", t))
            pe.wait_ge(qi_dup_ready, 1)
            banks.begin(pe, "qi_sample", 4)
            for h in range(IH):
                mm = pe.transpose(psum[:, 4, h * NS:(h + 1) * NS], qi_twice[0:NS, h].rearrange("p c d -> p (c d)"),
                                  ident[0:NS, 0:NS])
            banks.filled(mm, "qi_sample")
            banks.begin(pe, "wi_sample", 5)
            for c in range(4):
                mm = pe.transpose(psum[:, 5, c * NS:(c + 1) * NS], wi_place[0:NS, c * P:(c + 1) * P], ident[0:NS, 0:NS])
            banks.filled(mm, "wi_sample")

            for qb in range(1, NT):
                L = (qb + 1) * P
                if qb == 1:
                    for t in range(NT):
                        banks.wait_drained(pe, ("qkiT", t))
                banks.begin(pe, ("dots", qb), 0, 1, 2, 3)
                for h in range(IH):
                    o = HD * (h % 2)
                    mm = pe.matmul(psum[:, h, 0:L], qiT[o:o + ID, h // 2, qb * P:(qb + 1) * P], kiT[o:o + ID, 0:L],
                                   start=True, stop=True)
                banks.filled(mm, ("dots", qb))

            for b in range(NS):
                pe.wait_ge(ki_in[b % 2], 16 * (b // 2 + 1))
                for j in range(2):
                    banks.begin(pe, ("kiT", b, j), 4 + j)
                    for k in range(4):
                        r = 4 * j + k
                        mm = pe.transpose(psum[:, 4 + j, k * P:(k + 1) * P], ki_pages[:, b % 2, r * P:(r + 1) * P], ident)
                    banks.filled(mm, ("kiT", b, j))
                q = 32 * (b % 4)
                for j in range(2):
                    banks.wait_drained(pe, ("kiT", b, j))
                    if b % 4 == 0 and j == 0:
                        banks.wait_drained(pe, "qi_sample")
                        banks.begin(pe, ("dotsS", b // 4), 0 + 2 * (b // 4), 1 + 2 * (b // 4))
                    mm = pe.matmul(psum[q:q + 32, 2 * (b // 4) + j, :], qi_lhs[:, b, :],
                                   ki_T[:, b % 2, j * 512:(j + 1) * 512], start=True, stop=True, tile_position=(0, q))
                if b % 4 < 3:
                    mm.then_inc(ki_used, 1)
                else:
                    banks.filled(mm, ("dotsS", b // 4))
            banks.wait_drained(pe, "wi_sample")
            banks.wait_drained(pe, ("dotsS", 0))
            banks.wait_drained(pe, ("dotsS", 1))
            banks.begin(pe, "scoresS", 0, 1, 2, 3)
            for par in range(2):
                for j in range(2):
                    for g in range(2):
                        mm = pe.matmul(psum[0:NS, 2 * par + j, :], wi_lhs[:, 2 * g + par, :],
                                       relu_s[:, g, j * 512:(j + 1) * 512], start=(g == 0), stop=(g == 1))
            banks.filled(mm, "scoresS")

            rows_slice("B", NB)
            rows_slice("C", NC)
            rows_slice("D", ND)
            def blocks(ring_name, key, rhs, n, b_of):
                ring_wait(pe, ring_name)
                w = ring_at(ring_name, 512)
                for f in range(n):
                    banks.begin(pe, (key, f), b_of(f), b_of(f) + 1)
                    mm = feature_block((key, f), w, rhs, b_of(f), f)
                    banks.filled(mm, (key, f))
                last_use[ring_name] = (key, n - 1)

            blocks("U", "U", hT, 4, lambda f: 2 * (f % 2))

            pe.wait_ge(q_ready, 1)
            for t in range(NT):
                b = 4 + t % 2
                banks.begin(pe, ("qT", t), b)
                for j in range(4):
                    mm = pe.transpose(psum[:, b, j * P:(j + 1) * P], qraw[:, t, j * P:(j + 1) * P], ident)
                banks.filled(mm, ("qT", t))
            pe.wait_ge(k_ready, 1)
            banks.begin(pe, "kT", 6)
            for t in range(NT):
                mm = pe.transpose(psum[:, 6, t * P:(t + 1) * P], kraw[:, t, :], ident)
            banks.filled(mm, "kT")
            banks.begin(pe, "qkT_s", 7)
            for j in range(5):
                src = qraw[0:NS, NT, j * P:(j + 1) * P] if j < 4 else kraw[0:NS, NT, :]
                mm = pe.transpose(psum[:, 7, j * NS:(j + 1) * NS], src, ident[0:NS, 0:NS])
            banks.filled(mm, "qkT_s")

            pe.wait_ge(vg_ready, 1)
            pe.wait_ge(ws_masked, 1)
            for j in range(4):
                b = 4 + j % 2
                banks.begin(pe, ("mix", j), b)
                for c in range(NT):
                    for par in range(2):
                        g = 2 * j + par
                        mm = pe.matmul(psum[GD * par:GD * par + GD, b, c * P:(c + 1) * P], vg[:, c, g * GD:(g + 1) * GD],
                                       wsT[:, g, :], start=True, stop=True, tile_position=(0, GD * par))
                banks.filled(mm, ("mix", j))
            banks.begin(pe, "vgT_s", 6)
            for j in range(4):
                mm = pe.transpose(psum[:, 6, j * NS:(j + 1) * NS], vg[0:NS, NT, j * P:(j + 1) * P], ident[0:NS, 0:NS])
            banks.filled(mm, "vgT_s")

            groups = [(qb, kv) for qb in range(NT) for kv in range(NKV)]

            def att_scores(g):
                qb, kv = groups[g]
                L = (qb + 1) * P
                o = HD * kv
                if g == 0:
                    for t in range(NT):
                        banks.wait_drained(pe, ("qT", t))
                    banks.wait_drained(pe, "kT")
                banks.begin(pe, ("att_s", g), 0, 1, 2, 3)
                for j in range(4):
                    mm = pe.matmul(psum[:, j, 0:L], qT[o:o + HD, j, qb * P:(qb + 1) * P], kT[o:o + HD, 0:L],
                                   start=True, stop=True)
                banks.filled(mm, ("att_s", g))

            def att_values(g):
                qb, kv = groups[g]
                pe.wait_ge(probs_ready, g + 1)
                for c in range(qb + 1):
                    b = 4 + c % 2
                    banks.begin(pe, ("probsT", g, c), b)
                    for j in range(4):
                        mm = pe.transpose(psum[:, b, j * P:(j + 1) * P], soft[g % 2][:, j, c * P:(c + 1) * P], ident)
                    banks.filled(mm, ("probsT", g, c))
                if kv == 0:
                    banks.begin(pe, ("att", qb), 6 + qb % 2)
                for c in range(qb + 1):
                    banks.wait_drained(pe, ("probsT", g, c))
                    mm = pe.matmul(psum[HD * kv:HD * kv + HD, 6 + qb % 2, :], araw[:, c, VV + HD * kv:VV + HD * kv + HD],
                                   probsT[:, c, :], start=(c == 0), stop=(c == qb), tile_position=(0, HD * kv))
                if kv == 1:
                    banks.filled(mm, ("att", qb))
                else:
                    mm.then_inc(values_done, 1)

            def gate_block(n):
                c, f = n // 4, n % 4
                name = f"G{c}"
                if f == 0:
                    ring_wait(pe, name)
                banks.begin(pe, (name, f), 2 * (f % 2), 2 * (f % 2) + 1)
                banks.filled(feature_block((name, f), ring_at(name, 512), hT, 2 * (f % 2), f), (name, f))
                last_use[name] = (name, f)

            att_scores(0)
            for g in range(len(groups)):
                if g + 1 < len(groups):
                    att_scores(g + 1)
                att_values(g)
                gate_block(2 * g)
                gate_block(2 * g + 1)
                ada_product(4 + g, 6 + (g // NKV + 1) % 2)

            ring_wait(pe, "WG")
            pe.wait_ge(gm_ready, 1)
            for f in range(KD):
                b = 2 + 4 * (f % 2)
                banks.begin(pe, ("WG", f), b, b + 1)
                banks.filled(feature_block(("WG", f), ring_at("WG", D), uT, b, f), ("WG", f))
            last_use["WG"] = ("WG", KD - 1)

            pe.wait_ge(idx_ready, 1)
            banks.begin(pe, "idxT", 4)
            for h in range(2):
                mm = pe.transpose(psum[:, 4, h * NS:(h + 1) * NS], idx_f[0:NS, h * P:(h + 1) * P], ident[0:NS, 0:NS])
            banks.filled(mm, "idxT")

            def attention_half(part):
                for f in range(KD):
                    name, b = ("WA", part, f), 4 * part + f % 2
                    banks.begin(pe, name, b)
                    for k in range(4):
                        mm = pe.matmul(psum[:, b, 0:HALF], ring_at("WA", D)[:, k, f * P:(f + 1) * P],
                                       attT[:, k, part * HALF:(part + 1) * HALF], start=(k == 0), stop=(k == 3))
                    banks.filled(mm, name)
                last_use["WA"] = ("WA", part, KD - 1)

            ring_wait(pe, "WA")
            for t in range(NT):
                banks.wait_drained(pe, ("att", t))
            attention_half(0)
            pe.wait_ge(k_sel_in, 16 * 2 * NS)
            for b in range(NS):
                bank = 6 + b % 2
                banks.begin(pe, ("k_selT", b), bank)
                for h in range(2):
                    mm = pe.transpose(psum[:, bank, h * P:(h + 1) * P], k_sel[:, h * NS + b, :], ident)
                banks.filled(mm, ("k_selT", b))
            pe.wait_ge(key_bias_ready, 1)
            pe.wait_ge(q_lhs_ready, 2)
            spread = C("spread").rearrange("p (g n) -> p g n", g=2)
            for g in range(2):
                banks.begin(pe, ("att_ss", g), g)
                pe.matmul(psum[:, g, 0:TOPK_S + 1], spread[0:NS, g, :], key_bias[0:NS, :], start=True, stop=False,
                          skip_group_check=True)
                for i in range(4):
                    b = 4 * g + i
                    banks.wait_drained(pe, ("k_selT", b))
                    pe.matmul(psum[32 * i:32 * i + 32, g, 0:TOPK_S], q_lhs[:, b, :], k_selT[:, b, :],
                              start=False, stop=True, skip_group_check=True, tile_position=(0, 32 * i))
                    mm = pe.matmul(psum[32 * i:32 * i + 32, g, TOPK_S:TOPK_S + 1], q_lhs[:, b, :],
                                   kT[:, SEQ + b:SEQ + b + 1], start=False, stop=True, skip_group_check=True,
                                   tile_position=(0, 32 * i))
                banks.filled(mm, ("att_ss", g))
            pe.wait_ge(probs_s_ready, 1)
            banks.begin(pe, "probsT_s", 2)
            for g in range(2):
                for h in range(2):
                    a = 2 * g + h
                    mm = pe.transpose(psum[:, 2, a * P:(a + 1) * P], soft_s[:, g, h * P:(h + 1) * P], ident)
            banks.filled(mm, "probsT_s")
            banks.begin(pe, "new_probs", 3)
            rows_of = C("gather").rearrange("p (g b) -> p g b", g=2)
            for g in range(2):
                mm = pe.matmul(psum[0:NS, 3, 0:NH], rows_of[:, g, :], new_probs[:, g, :], start=(g == 0), stop=(g == 1))
            banks.filled(mm, "new_probs")
            pe.wait_ge(new_spread_ready, 1)
            pe.wait_ge(v_sel_in, 16 * 2 * NS)
            banks.wait_drained(pe, "probsT_s")
            banks.begin(pe, "att_samples", 4)
            pe.matmul(psum[:, 4, 0:NS * NH], araw[0:NS, NT, VV:VV + NKV * HD], new_spread[0:NS, :], start=True, stop=False,
                      skip_group_check=True)
            for b in range(NS):
                for h in range(2):
                    o = 32 * (b % 4)
                    mm = pe.matmul(psum[:, 4, b * NH:(b + 1) * NH], v_sel[:, h * NS + b, :],
                                   probsT_s[:, 2 * (b // 4) + h, o:o + NH], start=False, stop=True, skip_group_check=True)
            banks.filled(mm, "att_samples")

            banks.wait_drained(pe, "att_samples")
            attention_half(1)
            for c in range(4, 12):
                ada_spread(c)

            pe.wait_ge(merged, KD)
            rows_slice("O0", 512)
            rows_slice("O1", 512)

            for i, (_, n, t) in enumerate(ORDER):
                pe.wait_ge(t2_ready, i + 1)
                for j in range(2):
                    b = 4 + j
                    banks.begin(pe, ("t2T", t, j), b)
                    for k in range(4):
                        mm = pe.transpose(psum[:, b, k * n:(k + 1) * n], t2[0:n, t, (4 * j + k) * P:(4 * j + k + 1) * P],
                                          ident[0:n, 0:n])
                    banks.filled(mm, ("t2T", t, j))
            for t in range(T5):
                for j in range(2):
                    banks.wait_drained(pe, ("t2T", t, j))
            pe.wait_ge(router_in, 32)
            banks.begin(pe, "logits", 0, 1)
            for k in range(KD):
                for s in range(2):
                    mm = pe.matmul(psum[0:NEG + NE, s, 0:HALF], w_router[:, k, :], hT[:, k, s * HALF:(s + 1) * HALF],
                                   start=(k == 0), stop=(k == KD - 1))
            banks.filled(mm, "logits")
            banks.wait_drained(pe, "logits")
            banks.begin(pe, "logits_rows", 2)
            for t in range(T5):
                n = P if t < NT else NS
                mm = pe.transpose(psum[0:n, 2, t * 36:t * 36 + 36], logits_T[0:36, t * P:t * P + n], ident[0:36, 0:36])
            banks.filled(mm, "logits_rows")
            pe.wait_ge(chosen_ready, 1)
            banks.begin(pe, "places", 3)
            for t in range(T5):
                o = slice(t * NE, (t + 1) * NE)
                pe.matmul(psum[:, 3, o], C("before"), chosen[:, t, :], start=True, stop=False, skip_group_check=True)
                pe.matmul(psum[:, 3, o], C("ones"), before_sum[:, t, :], start=False, stop=True, skip_group_check=True)
            mm = pe.matmul(psum[:, 3, T5 * NE:(T5 + 1) * NE], C("ones"), before_sum[:, T5, :], start=True, stop=True)
            banks.filled(mm, "places")
            pe.wait_ge(tables_hot_ready, 1)
            banks.begin(pe, "tables", 4)
            for a in range(2 * T5):
                mm = pe.matmul(psum[:, 4, 0:2 * N_ITEMS], slot_hot[:, a, :], item_hot[:, a, :],
                               start=(a == 0), stop=(a == 2 * T5 - 1))
            banks.filled(mm, "tables")

            def x_transposes(p, full):
                for k in range(KD):
                    mm = pe.transpose(psum[:, p, k * SB:(k + 1) * SB], x_rows[0:SB, p, k * P:(k + 1) * P],
                                      ident[0:SB, 0:SB])
                mm.then_inc(full, 1)

            def gate_up(p, w, full):
                for k in range(KD):
                    for half in range(2):
                        col = DE * (1 - half)
                        mm = pe.matmul(psum[SB * half:SB * half + SB, 2 + p, 0:DE], x_T[:, p, k, :],
                                       w[:, k, col:col + DE], start=(k == 0), stop=(k == KD - 1),
                                       tile_position=(0, SB * half))
                mm.then_inc(full, 1)

            def hidden_transposes(p, full):
                for f in range(2):
                    mm = pe.transpose(psum[:, 4 + p, f * SB:(f + 1) * SB], hidden[0:SB, p, f * P:(f + 1) * P],
                                      ident[0:SB, 0:SB])
                mm.then_inc(full, 1)

            def down(p, w, full):
                for f in range(2):
                    for half in range(2):
                        mm = pe.matmul(psum[SB * half:SB * half + SB, 6 + p, :], hidden_T[:, p, f, :],
                                       w[:, f, 512 * half:512 * half + 512], start=(f == 0), stop=(f == 1),
                                       tile_position=(0, SB * half))
                mm.then_inc(full, 1)

            for name in ("logits", "logits_rows", "places", "tables"):
                banks.wait_drained(pe, name)
            pe.wait_ge(x_got[0], 16)
            x_transposes(0, xT_full)

            def pe_item(i, k, first):
                e, p = i * 4 + k, k % 2
                pe.wait_ge(w_got[k], i * 16 + 16)
                pe.wait_ge(xT_out, e + 1)
                if not (first and k < 2):
                    pe.wait_ge(hidden_done, e - 1)
                gate_up(p, w_gu[k], gu_full)
                if not (first and k < 1):
                    pe.wait_ge(xT_out, e)
                lone_wait(pe, x_got[1 - p], i * 32 + 16 * ((k + 1) // 2) + 16, pe_passed)
                x_transposes(1 - p, xT_full)
                if not (first and k < 2):
                    pe.wait_ge(hT_out, e - 1)
                lone_wait(pe, hidden_done, e + 1, pe_passed)
                hidden_transposes(p, hT_full)
                pe.wait_ge(hT_out, e + 1)
                if not (first and k < 2):
                    pe.wait_ge(y_out, e - 1)
                down(p, w_dn[k], y_full)

            n_items = each_item(pe, pe_item)
            pe.wait_ge(pe_passed, n_items * 2)
            lone_wait(pe, xT_out, n_items + 1, pe_finished)

        @block.sync
        def _(sp):
            sp.dma_start(const[:, :], io["consts"]).then_inc(const_in, 16)
            sp.dma_start(ada_bias[0:12, :], io["b_ada"]).then_inc(ada_bias_in, 16)
            sp.dma_start(c_T[:, :, :], io["c_T"].rearrange("p (k n) -> p k n", k=KD)).then_inc(c_in, 16)
            for n, (name, size) in enumerate(STREAM):
                if n == 1:
                    sp.dma_start(gain1, io["norm_mix_g"].partition_broadcast(P)).then_inc(bias_in, 16)
                if n == 2:
                    sp.dma_start(gains[:, :], io["head_gains"].partition_broadcast(P)).then_inc(bias_in, 16)
                if n >= RING:
                    banks.wait_full(sp, last_use[STREAM[n - RING][0]])
                sp.dma_start(ring[:, n % RING, 0:size], io["stream"][n, :, 0:size]).then_inc(ring_full[n % RING], 16)
            def expert_src(e):
                return io["experts"].rearrange("e p n -> (e p) n")[bass.ds(e * P, P), :]

            def load_w(k, e):
                sp.dma_start(expert_w[k], expert_src(e)).then_inc(w_got[k], 16)

            banks.wait_full(sp, last_use["O1"])
            load_w(0, 0)
            load_w(1, 1)
            sp.wait_ge(t2_ready, T5)
            load_w(2, 2)
            for t in range(T5):
                for j in range(2):
                    banks.wait_drained(sp, ("t2T", t, j))
            sp.wait_ge(t2_stored, 16 * T5)
            load_w(3, 3)
            sp.wait_ge(over_zeroed, 16)

            def store_item(i, k):
                e, p = i * 4 + k, k % 2
                sp.wait_ge(y_out, e + 1)
                for half in range(2):
                    dst = io["expert_rows"][bass.ds(e * SB, SB), 512 * half:512 * half + 512]
                    sp.dma_start(dst, y_rows[SB * half:SB * half + SB, p, :]).then_inc(y_stored[p], 16)

            def sp_item(i, k):
                e = i * 4 + k
                sp.wait_ge(y_full, e + 1)
                load_w(k, e + 4)
                store_item(i, k)

            def load_if_any(i, k, n_items):
                e = i * 4 + k
                with sp.If(e + 4 < n_items):
                    expert = sp.value_load(over_expert[0:1, bass.ds(e + 4 - NE, 1)], min_val=0, max_val=NE - 1)
                    sp.wait_ge(y_full, e + 1)
                    load_w(k, expert)

            for k in range(4):
                sp_item(0, k)
            with sp.Fori(1, NE // 4 - 1) as i:
                for k in range(4):
                    sp_item(i, k)
            n_items = load_n_items(sp)
            for k in range(4):
                load_if_any(NE // 4 - 1, k, n_items)
                store_item(NE // 4 - 1, k)
            with sp.Fori(NE // 4, N_ITEMS // 4) as i:
                for k in range(4):
                    load_if_any(i, k, n_items)
                    with sp.If(i * 4 + k < n_items):
                        store_item(i, k)
            stores = [load_n_items(sp, 1), load_n_items(sp, 2)]
            sp.wait_ge(pe_finished, 1)
            sp.wait_ge(pool_finished, 1)
            for p in range(2):
                sp.wait_ge(y_stored[p], stores[p])
            sp.sem_inc(experts_done, 1)
            for i, (_, n, t) in enumerate([(t, P if t < NT else NS, t) for t in range(T5)]):
                sp.wait_ge(y_ready, i + 1)
                dst = io["y_p"][t * P:(t + 1) * P, :] if t < NT else io["y_s"]
                sp.dma_start(dst, x2[0:n, t, :]).then_inc(y_outs, 16)
            sp.wait_ge(y_outs, 16 * T5)

        @block.gpsimd
        def _(pool):
            lane = Lane(pool, pool_lane)

            def rsqrt(n_asked, out, in_, width):
                pool.wait_ge(rstd_asked, n_asked)
                pool.tensor_tensor(out, in_, minus_half[:, 0:width], ALU.pow).then_inc(rstd_ready, 1)

            def store(dst, src):
                pool.dma_start(dst, src).then_inc(outs, 16)
                n_outs[0] += 1

            for t in range(NT):
                pool.dma_start(xbuf[:, t, :], io["x_prompt"][t * P:(t + 1) * P, :]).then_inc(x_in[t], 16)
            pool.dma_start(xbuf[0:NS, NT, :], io["x_sample"]).then_inc(x_in[NT], 16)
            pool.dma_start(page_rep, io["page_rep"]).then_inc(pages_in, 16)
            pool.dma_start(ln, io["ln"].partition_broadcast(P)).then_inc(ln_in, 16)
            pool.dma_start(wsT, io["ws_T"].rearrange("p (g t) -> p g t", g=GG)).then_inc(ws_in, 16)
            gm_b = io["gm_b"].rearrange("(j c) t -> c j t", c=2)
            for par in range(2):
                rows = slice(GD * par, GD * par + GD)
                pool.dma_start(bT[rows], gm_b[par].partition_broadcast(GD)).then_inc(gmlp_in, 16)
                pool.dma_start(gm_w0[rows], io["ws_00"][par].partition_broadcast(GD)).then_inc(gmlp_in, 16)
            pool.wait_ge(ws_in, 16)
            pool.affine_select(out=wsT, in_=wsT, pattern=[[0, GG], [1, CHUNK]], compare_op=ALU.is_ge, fill=0.0,
                               base=0, channel_multiplier=-1).then_inc(ws_masked, 1)
            pool.wait_ge(zeroed, 1)
            rsqrt(1, rstd, ssq, 5)

            pool.wait_ge(page_rows_ready, 1)
            banks.wait_drained(pool, ("hT", NT, 1))
            for b in range(NS):
                if b >= 2:
                    banks.wait_full(pool, ("kiT", b - 2, 1))
                pool.indirect_dma_start(ki_pages[:, b % 2, :], None, io["cache_ki"],
                                        bass.IndirectOffsetOnAxis(page_rows[:, b:b + 1], 0)).then_inc(ki_in[b % 2], 16)
                if b == 1:
                    rsqrt(2, ki_r, ki_ms, 5)
            pool.wait_ge(a_ready, 1)
            store(io["new_ki_p"].rearrange("(t p) d -> p t d", p=P), araw[:, 0:NT, KI:KI + ID])
            store(io["new_ki_s"], araw[0:NS, NT, KI:KI + ID])
            store(io["new_v_p"].rearrange("(t p) d -> p t d", p=P), araw[:, 0:NT, VV:VV + P])
            store(io["new_v_s"], araw[0:NS, NT, VV:VV + P])
            over_rows = io["expert_rows"][NE * SB:, :].rearrange("(p a) (b n) -> p (a b) n", p=P, n=256)
            pool.dma_start(over_rows, spread_dim(zeros[:, :], 1, over_rows.shape[1])).then_inc(over_zeroed, 16)
            rsqrt(3, q_r, q_ms, 40)
            rsqrt(4, k_r, k_ms, 10)
            pool.wait_ge(k_ready, 1)
            store(io["new_k_p"].rearrange("(t p) d -> p t d", p=P), kraw[:, 0:NT, :])
            store(io["new_k_s"], kraw[0:NS, NT, :])
            rsqrt(5, vg_r, mu_var[:, :, 1], 5)
            pool.wait_ge(vg_ready, 1)
            pool.dma_start(io["new_vg_s"], vg[0:NS, NT, :]).then_inc(vg_s_stored, 16)
            pool.dma_start(pages_i, io["pages"].partition_broadcast(P)).then_inc(pages_all_in, 16)
            for qb in range(NT):
                banks.wait_drained(pool, ("att", qb))
            pool.wait_ge(sel_rows_ready, 1)
            for dst, src, got in ((k_sel, "cache_k", k_sel_in), (v_sel, "cache_v", v_sel_in)):
                for a in range(2 * NS):
                    pool.indirect_dma_start(dst[:, a, :], None, io[src], bass.IndirectOffsetOnAxis(sel_rows[:, a:a + 1], 0))\
                        .then_inc(got, 16)
            pool.wait_ge(merged, KD)
            pool.dma_start(gain2, io["norm_ffn_g"].partition_broadcast(P)).then_inc(late_in, 16)
            for t in range(NT):
                pool.dma_start(x2[:, t, :], io["x_prompt"][t * P:(t + 1) * P, :]).then_inc(x2_in, 16)
            pool.dma_start(x2[0:NS, NT, :], io["x_sample"]).then_inc(x2_in, 16)
            pool.dma_start(w_router, io["w_router"].rearrange("p (k n) -> p k n", k=KD)).then_inc(router_in, 16)
            pool.dma_start(b_router, io["b_router"].partition_broadcast(P)).then_inc(router_in, 16)
            rsqrt(6, rstd, ssq, 5)
            pool.wait_ge(t2_stored, 16 * T5)
            pool.wait_ge(tables_ready, 1)
            for e in range(NE + 1):
                if e >= 2:
                    pool.wait_ge(xT_full, e - 1)
                pool.indirect_dma_start(x_rows[0:SB, e % 2, :], None, io["t2_rows"],
                                        bass.IndirectOffsetOnAxis(token_tab[0:SB, e:e + 1], 0)).then_inc(x_got[e % 2], 16)
            n_items = load_n_items(pool)
            pool.sem_inc(pool_passed, 2 * NE)
            with pool.Fori(NE // 4, N_ITEMS // 4) as i:
                for k in range(4):
                    e, p = i * 4 + k, k % 2
                    with pool.If(e < n_items):
                        lone_wait(pool, xT_full, e, pool_passed)
                        pool.tensor_copy(next_token[0:SB, 1 - p:2 - p], token_tab[0:SB, bass.ds(e + 1, 1)])\
                            .then_inc(token_copied, 1)
                        lone_wait(pool, token_copied, e + 1 - NE, pool_passed)
                        pool.indirect_dma_start(x_rows[0:SB, 1 - p, :], None, io["t2_rows"],
                                                bass.IndirectOffsetOnAxis(next_token[0:SB, 1 - p:2 - p], 0))\
                            .then_inc(x_got[1 - p], 16)
            lone_wait(pool, pool_passed, n_items * 2, pool_finished)
            pool.wait_ge(experts_done, 1)
            pool.wait_ge(y_full, NE)
            for t in range(T5):
                n = P if t < NT else NS
                for c in range(2):
                    a = c * T5 + t
                    pool.indirect_dma_start(picked[0:n, t, c, :], None, io["expert_rows"],
                                            bass.IndirectOffsetOnAxis(rank_i[0:n, a:a + 1], 0)).then_inc(picked_in[t], 16)
            pool.wait_ge(outs, 16 * n_outs[0])

        @block.scalar
        def _(act):
            lane = Lane(act, scalar_lane)
            act.wait_ge(c_in, 16)
            act.activation(c_T[:, :, :], c_T[:, :, :], ACT.Silu).then_inc(c_silu, 1)

            def evac(name, pairs, func=ACT.Copy, scale=1.0):
                banks.wait_full(act, name)
                for out, in_ in pairs:
                    ins = act.activation(out, in_, func, scale=scale)
                banks.drained(ins, name)

            def ada_out(c):
                if c >= 2:
                    banks.wait_full(act, ("adaS", c - 2))
                evac(("ada", c), [(G[:, c % 2, :], psum[:, c % 2, :])])

            act.wait_ge(zeroed, 1)
            for t in range(NT + 1):
                n = P if t < NT else NS
                act.wait_ge(x_in[t], 16)
                lane.wait()
                ins = act.activation(junk[0:n, :], xbuf[0:n, t, :], ACT.Square, accum_out=ssq[0:n, t:t + 1])
                lane.mark(ins) if t < NT else ins.then_inc(ssq_ready, 1)
            for c in range(4):
                ada_out(c)
            for t in range(NT):
                for j in range(2):
                    evac(("hT", t, j), [(hT[:, 4 * j:4 * j + 4, t * P:(t + 1) * P],
                                         psum[:, 6 + j, :].rearrange("p (k n) -> p k n", k=4))])
            for j in range(2):
                src = psum[:, 6 + j, 0:4 * NS].rearrange("p (k n) -> p k n", k=4)
                evac(("hT", NT, j), [(hT[:, 4 * j:4 * j + 4, SEQ:TOK], src), (hTs[:, 4 * j:4 * j + 4, 0:NS], src)])

            def rows_out(name, outs_of, gelu_from=None):
                def go(part, rows, t):
                    b = {"S": 3}.get(part, t % 2)
                    banks.wait_full(act, (name, part))
                    for dst, o, w, func in outs_of:
                        ins = act.activation(dst[0:rows, t, :], psum[0:rows, b, o:o + w], func)
                    banks.drained(ins, (name, part))
                width = sum(w for _, _, w, _ in outs_of)
                go(0, P, 0)
                evac((name, "s"), [(G[:, 1, 0:width], psum[:, 2, 0:width])])
                go(1, P, 1)
                go("S", NS, NT)
                go(2, P, 2)
                go(3, P, 3)

            banks.wait_full(act, ("adaS", 3))
            banks.wait_full(act, ("adaS", 2))
            act.wait_ge(zeroed, 2)
            rows_out("A", [(araw, 0, NA, ACT.Copy)])
            for t in range(NT):
                b = 4 + t % 2
                evac(("qkiT", t), [
                    (qiT[:, :, t * P:(t + 1) * P], psum[:, b, 0:2 * P].rearrange("p (j n) -> p j n", j=2)),
                    (kiT[:, t * P:(t + 1) * P], psum[:, b, 2 * P:3 * P])])
            src = psum[:, 4, 0:IH * NS].rearrange("p (h b) -> p b h", h=IH)
            act.wait_ge(qi_lhs_ready, 1)
            evac("qi_sample", [(qi_lhs[0:ID, :, 0:IH], src[0:ID]), (qi_lhs[ID:P, :, IH:2 * IH], src[ID:P])])
            evac("wi_sample", [(wi_lhs, psum[:, 5, 0:4 * NS].rearrange("p (c b) -> p c b", c=4))])
            index_scale = ID ** -0.5 * IH ** -0.5
            for qb in range(1, NT):
                L = (qb + 1) * P
                if qb > 1:
                    act.wait_ge(relu_p_read, qb - 1)
                evac(("dots", qb), [(relu_p[:, :, 0:L], psum[:, 0:4, 0:L])], ACT.Relu, index_scale)
            for b in range(NS):
                if b >= 2 and (b - 2) % 4 == 3:
                    banks.wait_full(act, ("dotsS", (b - 2) // 4))
                elif b >= 2:
                    act.wait_ge(ki_used, (b - 1) - (b - 1) // 4)
                for j in range(2):
                    evac(("kiT", b, j), [(ki_T[:, b % 2, j * 512:(j + 1) * 512], psum[:, 4 + j, :])])
                if b % 4 == 3:
                    g = b // 4
                    evac(("dotsS", g), [(relu_s[:, g, :].rearrange("p (j n) -> p j n", j=2), psum[:, 2 * g:2 * g + 2, :])],
                         ACT.Relu, index_scale)
            banks.wait_full(act, "scoresS")
            for half in range(2):
                view = scores[32 * half:32 * half + NS, 0:PAST // 2].rearrange("s (n r e) -> s e r n", r=8, e=2)
                for par in range(2):
                    src = psum[0:NS, 2 * par:2 * par + 2, :].rearrange("s j (r n) -> s (j r) n", r=4)
                    ins = act.activation(view[:, par], src[:, :, 64 * half:64 * half + 64], ACT.Copy)
            banks.drained(ins, "scoresS")
            rows_out("B", [(qraw, 0, NB, ACT.Copy)])
            rows_out("C", [(kraw, 0, NKV * HD, ACT.Copy), (vg[:, :, 0:VG0], NKV * HD, VG0, ACT.Gelu_apprx_tanh)])
            rows_out("D", [(vg[:, :, VG0:GM], 0, ND, ACT.Gelu_apprx_tanh)])
            for f in range(4):
                b = 2 * (f % 2)
                evac(("U", f), [(halves(uT[:, f, :]), pair(b))], ACT.Gelu_apprx_tanh)
            for t in range(NT):
                if t == 0:
                    banks.wait_drained(act, "scoresS")
                evac(("qT", t), [(qT[:, :, t * P:(t + 1) * P], psum[:, 4 + t % 2, :].rearrange("p (j n) -> p j n", j=4))])
            evac("kT", [(kT[:, 0:SEQ], psum[:, 6, :])])
            evac("qkT_s", [(qT[:, :, SEQ:TOK], psum[:, 7, 0:4 * NS].rearrange("p (j n) -> p j n", j=4)),
                           (kT[:, SEQ:TOK], psum[:, 7, 4 * NS:5 * NS])])
            def exponentials(g):
                L = (g // NKV + 1) * P
                act.wait_ge(max_ready, g + 1)
                for j in range(4):
                    s_j = soft[g % 2][:, j, 0:L]
                    ins = act.activation(s_j, s_j, ACT.Exp, bias=mx4[g % 2][:, j:j + 1], accum_out=sum4[g % 2][:, j:j + 1])
                ins.then_inc(exp_ready, 1)

            act.wait_ge(vg_ready, 1)
            exponentials(0)
            for g, (qb, kv) in enumerate([(qb, kv) for qb in range(NT) for kv in range(NKV)]):
                for c in range(qb + 1):
                    if g and kv == 1:
                        act.wait_ge(values_done, qb + 1)
                    elif g:
                        banks.wait_full(act, ("att", qb - 1))
                    evac(("probsT", g, c), [(probsT[:, c, :], psum[:, 4 + c % 2, :])])
                if kv == 1:
                    evac(("att", qb), [(attT[:, :, qb * P:(qb + 1) * P],
                                        psum[:, 6 + qb % 2, :].rearrange("p (j n) -> p j n", j=4))])
                if g + 1 < NT * NKV:
                    exponentials(g + 1)
                for n in (2 * g, 2 * g + 1):
                    c, f = n // 4, n % 4
                    to = 2 * c + f if f < 2 else KD + 2 * c + f - 2
                    evac((f"G{c}", f), [(halves(gates[:, to, :]), pair(2 * (f % 2)))], ACT.Sigmoid)
                if g == 3:
                    act.wait_ge(gm_ready, 1)
                if g == 6:
                    act.wait_ge(vg_s_stored, 16)
                evac(("ada", 4 + g), [(late_G[g], psum[:, 6 + (qb + 1) % 2, :])])
            for b in range(NS):
                if b == 0:
                    act.wait_ge(probs_ready, 8)
                evac(("k_selT", b), [(k_selT[:, b, :], psum[:, 6 + b % 2, 0:2 * P])])
            act.wait_ge(max_s_ready, 1)
            for g in range(2):
                ins = act.activation(soft_s[:, g, :], psum[:, g, 0:TOPK_S + 1], ACT.Exp, bias=mx2[:, g:g + 1],
                                     scale=HD ** -0.5, accum_out=sum2[:, g:g + 1])
                banks.drained(ins, ("att_ss", g))
            evac("probsT_s", [(probsT_s, psum[:, 2, :].rearrange("p (a n) -> p a n", n=P))])
            src = psum[:, 4, 0:NS * NH].rearrange("p (b v j) -> p v j b", b=NS, v=NKV)
            evac("att_samples", [(attT[0:HD, :, SEQ:TOK], src[0:HD, 0]), (attT[HD:P, :, SEQ:TOK], src[HD:P, 1])])
            act.wait_ge(merged, KD)
            for c in (4, 5, 6, 7, 10, 11):
                m, half = ("gate1", "shift2", "scale2", "gate2")[c // 2 - 2], slice(512 * (c % 2), 512 * (c % 2) + 512)
                for g, name, b, rows in ((0, "adaP", 2 + c % 2, P), (1, "adaS", 4 + c % 2, NS)):
                    evac((name, c), [(mod2[m][0:rows, g, half], psum[0:rows, b, :])])
            for name in ("O0", "O1"):
                if name == "O0":
                    banks.wait_full(act, ("adaS", 10))
                    banks.wait_full(act, ("adaS", 11))
                else:
                    banks.wait_full(act, ("O0", "S"))
                evac((name, "s"), [(G[:, 1, :], psum[:, 2, :])])
            for i, (_, n, t) in enumerate(ORDER):
                act.wait_ge(x2_ready, i + 1)
                lane.wait()
                ins = act.activation(junk2[0:n, :], x2[0:n, t, :], ACT.Square, accum_out=ssq[0:n, t:t + 1])
                lane.mark(ins) if i < NT else ins.then_inc(ssq2_ready, 1)
            banks.wait_full(act, ("O1", 3))
            for i, (_, n, t) in enumerate(ORDER):
                cols = slice(t * P, t * P + n)
                for j in range(2):
                    evac(("t2T", t, j), [(hT[:, 4 * j:4 * j + 4, cols],
                                          psum[:, 4 + j, 0:4 * n].rearrange("p (k n) -> p k n", k=4))])
                dst = io["t2_rows"][t * P:t * P + n, :]
                act.dma_start(dst, t2[0:n, t, :]).then_inc(t2_stored, 16)
            evac("logits", [(halves(logits_T[0:NEG + NE]), psum[0:NEG + NE, 0:2, 0:HALF])])
            act.wait_ge(g_diff_ready, 1)
            act.activation(g_exp, g_tmp, ACT.Exp).then_inc(g_exp_ready, 1)
            act.wait_ge(e_diff_ready, 1)
            act.activation(e_ratio, e_ratio, ACT.Exp).then_inc(e_exp_ready, 1)

            def x_out(p, done):
                act.activation(x_T[:, p], psum[:, p, :].rearrange("p (k n) -> p k n", k=KD), ACT.Copy).then_inc(done, 1)

            def silu(p, done):
                act.activation(silu_g[0:SB, p, :], psum[SB:2 * SB, 2 + p, 0:DE], ACT.Silu).then_inc(done, 1)

            act.wait_ge(tables_ready, 1)
            act.wait_ge(xT_full, 1)
            x_out(0, xT_out)

            def act_item(i, k, first):
                e, p = i * 4 + k, k % 2
                act.wait_ge(gu_full, e + 1)
                if not (first and k < 2):
                    act.wait_ge(hidden_done, e - 1)
                silu(p, silu_done)
                act.wait_ge(xT_full, e + 2)
                if not (first and k < 1):
                    act.wait_ge(gu_full, e)
                x_out(1 - p, xT_out)

            each_item(act, act_item)

        @block.vector
        def _(dve):
            lane = Lane(dve, vector_lane)
            asked = [0]

            def rsqrt_of(ms, sums, count, wait=True):
                asked[0] += 1
                dve.tensor_scalar(ms, sums, 1.0 / count, EPS, ALU.mult, ALU.add).then_inc(rstd_asked, 1)
                if wait:
                    dve.wait_ge(rstd_ready, asked[0])

            def rope(rope_tmp, view, heads):
                nt = view.shape[1]
                t1 = rope_tmp[:, 0:nt * heads * ROT].rearrange("p (t h r) -> p t h r", t=nt, h=heads)
                t2 = rope_tmp[:, nt * heads * ROT:2 * nt * heads * ROT].rearrange("p (t h r) -> p t h r", t=nt, h=heads)
                cos = spread_dim(C("cos").rearrange("p (t r) -> p t r", r=ROT), 2, heads)
                sin = spread_dim(C("sin").rearrange("p (t r) -> p t r", r=ROT), 2, heads)
                half = ROT // 2
                dve.tensor_tensor(t1, view[:, :, :, 0:ROT], cos, ALU.mult)
                dve.tensor_tensor(t2[:, :, :, 0:half], view[:, :, :, half:ROT], sin[:, :, :, 0:half], ALU.mult)
                lane.then(dve.tensor_tensor(t2[:, :, :, half:ROT], view[:, :, :, 0:half], sin[:, :, :, half:ROT], ALU.mult))
                return dve.tensor_tensor(view[:, :, :, 0:ROT], t1, t2, ALU.add)

            lane.then(dve.memset(stat[:, 16:212], 0.0))
            dve.memset(minus_half, -0.5).then_inc(zeroed, 1)
            dve.memset(hTs[:, :, :], 0.0)
            dve.memset(zeros[:, :], 0.0)
            dve.memset(araw[:, NT, :], 0.0)
            dve.memset(kraw[:, NT, :], 0.0)
            lane.mark(dve.memset(scores[0:32 + NS], TAKEN))
            dve.memset(qi_lhs, 0.0).then_inc(qi_lhs_ready, 1)
            dve.wait_ge(pages_in, 16)
            dve.wait_ge(const_in, 16)
            dve.tensor_scalar(page_rows, page_rep, float(PAGE // 16), C("page_seg"), ALU.mult, ALU.add)\
               .then_inc(page_rows_ready, 1)
            dve.wait_ge(ssq_ready, 1)
            rsqrt_of(ssq, ssq, D, wait=False)
            dve.wait_ge(bias_in, 32)
            for c in range(4):
                m, half = c // 2, slice(512 * (c % 2), 512 * (c % 2) + 512)
                for g, name, b, rows in ((0, "adaP", 2 + c % 2, P), (1, "adaS", 4 + c % 2, NS)):
                    banks.wait_full(dve, (name, c))
                    out = mod1[0:rows, g, m, half]
                    if m == 0:
                        ins = dve.tensor_copy(out, psum[0:rows, b, :])
                    else:
                        ins = dve.scalar_tensor_tensor(out, psum[0:rows, b, :], 1.0, gain1[0:rows, half], ALU.add, ALU.mult)
                    banks.drained(ins, (name, c))
            for c in range(4):
                banks.wait_drained(dve, ("adaP", c))
                banks.wait_drained(dve, ("adaS", c))
            dve.wait_ge(rstd_ready, 1)
            for t in range(NT + 1):
                rows, g = (P, 0) if t < NT else (NS, 1)
                xt = xbuf[0:rows, t, :]
                lane.then(dve.scalar_tensor_tensor(xt, xt, rstd[0:rows, t:t + 1], mod1[0:rows, g, 1, :], ALU.mult, ALU.mult))
                dve.tensor_tensor(xt, xt, mod1[0:rows, g, 0, :], ALU.add).then_inc(h_ready, 1)
            dve.memset(vg[:, NT, :], 0.0)
            dve.memset(qraw[:, NT, :], 0.0).then_inc(zeroed, 1)

            for part in (0, 1, "S", 2, 3):
                banks.wait_drained(dve, ("A", part))
            ki = araw[:, :, KI:KI + ID]
            sq = ki_twice[:, :, 0:ID]
            lane.then(dve.tensor_tensor(sq, ki, ki, ALU.mult))
            lane.then(dve.tensor_reduce(ki_ms, sq, AX_X, ALU.add))
            rsqrt_of(ki_ms, ki_ms, ID)
            lane.then(dve.tensor_tensor(ki, ki, spread_dim(ki_r, 2, ID), ALU.mult))
            lane.then(dve.tensor_tensor(ki, ki, spread_dim(gains[:, 2 * HD:3 * HD], 1, NT + 1), ALU.mult))
            lane.then(rope(work, araw[:, :, 0:WI].rearrange("p t (h d) -> p t h d", d=ID), IH + 1))
            dve.tensor_copy(ki_twice.rearrange("p t (c d) -> p t c d", c=2), spread_dim(ki, 2, 2)).then_inc(a_ready, 1)
            qi_s = araw[0:NS, NT, QI:KI].rearrange("p (h d) -> p h d", h=IH)
            wi_s = araw[0:NS, NT, WI:VV]
            dve.tensor_copy(qi_twice[0:NS], spread_dim(qi_s, 2, 2))
            dve.tensor_tensor(wi_place[0:NS].rearrange("p (c h) -> p c h", h=IH),
                              C("place")[0:NS].rearrange("p (c h) -> p c h", h=IH), spread_dim(wi_s, 1, P), ALU.mult)\
               .then_inc(qi_dup_ready, 1)

            prod = work[0:NS, 0:IH * ID].rearrange("p (h d) -> p h d", h=IH)
            nd = new_dots[0:NS]
            lane.then(dve.tensor_tensor(prod, qi_s, spread_dim(araw[0:NS, NT, KI:KI + ID], 1, IH), ALU.mult))
            lane.then(dve.tensor_reduce(nd, prod, AX_X, ALU.add))
            lane.then(dve.tensor_scalar(nd, nd, ID ** -0.5 * IH ** -0.5, 0.0, ALU.mult, ALU.max))
            lane.then(dve.tensor_tensor(nd, nd, wi_s, ALU.mult))
            lane.then(dve.tensor_reduce(scores[32:32 + NS, PAST // 2:PAST // 2 + 1], nd, AX_X, ALU.add))

            w_at = {1: 0, 2: 256, 3: 640}
            for qb in range(1, NT):
                L = (qb + 1) * P
                s = work[:, w_at[qb]:w_at[qb] + L]
                banks.wait_drained(dve, ("dots", qb))
                lane.then(dve.tensor_scalar(s, relu_p[:, 0, 0:L], araw[:, qb, WI:WI + 1], None, ALU.mult))
                for h in range(1, IH):
                    ins = dve.scalar_tensor_tensor(s, relu_p[:, h, 0:L], araw[:, qb, WI + h:WI + h + 1], s,
                                                   ALU.mult, ALU.add)
                    if h < IH - 1:
                        lane.then(ins)
                ins.then_inc(relu_p_read, 1)
                dve.wait_ge(relu_p_read, qb)
                lane.mark(dve.tensor_tensor(s[:, L - P:L], s[:, L - P:L], C("causal"), ALU.add))
            lane.wait()
            for _ in range(TOPK_P // 8):
                for qb in range(1, NT):
                    lane.mark(dve.max(top8[:, 8 * (qb - 1):8 * qb], work[:, w_at[qb]:w_at[qb] + (qb + 1) * P]))
                lane.wait()
                for qb in range(1, NT):
                    s = work[:, w_at[qb]:w_at[qb] + (qb + 1) * P]
                    lane.mark(dve.match_replace(s, top8[:, 8 * (qb - 1):8 * qb], s, TAKEN))
                lane.wait()
            lane.then(dve.tensor_scalar(work, work, TAKEN / 2, -BIG, ALU.is_gt, ALU.mult))

            rounds = [0]

            def sample_rounds(n):
                s = scores[0:32 + NS, :]
                for r in range(rounds[0], min(rounds[0] + n, TOPK_S // 8)):
                    best = top_values[0:32 + NS, 8 * r:8 * r + 8]
                    lane.then(dve.max(best, s))
                    lane.mark(dve.max_index(idx_u[0:32 + NS, 8 * r:8 * r + 8], best, s))
                    lane.then(dve.match_replace(s, best, s, TAKEN))
                rounds[0] += n

            def norm_heads(raw, heads, ms, r, gain):
                view = raw.rearrange("p t (h d) -> p (t h) d", d=HD)
                sq = norm_tmp[:, 0:(NT + 1) * heads * HD].rearrange("p (a d) -> p a d", d=HD)
                lane.then(dve.tensor_tensor(sq, view, view, ALU.mult))
                lane.then(dve.tensor_reduce(ms, sq, AX_X, ALU.add))
                rsqrt_of(ms, ms, HD)
                lane.then(dve.tensor_tensor(view, view, spread_dim(r, 2, HD), ALU.mult))
                lane.then(dve.tensor_tensor(view, view, spread_dim(gain, 1, (NT + 1) * heads), ALU.mult))
                return rope(norm_tmp, raw.rearrange("p t (h d) -> p t h d", d=HD), heads)

            banks.wait_drained(dve, "scoresS")
            sample_rounds(ROUNDS[0])
            for part in (0, 1, "S", 2, 3):
                banks.wait_drained(dve, ("B", part))
            norm_heads(qraw, NH, q_ms, q_r, gains[:, 0:HD]).then_inc(q_ready, 1)
            for part in (0, 1, "S", 2, 3):
                banks.wait_drained(dve, ("C", part))
            dve.wait_ge(q_ready, 1)
            norm_heads(kraw, NKV, k_ms, k_r, gains[:, HD:2 * HD]).then_inc(k_ready, 1)
            sample_rounds(ROUNDS[1])
            for part in (0, 1, "S", 2, 3):
                banks.wait_drained(dve, ("D", part))
            dve.wait_ge(ln_in, 16)
            for t in range(NT + 1):
                lane.mark(dve.bn_stats(bn[:, t, :], vg[:, t, :]))
            lane.wait()
            for t in range(NT + 1):
                lane.mark(dve.bn_aggr(mu_var[:, t, :], bn[:, t, :]))
            lane.wait()
            rsqrt_of(mu_var[:, :, 1], mu_var[:, :, 1], 1)
            for t in range(NT + 1):
                lane.mark(dve.tensor_scalar(vg[:, t, :], vg[:, t, :], mu_var[:, t, 0:1], vg_r[:, t:t + 1],
                                            ALU.subtract, ALU.mult))
            lane.wait()
            lane.then(dve.tensor_tensor(vg, vg, spread_dim(ln[:, 0, :], 1, NT + 1), ALU.mult))
            dve.tensor_tensor(vg, vg, spread_dim(ln[:, 1, :], 1, NT + 1), ALU.add).then_inc(vg_ready, 1)
            sample_rounds(ROUNDS[2])
            dve.wait_ge(gmlp_in, 64)
            for j in range(4):
                banks.wait_drained(dve, ("U", j))
            mixed = norm_tmp[:, 0:SEQ]
            for j in range(4):
                banks.wait_full(dve, ("mix", j))
                banks.drained(dve.tensor_tensor(
                    mixed.rearrange("p (c t) -> p c t", t=P), psum[:, 4 + j % 2, :].rearrange("p (c t) -> p c t", t=P),
                    spread_dim(bT[:, j, :], 1, NT), ALU.add), ("mix", j))
                banks.wait_drained(dve, ("mix", j))
                dve.tensor_tensor(uT[:, j, 0:SEQ], uT[:, j, 0:SEQ], mixed, ALU.mult).then_inc(gm_tile, 1)
                dve.wait_ge(gm_tile, j + 1)
            banks.wait_full(dve, "vgT_s")
            ms = norm_tmp[:, 0:4 * NS].rearrange("p (j s) -> p j s", j=4)
            banks.drained(dve.tensor_tensor(ms, psum[:, 6, 0:4 * NS].rearrange("p (j s) -> p j s", j=4),
                                            spread_dim(gm_w0, 2, NS), ALU.mult), "vgT_s")
            banks.wait_drained(dve, "vgT_s")
            lane.then(dve.tensor_tensor(ms, ms, spread_dim(bT[:, :, 0], 2, NS), ALU.add))
            dve.tensor_tensor(uT[:, :, SEQ:TOK], uT[:, :, SEQ:TOK], ms, ALU.mult).then_inc(gm_ready, 1)
            dve.wait_ge(gm_ready, 1)

            for g, (qb, kv) in enumerate([(qb, kv) for qb in range(NT) for kv in range(NKV)]):
                L = (qb + 1) * P
                s, mx, su, inv = soft[g % 2][:, :, 0:L], mx4[g % 2], sum4[g % 2], inv4[g % 2]
                mask = C("causal") if qb == 0 else work[:, w_at[qb]:w_at[qb] + L]
                if g >= 2:
                    banks.wait_full(dve, ("probsT", g - 2, (g - 2) // NKV))
                banks.wait_full(dve, ("att_s", g))
                if g == 0:
                    for t in range(NT):
                        banks.wait_drained(dve, ("qT", t))
                    banks.wait_full(dve, "qkT_s")
                banks.drained(dve.scalar_tensor_tensor(s, psum[:, 0:4, 0:L], HD ** -0.5, spread_dim(mask, 1, 4),
                                                       ALU.mult, ALU.add), ("att_s", g))
                banks.wait_drained(dve, ("att_s", g))
                lane.then(dve.tensor_reduce(mx, s, AX_X, ALU.max))
                dve.tensor_scalar(mx, mx, -1.0, None, ALU.mult).then_inc(max_ready, 1)
                sample_rounds(ROUNDS[3])
                dve.wait_ge(exp_ready, g + 1)
                lane.then(dve.reciprocal(inv, su))
                dve.tensor_tensor(s, s, spread_dim(inv, 2, L), ALU.mult).then_inc(probs_ready, 1)
            for f in range(KD):
                sample_rounds(ROUNDS[4])
                banks.wait_full(dve, ("WG", f))
                if f == 0:
                    for n in range(16):
                        banks.wait_drained(dve, (f"G{n // 4}", n % 4))
                g = KD + f
                banks.drained(dve.tensor_tensor(halves(gates[:, g, :]), halves(gates[:, g, :]), pair(2 + 4 * (f % 2)),
                                                ALU.mult), ("WG", f))
            sample_rounds(TOPK_S // 8)
            back = slice(None, None, -1)
            lane.mark(dve.tensor_copy(second_values[0:NS], top_values[32:32 + NS, back]))
            lane.then(dve.tensor_copy(half_idx[0:32 + NS], idx_u[0:32 + NS]))
            lane.mark(dve.tensor_tensor(second_values[0:NS], top_values[0:NS], second_values[0:NS], ALU.is_ge))
            lane.then(dve.tensor_scalar(second_idx[0:NS], half_idx[32:32 + NS, back], float(PAST // 2), None, ALU.add))
            lane.then(dve.tensor_tensor(half_idx[0:NS], half_idx[0:NS], second_idx[0:NS], ALU.subtract))
            lane.then(dve.tensor_tensor(half_idx[0:NS], half_idx[0:NS], second_values[0:NS], ALU.mult))

            lane.then(dve.tensor_tensor(idx_f[0:NS], half_idx[0:NS], second_idx[0:NS], ALU.add))
            dve.tensor_scalar(key_bias[0:NS, 0:TOPK_S], idx_f[0:NS], float(PAST), -BIG, ALU.is_equal, ALU.mult)\
               .then_inc(idx_ready, 1)
            lane.then(dve.tensor_reduce(idx_max[0:NS], idx_f[0:NS], AX_X, ALU.max))
            dve.tensor_scalar(key_bias[0:NS, TOPK_S:TOPK_S + 1], idx_max[0:NS], float(PAST), -BIG, ALU.is_lt, ALU.mult)\
               .then_inc(key_bias_ready, 1)
            dve.wait_ge(pages_all_in, 16)
            lane.then(dve.tensor_copy(pages_f, pages_i))
            banks.wait_full(dve, "idxT")
            banks.drained(dve.tensor_copy(slot_i, psum[:, 4, 0:2 * NS]), "idxT")
            banks.wait_drained(dve, "idxT")
            lane.mark(dve.tensor_scalar(off_i, slot_i, PAGE - 1, None, ALU.bitwise_and))
            lane.then(dve.tensor_scalar(slot_i, slot_i, 7, None, ALU.logical_shift_right))
            lane.mark(dve.tensor_copy(page_f, slot_i))
            lane.then(dve.tensor_copy(off_f, off_i))
            lane.then(dve.tensor_tensor(page_hot, spread_dim(C("iota")[:, 0:N_PAGES], 1, 2 * NS),
                                        spread_dim(page_f, 2, N_PAGES), ALU.is_equal))
            hot = page_hot.rearrange("p (h b) n -> p h (b n)", h=2)
            lane.then(dve.tensor_tensor(hot, hot, spread_dim(pages_f, 1, 2), ALU.mult))
            lane.then(dve.tensor_reduce(slot_f, page_hot, AX_X, ALU.add))
            dve.scalar_tensor_tensor(sel_rows, slot_f, float(PAGE), off_f, ALU.mult, ALU.add).then_inc(sel_rows_ready, 1)
            lane.then(dve.memset(q_lhs, 0.0))
            banks.wait_drained(dve, "qkT_s")
            for v in range(NKV):
                o = HD * v
                dve.tensor_copy(q_lhs[o:o + HD, :, 4 * v:4 * v + 4], qT[o:o + HD, :, SEQ:TOK].rearrange("p j b -> p b j"))\
                   .then_inc(q_lhs_ready, 1)
            def attention_gated(part, f):
                banks.wait_full(dve, ("WA", part, f))
                cols = gates[:, f, part * HALF:(part + 1) * HALF]
                banks.drained(dve.tensor_tensor(cols, cols, psum[:, 4 * part + f % 2, 0:HALF], ALU.mult), ("WA", part, f))

            for f in range(KD):
                attention_gated(0, f)
            for g in range(2):
                banks.wait_full(dve, ("att_ss", g))
            lane.then(dve.tensor_reduce(mx2, psum[:, 0:2, 0:TOPK_S + 1], AX_X, ALU.max))
            dve.tensor_scalar(mx2, mx2, -HD ** -0.5, None, ALU.mult).then_inc(max_s_ready, 1)
            for g in range(2):
                banks.wait_drained(dve, ("att_ss", g))
            lane.then(dve.reciprocal(inv2, sum2))
            lane.then(dve.tensor_tensor(soft_s, soft_s, spread_dim(inv2, 2, TOPK_S + 1), ALU.mult))
            lane.mark(dve.tensor_scalar(new_probs[:, 0, :], C("head"), soft_s[:, 0, TOPK_S:TOPK_S + 1], None, ALU.mult))
            dve.tensor_scalar(new_probs[:, 1, :], C("head"), soft_s[:, 1, TOPK_S:TOPK_S + 1], None, ALU.mult)\
               .then_inc(probs_s_ready, 1)
            banks.wait_full(dve, "new_probs")
            banks.drained(dve.tensor_copy(sstat[0:NS, 52:60], psum[0:NS, 3, 0:NH]), "new_probs")
            banks.wait_drained(dve, "new_probs")
            dve.tensor_tensor(new_spread[0:NS].rearrange("p (b h) -> p b h", b=NS),
                              C("own")[0:NS].rearrange("p (b h) -> p b h", b=NS),
                              spread_dim(sstat[0:NS, 52:60], 1, NS), ALU.mult).then_inc(new_spread_ready, 1)

            for f in range(KD):
                attention_gated(1, f)
                banks.wait_drained(dve, ("WG", f))
                banks.wait_drained(dve, ("WA", 0, f))
                banks.wait_drained(dve, ("WA", 1, f))
                lane.mark(dve.tensor_tensor(hT[:, f, :], gates[:, f, :], gates[:, KD + f, :], ALU.add))
                lane.wait()
                dve.tensor_copy(hTs[:, f, 0:NS], hT[:, f, SEQ:TOK]).then_inc(merged, 1)
            dve.wait_ge(late_in, 16)
            for c in (8, 9):
                half = slice(512 * (c % 2), 512 * (c % 2) + 512)
                for g, name, b, rows in ((0, "adaP", 2 + c % 2, P), (1, "adaS", 4 + c % 2, NS)):
                    banks.wait_full(dve, (name, c))
                    banks.drained(dve.scalar_tensor_tensor(mod2["scale2"][0:rows, g, half], psum[0:rows, b, :], 1.0,
                                                           gain2[0:rows, half], ALU.add, ALU.mult), (name, c))
            for c in (4, 5):
                banks.wait_drained(dve, ("adaP", c))
                banks.wait_drained(dve, ("adaS", c))
            dve.wait_ge(x2_in, 16 * T5)
            for c in range(2):
                half = slice(512 * c, 512 * c + 512)
                for i, (part, rows, t) in enumerate(ORDER):
                    b = 3 if part == "S" else t % 2
                    banks.wait_full(dve, (f"O{c}", part))
                    tmp = w_tmp[0:rows, i % 2, :]
                    g = 1 if part == "S" else 0
                    if c + i:
                        dve.wait_ge(x2_half if c == 0 or i == 0 else x2_ready, 5 if c and i == 0 else i)
                    banks.drained(dve.tensor_tensor(tmp, psum[0:rows, b, :], mod2["gate1"][0:rows, g, half], ALU.mult),
                                  (f"O{c}", part))
                    banks.wait_drained(dve, (f"O{c}", part))
                    dve.tensor_tensor(x2[0:rows, t, half], x2[0:rows, t, half], tmp, ALU.add)\
                       .then_inc(x2_ready if c else x2_half, 1)
            dve.wait_ge(ssq2_ready, 1)
            rsqrt_of(ssq, ssq, D)
            for c in (6, 7, 8, 9):
                banks.wait_drained(dve, ("adaP", c))
                banks.wait_drained(dve, ("adaS", c))
            for _, rows, t in ORDER:
                g = 0 if t < NT else 1
                out = t2[0:rows, t, :]
                lane.then(dve.scalar_tensor_tensor(out, x2[0:rows, t, :], rstd[0:rows, t:t + 1],
                                                   mod2["scale2"][0:rows, g, :], ALU.mult, ALU.mult))
                dve.tensor_tensor(out, out, mod2["shift2"][0:rows, g, :], ALU.add).then_inc(t2_ready, 1)

            lane.then(dve.memset(logits, 0.0))
            banks.wait_full(dve, "logits_rows")
            n36 = NEG + NE
            lane.mark(dve.tensor_tensor(logits[:, 0:NT, :], psum[:, 2, 0:NT * n36].rearrange("p (t n) -> p t n", t=NT),
                                        spread_dim(b_router, 1, NT), ALU.add))
            banks.drained(dve.tensor_tensor(logits[0:NS, NT, :], psum[0:NS, 2, NT * n36:T5 * n36], b_router[0:NS], ALU.add),
                          "logits_rows")
            banks.wait_drained(dve, "logits_rows")

            def first_best(hot, values, best, rev, tmp, width):
                lane.then(dve.tensor_reduce(best, values, AX_X, ALU.max))
                lane.then(dve.tensor_tensor(tmp, values, spread_dim(best, 2, width), ALU.is_equal))
                lane.then(dve.tensor_tensor(tmp, tmp, spread_dim(C(rev), 1, T5), ALU.mult))
                lane.then(dve.tensor_reduce(w_max, tmp, AX_X, ALU.max))
                lane.then(dve.tensor_tensor(hot, tmp, spread_dim(w_max, 2, width), ALU.is_equal))

            g_logits = logits[:, :, 0:NEG]
            first_best(g_exp, g_logits, g_max, "rev4", g_tmp, NEG)
            lane.then(dve.tensor_scalar(g_exp, g_exp, -1.0, BIG, ALU.add, ALU.mult))
            lane.mark(dve.tensor_tensor(e_logits.rearrange("p t (g e) -> p t g e", g=NEG),
                                        logits[:, :, NEG:n36].rearrange("p t (g e) -> p t g e", g=NEG),
                                        spread_dim(g_exp, 3, EPG), ALU.add))
            lane.wait()
            dve.tensor_tensor(g_tmp, g_logits, spread_dim(g_max, 2, NEG), ALU.subtract).then_inc(g_diff_ready, 1)
            first_best(hot1, e_logits, e_max1, "rev32", e_tmp, NE)
            lane.then(dve.scalar_tensor_tensor(e_logits, hot1, -BIG, e_logits, ALU.mult, ALU.add))
            first_best(hot2, e_logits, e_max2, "rev32", e_tmp, NE)
            dve.tensor_tensor(e_ratio, e_max2, e_max1, ALU.subtract).then_inc(e_diff_ready, 1)
            lane.then(dve.tensor_tensor(chosen, hot1, hot2, ALU.add))
            lane.mark(dve.tensor_tensor(chosen, chosen, spread_dim(C("valid"), 2, NE), ALU.mult))
            lane.then(dve.memset(before_sum[:, 0, :], 0.0))
            for t in range(T5):
                ins = dve.tensor_tensor(before_sum[:, t + 1, :], before_sum[:, t, :], chosen[:, t, :], ALU.add)
                lane.then(ins) if t < NT else ins.then_inc(chosen_ready, 1)
            dve.wait_ge(g_exp_ready, 1)
            lane.then(dve.tensor_reduce(g_sum, g_exp, AX_X, ALU.add))
            dve.wait_ge(e_exp_ready, 1)
            lane.then(dve.tensor_scalar(p_first, e_ratio, 1.0, None, ALU.add))
            lane.then(dve.tensor_tensor(p_first, p_first, g_sum, ALU.mult))
            lane.then(dve.reciprocal(gate_of[:, 0, :], p_first))
            lane.mark(dve.tensor_tensor(gate_of[:, 1, :], gate_of[:, 0, :], e_ratio, ALU.mult))
            lane.mark(dve.tensor_copy(token_of, spread_dim(C("tok"), 1, 2)))

            banks.wait_full(dve, "places")
            lane.mark(dve.tensor_copy(place, psum[:, 3, 0:T5 * NE].rearrange("p (t n) -> p t n", t=T5)))
            banks.drained(dve.tensor_copy(counts, psum[:, 3, T5 * NE:(T5 + 1) * NE]), "places")
            banks.wait_drained(dve, "places")
            lane.then(dve.tensor_tensor(over_cmp, spread_dim(counts, 2, 8), spread_dim(C("over"), 1, NE), ALU.is_gt))
            lane.then(dve.tensor_reduce(n_over, over_cmp, AX_X, ALU.add))
            lane.then(dve.tensor_tensor_scan(over_end, C("ones")[:, 0:NE], n_over, 0.0, ALU.mult, ALU.add))
            lane.then(dve.tensor_tensor(over_shift, over_end, n_over, ALU.subtract))
            lane.then(dve.tensor_scalar(over_shift, over_shift, float(SB), float(SB * (NE - 1)), ALU.mult, ALU.add))
            lane.then(dve.tensor_tensor(over_shift, over_shift, C("first_slot"), ALU.subtract))
            lane.then(dve.tensor_scalar(e_tmp, place, float(SB), None, ALU.is_ge))
            lane.then(dve.tensor_tensor(e_tmp, e_tmp, spread_dim(over_shift, 1, T5), ALU.mult))
            lane.then(dve.tensor_tensor(place, place, e_tmp, ALU.add))
            lane.then(dve.tensor_tensor(place, place, spread_dim(C("first_slot"), 1, T5), ALU.add))
            for c, hot in enumerate((hot1, hot2)):
                lane.then(dve.tensor_tensor(e_tmp, hot, place, ALU.mult))
                lane.then(dve.tensor_reduce(rank[:, c, :], e_tmp, AX_X, ALU.add))
            flat = lambda a: a.rearrange("p c t -> p (c t)")
            lane.then(dve.tensor_copy(rank_i, flat(rank)))
            lane.mark(dve.tensor_scalar(slot_of_i, rank_i, SB - 1, None, ALU.bitwise_and))
            lane.then(dve.tensor_scalar(item_of_i, rank_i, 6, None, ALU.logical_shift_right))
            lane.mark(dve.tensor_copy(slot_of, slot_of_i))
            lane.then(dve.tensor_copy(item_of, item_of_i))
            item2 = item_of.rearrange("p (c t) -> p c t", c=2)
            valid2 = spread_dim(C("valid"), 1, 2)
            lane.then(dve.tensor_scalar(item_of, item_of, 1.0, None, ALU.add))
            lane.then(dve.tensor_tensor(item2, item2, valid2, ALU.mult))
            lane.then(dve.tensor_scalar(item_of, item_of, -1.0, None, ALU.add))
            for half in range(2):
                lane.mark(dve.tensor_tensor(slot_hot[:, :, SB * half:SB * half + SB],
                                            spread_dim(C("iota")[:, 0:SB], 1, 2 * T5), spread_dim(slot_of, 2, SB),
                                            ALU.is_equal))
            gate_cols = item_hot[:, :, N_ITEMS:2 * N_ITEMS]
            token_cols = item_hot[:, :, 0:N_ITEMS]
            lane.then(dve.tensor_tensor(gate_cols, spread_dim(C("iota")[:, 0:N_ITEMS], 1, 2 * T5),
                                        spread_dim(item_of, 2, N_ITEMS), ALU.is_equal))
            lane.then(dve.tensor_tensor(token_cols, gate_cols, spread_dim(flat(token_of), 2, N_ITEMS), ALU.mult))
            dve.tensor_tensor(gate_cols, gate_cols, spread_dim(flat(gate_of), 2, N_ITEMS), ALU.mult)\
               .then_inc(tables_hot_ready, 1)
            lane.then(dve.tensor_tensor(over_hot[0:1], spread_dim(over_end[0:1], 1, N_OVER),
                                        spread_dim(C("iota")[0:1, 0:N_OVER], 2, NE), ALU.is_le))
            lane.then(dve.tensor_reduce(over_expert_f[0:1], over_hot[0:1], AX_X, ALU.add))
            lane.mark(dve.memset(over_expert[0:1], 0))
            lane.mark(dve.memset(token_tab[:, N_ITEMS:], 0))
            lane.then(dve.tensor_scalar(item_counts[0:1, 0:1], over_end[0:1, NE - 1:NE], float(NE), None, ALU.add))
            lane.mark(dve.tensor_scalar(over_expert[0:1, 0:N_OVER], over_expert_f[0:1], float(NE - 1), None, ALU.min))
            lane.then(dve.tensor_scalar(item_counts[0:1, 1:2], over_end[0:1, NE - 1:NE], float(NE + 1), None, ALU.add))
            lane.mark(dve.tensor_scalar(item_counts[0:1, 1:2], item_counts[0:1, 1:2], 1, 5, ALU.logical_shift_right,
                                        ALU.logical_shift_left))
            lane.mark(dve.tensor_scalar(item_counts[0:1, 2:3], item_counts[0:1, 0:1], 1, 5, ALU.logical_shift_right,
                                        ALU.logical_shift_left))
            banks.wait_full(dve, "tables")
            banks.drained(dve.tensor_copy(gate_tab, psum[:, 4, N_ITEMS:2 * N_ITEMS]), "tables")
            dve.tensor_copy(token_tab[:, 0:N_ITEMS], psum[:, 4, 0:N_ITEMS]).then_inc(tables_ready, 1)

            def hidden_of(p, done):
                dve.tensor_tensor(hidden[0:SB, p, :], silu_g[0:SB, p, :], psum[0:SB, 2 + p, 0:DE], ALU.mult).then_inc(done, 1)

            def hidden_out(p, done):
                dve.tensor_copy(hidden_T[:, p], psum[:, 4 + p, 0:2 * SB].rearrange("p (f n) -> p f n", f=2)).then_inc(done, 1)

            def y_scaled(p, gate, done):
                dve.tensor_scalar(y_rows[:, p, :], psum[:, 6 + p, :], gate, None, ALU.mult).then_inc(done, 1)

            def dve_item(i, k, first):
                e, p = i * 4 + k, k % 2
                dve.wait_ge(silu_done, e + 1)
                if not (first and k < 2):
                    dve.wait_ge(hT_full, e - 1)
                hidden_of(p, hidden_done)
                dve.wait_ge(hT_full, e + 1)
                if not (first and k < 2):
                    dve.wait_ge(y_full, e - 1)
                hidden_out(p, hT_out)
                dve.wait_ge(y_full, e + 1)
                if not (first and k < 2):
                    dve.wait_ge(y_stored[p], i * 64 + 32 * (k // 2))
                gate = gate_tab[:, e:e + 1] if first else gate_tab[:, bass.ds(e, 1)]
                y_scaled(p, gate, y_out)

            dve.wait_ge(tables_ready, 1)
            each_item(dve, dve_item)

            for c in (10, 11):
                banks.wait_drained(dve, ("adaP", c))
                banks.wait_drained(dve, ("adaS", c))
            for t in range(T5):
                rows, g = (P, 0) if t < NT else (NS, 1)
                dve.wait_ge(picked_in[t], 32)
                a, b = picked[0:rows, t, 0, :], picked[0:rows, t, 1, :]
                lane.then(dve.tensor_tensor(a, a, b, ALU.add))
                lane.then(dve.tensor_tensor(a, a, mod2["gate2"][0:rows, g, :], ALU.mult))
                dve.tensor_tensor(x2[0:rows, t, :], x2[0:rows, t, :], a, ALU.add).then_inc(y_ready, 1)


def _tiles(w, width):
    k = w.shape[0] // P
    return w.reshape(k, P, width).transpose(1, 0, 2).reshape(P, k * width)


def _stream(inputs):
    w_in, w_ada = inputs["w_in"][0], inputs["w_ada"][0]
    o = np.cumsum([0, NH * HD, NKV * HD, NKV * HD, IH * ID, ID, IH, GM, GM, 2 * D])
    q, k, v, qi, ki, wi, u, vg, gates = (w_in[:, o[i]:o[i + 1]] for i in range(9))
    q = q.reshape(D, NH, HD)[:, HEAD_ORDER].reshape(D, NH * HD)
    wa = inputs["w_proj_attn"][0].reshape(NH, HD, D)[HEAD_ORDER].reshape(NH * HD, D)
    parts = {f"ada{c}": w_ada[:, 512 * c:512 * c + 512] for c in range(12)}
    parts |= {"A": np.concatenate([qi, ki, wi, v], 1), "B": q, "C": np.concatenate([k, vg[:, :VG0]], 1),
              "D": vg[:, VG0:], "U": u}
    parts |= {f"G{c}": np.concatenate([gates[:, 256 * c:256 * c + 256], gates[:, D + 256 * c:D + 256 * c + 256]], 1)
              for c in range(4)}
    parts |= {"WA": wa, "WG": inputs["w_proj_gmlp"][0]}
    parts |= {f"O{c}": inputs["w_out"][0][:, 512 * c:512 * c + 512] for c in range(2)}
    out = np.zeros((len(STREAM), P, KD * 512), np.float32)
    for n, (name, size) in enumerate(STREAM):
        w = parts[name]
        out[n, :, :size] = _tiles(w, w.shape[1])
    return out


def _layout(inputs):
    x = {k: np.asarray(v) for k, v in inputs.items()}
    c = np.concatenate([x["c_sample"], x["c_prompt"]], 0)
    c_T = np.zeros((P, KD, 32), np.float32)
    c_T[:, :, :NS + 1] = c.reshape(NS + 1, KD, P).transpose(2, 1, 0)
    a = {
        "consts": np.concatenate(list(CONSTS.values()), 1),
        "stream": _stream(x),
        "c_T": c_T.reshape(P, -1),
        "b_ada": x["b_ada"].reshape(12, 512),
        "norm_mix_g": x["norm_mix_g"][0],
        "norm_ffn_g": x["norm_ffn_g"][0],
        "head_gains": np.concatenate([x["q_norm_g"][0], x["k_norm_g"][0], x["kidx_norm_g"][0]]),
        "ln": np.concatenate([x["gm_ln_g"], x["gm_ln_b"]], 0),
        "x_prompt": x["x_prompt"][0],
        "x_sample": x["x_sample"][:, 0],
        "page_rep": np.repeat(x["page_table"].T, 8, axis=0),
        "pages": x["page_table"].reshape(-1),
        "cache_ki": x["cache_kidx"].reshape(POOL_PAGES * 8, 16 * ID),
        "cache_k": x["cache_k"].reshape(POOL_PAGES * PAGE, NKV * HD),
        "cache_v": x["cache_v"].reshape(POOL_PAGES * PAGE, NKV * HD),
        "ws_T": x["gm_spatial_w"][0].transpose(2, 0, 1).reshape(P, GG * CHUNK),
        "ws_00": x["gm_spatial_w"][0][:, 0, 0].reshape(4, 2).T,
        "gm_b": x["gm_spatial_b"][0],
        "w_router": _tiles(np.concatenate([x["w_router_group"][0], x["w_router_expert"][0]], 1), NEG + NE),
        "b_router": np.concatenate([x["b_router_group"][0], x["b_router_expert"][0]]),
        "experts": np.concatenate([
            np.concatenate([x["w_expert_gate"][0], x["w_expert_up"][0]], 2)
            .reshape(NE, KD, P, 2 * DE).transpose(0, 2, 1, 3).reshape(NE, P, KD * 2 * DE),
            x["w_expert_down"][0].reshape(NE, 2, P, D).transpose(0, 2, 1, 3).reshape(NE, P, 2 * D)], 2),
    }
    return {k: np.ascontiguousarray(v) for k, v in a.items()}


OUTS = {
    "y_p": (SEQ, D), "y_s": (NS, D),
    "new_k_p": (SEQ, NKV * HD), "new_v_p": (SEQ, NKV * HD), "new_ki_p": (SEQ, ID),
    "new_k_s": (NS, NKV * HD), "new_v_s": (NS, NKV * HD), "new_ki_s": (NS, ID), "new_vg_s": (NS, GM),
}
SCRATCH = {"t2_rows": (TOK, D), "expert_rows": (N_ITEMS * SB, D)}


def kernel(**inputs):
    import concourse.bacc as bacc
    from concourse.bass_utils import run_bass_kernel_spmd

    arrays = _layout(inputs)
    nc = bacc.Bacc("TRN2", target_bir_lowering=False, num_devices=1)
    io = {k: nc.dram_tensor(f"in_{k}", a.shape, mybir.dt.from_np(a.dtype), kind="ExternalInput").ap()
          for k, a in arrays.items()}
    io |= {k: nc.dram_tensor(f"out_{k}", s, F32, kind="ExternalOutput").ap() for k, s in OUTS.items()}
    io |= {k: nc.dram_tensor(k, s, F32, kind="Internal").ap() for k, s in SCRATCH.items()}
    decoder_step(nc, io)
    run = run_bass_kernel_spmd(nc, [{f"in_{k}": a for k, a in arrays.items()}], core_ids=[0])
    got = {k: run.results[0][f"out_{k}"] for k in OUTS}
    return (
        got["y_p"].reshape(1, SEQ, D), got["y_s"].reshape(NS, 1, D),
        got["new_k_p"].reshape(1, 1, SEQ, NKV, HD), got["new_v_p"].reshape(1, 1, SEQ, NKV, HD),
        got["new_ki_p"].reshape(1, 1, SEQ, ID),
        got["new_k_s"].reshape(1, NS, 1, NKV, HD), got["new_v_s"].reshape(1, NS, 1, NKV, HD),
        got["new_ki_s"].reshape(1, NS, 1, ID), got["new_vg_s"].reshape(1, NS, 1, GM),
    )
```

```python
from contextlib import ExitStack

import numpy as np

import concourse.bass as bass
from concourse import mybir

F32 = mybir.dt.float32
I32 = mybir.dt.int32
U32 = mybir.dt.uint32
ALU = mybir.AluOpType
ACT = mybir.ActivationFunctionType
AX_X = mybir.AxisListType.X

P = 128
D = 1024
KD = D // P
SEQ = 512
NT = SEQ // P
NS = 8
TOK = SEQ + NS
HALF = TOK // 2
PAST = 2048
PAGE = 128
N_PAGES = PAST // PAGE
POOL_PAGES = 160
NH, HD, NKV = 8, 64, 2
ROT = HD // 4
THETA = 500000.0
IH, ID = 4, 64
TOPK_P = min(256, SEQ // 4)
TOPK_S = min(256, (PAST + 1) // 4)
GM, GG, GD = 512, 8, 64
CHUNK = 128
NEG, EPG = 4, 8
NE = NEG * EPG
DE = D // 4
EPS = 1e-6
BIG = 1e30
TAKEN = -3e38

QI, KI, WI, VV = 0, 256, 320, 324
NA = VV + NKV * HD
NB = NH * HD
VG0 = 192
NC = NKV * HD + VG0
ND = GM - VG0
HEAD_ORDER = [h for j in range(4) for h in (j, j + 4)]

STREAM = ([(f"ada{c}", KD * 512) for c in range(4)] + [("A", KD * NA), ("B", KD * NB), ("C", KD * NC), ("D", KD * ND)]
          + [("U", KD * 512)]
          + [(name, KD * 512) for c in range(4) for name in (f"G{c}", f"ada{4 + 2 * c}", f"ada{5 + 2 * c}")]
          + [("WG", 4 * D), ("WA", 4 * D), ("O0", KD * 512), ("O1", KD * 512)])
SLOT_OF = {name: n for n, (name, _) in enumerate(STREAM)}
RING = 3

ROUNDS = (1, 1, 2, 2, 2, 2, 2, 3, 3, 3, 3)
assert sum(ROUNDS) + 8 == TOPK_S // 8

SB = 64
ASSIGNED = 2 * TOK
N_OVER = ASSIGNED // (SB + 1)
N_ITEMS = NE + N_OVER
BUFFERS = 6
LATE = NE // BUFFERS
assert N_ITEMS % BUFFERS == 0 and BUFFERS % 2 == 0

O_GATES, O_QT, O_ATT, O_U, O_KT, O_QIT, O_KIT = 0, 8320, 10400, 12480, 14560, 15080, 16120
O_VG, O_QR, O_KR, O_AR, O_WS, O_BT, O_S, O_PT, O_WORK, O_SC = (
    16640, 19200, 21760, 22400, 24660, 25684, 26196, 28244, 29268, 30420)
ARENA = 33024


def constant_fields():
    eye = np.eye(P, dtype=np.float32)
    row = np.arange(P)
    f = {}
    f["ident"] = eye
    sel_p = np.zeros((P, P)); sel_p[8::32, :] = 1.0
    f["sel_p"] = sel_p
    sel_s = np.zeros((P, NS))
    for i in range(NS):
        sel_s[i::32, i] = 1.0
    f["sel_s"] = sel_s
    f["before"] = (row[:, None] < row[None, :]).astype(np.float32)
    f["ones"] = np.ones((P, P))
    f["causal"] = np.where(row[None, :] <= row[:, None], 0.0, -BIG)
    pos = np.zeros((P, NT + 1), np.float32)
    for t in range(NT):
        pos[:, t] = t * P + row
    pos[:, NT] = PAST
    half = ROT // 2
    inv = np.float32(THETA) ** (-np.arange(half, dtype=np.float32) / np.float32(half))
    ang = (pos[:, :, None] * inv[None, None, :].astype(np.float32)).astype(np.float32)
    cos, sin = np.cos(ang), np.sin(ang)
    f["cos"] = np.concatenate([cos, cos], -1).reshape(P, -1)
    f["sin"] = np.concatenate([-sin, sin], -1).reshape(P, -1)
    f["iota"] = np.tile(np.arange(P, dtype=np.float32), (P, 1))
    tok = np.zeros((P, NT + 1)); valid = np.zeros((P, NT + 1))
    for t in range(NT):
        tok[:, t] = t * P + row; valid[:, t] = 1.0
    tok[:NS, NT] = SEQ + row[:NS]; valid[:NS, NT] = 1.0
    f["tok"] = tok
    f["valid"] = valid
    f["page_seg"] = (row % 8)[:, None]
    place = np.zeros((P, 2, 2, 4, 8, 4))
    for b in range(NS):
        for par in range(2):
            place[b, b // 4, par, b % 4, par, :] = 1.0
    f["place"] = place.reshape(P, -1)
    spread = np.zeros((P, 2, P)); gather = np.zeros((P, 2, NS))
    for b in range(NS):
        spread[b, b // 4, 32 * (b % 4):32 * (b % 4) + NH] = 1.0
        gather[32 * (b % 4):32 * (b % 4) + NH, b // 4, b] = 1.0
    f["spread"] = spread.reshape(P, -1)
    f["gather"] = gather.reshape(P, -1)
    f["head"] = (row[:, None] % 32 == np.arange(NH)[None, :])
    f["own"] = np.concatenate([np.repeat(np.eye(NS), NH, axis=1), np.zeros((P - NS, NS * NH))])
    f["rev4"] = np.tile(4.0 - np.arange(4), (P, 1))
    f["rev32"] = np.tile(32.0 - np.arange(32), (P, 1))
    f["first_slot"] = np.tile(SB * np.arange(NE), (P, 1))
    f["over"] = np.tile(SB * np.arange(1, 9), (P, 1))
    return {k: np.ascontiguousarray(v, dtype=np.float32) for k, v in f.items()}


CONSTS = constant_fields()
CONST_AT = {}
_n = 0
for _k, _v in CONSTS.items():
    CONST_AT[_k] = (_n, _v.shape[1])
    _n += _v.shape[1]
N_CONST = _n


class Lane:

    def __init__(self, engine, semaphore):
        self.engine, self.semaphore, self.count = engine, semaphore, 0

    def mark(self, instruction):
        instruction.then_inc(self.semaphore, 1)
        self.count += 1

    def wait(self):
        if self.count:
            self.engine.wait_ge(self.semaphore, self.count)

    def then(self, instruction):
        self.mark(instruction)
        self.wait()


class Banks:

    def __init__(self, full, free):
        self.full, self.free = full, free
        self.count = [0] * 8
        self.last = [None] * 8
        self.at = {}

    def begin(self, pe, name, *banks):
        before = {self.at[self.last[b]] for b in banks if self.last[b] is not None}
        lead = banks[0]
        self.at[name] = (lead, self.count[lead])
        self.count[lead] += 1
        for b in banks:
            self.last[b] = name
        for b, n in sorted(before):
            pe.wait_ge(self.free[b], n + 1)

    def filled(self, instruction, name):
        instruction.then_inc(self.full[self.at[name][0]], 1)

    def wait_full(self, engine, name):
        b, n = self.at[name]
        engine.wait_ge(self.full[b], n + 1)

    def drained(self, instruction, name):
        instruction.then_inc(self.free[self.at[name][0]], 1)

    def wait_drained(self, engine, name):
        b, n = self.at[name]
        engine.wait_ge(self.free[b], n + 1)


def spread_dim(ap, axis, n):
    wide = ap.unsqueeze(axis)
    shape = list(wide.shape)
    shape[axis] = n
    return wide.broadcast_to(shape)


def decoder_step(nc, io):
    ctx = ExitStack()
    with ctx:
        def sb(name, shape, dt=F32):
            return ctx.enter_context(nc.sbuf_tensor(name, shape, dt))

        def sem(name):
            return ctx.enter_context(nc.semaphore(name))

        ring = sb("ring", [P, RING, KD * 512])
        hT = sb("hT", [P, KD, TOK])
        hTs = sb("hTs", [P, KD, 32])
        c_T = sb("c_T", [P, KD, 32])
        bn = sb("bn", [P, NT + 1, 6])
        zeros = sb("zeros", [P, 256])
        arena = sb("arena", [P, ARENA])
        const = sb("const", [P, N_CONST])
        gains = sb("gains", [P, 3 * HD])
        stat = sb("stat", [P, 256])
        psum = ctx.enter_context(nc.psum_tensor("psum", [P, 8, 512], F32))

        def at(offset, size):
            return arena[:, offset:offset + size]

        def C(name):
            o, n = CONST_AT[name]
            return const[:, o:o + n]

        ident = C("ident")
        early = O_GATES
        mod1 = at(early, 4096).rearrange("p (g m n) -> p g m n", g=2, m=2)
        ln = at(early + 4096, 2 * GM).rearrange("p (m n) -> p m n", m=2)
        xbuf = at(early + 5120, (NT + 1) * D).rearrange("p (t n) -> p t n", n=D)
        relu_p = at(early, 4 * 512).rearrange("p (h n) -> p h n", h=4)
        ki_pages = at(early + 2048, 2 * D).rearrange("p (b n) -> p b n", b=2)
        ki_T = at(early + 5120, 2 * D).rearrange("p (b n) -> p b n", b=2)
        relu_s = at(early + 5120 + 2 * D, 2 * D).rearrange("p (b n) -> p b n", b=2)
        gain1 = at(O_QR, D)
        junk = at(O_QR + D, D)
        G = at(O_PT, 2 * 512).rearrange("p (b n) -> p b n", b=2)
        late_G = [at(o, 512) for o in (O_QIT, O_QIT + 512, O_QIT + 1024, O_WS + 512, O_WS + 1024, O_VG + NT * GM,
                                       O_WS, O_QR + NT * NB)]
        ada_bias = at(O_SC + 1540, 512)
        gates = at(O_GATES, 16 * TOK).rearrange("p (f n) -> p f n", f=16)
        qT = at(O_QT, 4 * TOK).rearrange("p (j n) -> p j n", j=4)
        attT = at(O_ATT, 4 * TOK).rearrange("p (j n) -> p j n", j=4)
        uT = at(O_U, 4 * TOK).rearrange("p (j n) -> p j n", j=4)
        kT = at(O_KT, TOK)
        qiT = at(O_QIT, 2 * TOK).rearrange("p (j n) -> p j n", j=2)
        kiT = at(O_KIT, TOK)
        vg = at(O_VG, (NT + 1) * GM).rearrange("p (t n) -> p t n", n=GM)
        qraw = at(O_QR, (NT + 1) * NB).rearrange("p (t n) -> p t n", n=NB)
        kraw = at(O_KR, (NT + 1) * NKV * HD).rearrange("p (t n) -> p t n", n=NKV * HD)
        araw = at(O_AR, (NT + 1) * NA).rearrange("p (t n) -> p t n", n=NA)
        wsT = at(O_WS, GG * CHUNK).rearrange("p (g n) -> p g n", g=GG)
        bT = at(O_BT, 4 * CHUNK).rearrange("p (j n) -> p j n", j=4)
        ki_twice = at(O_S, (NT + 1) * P).rearrange("p (t n) -> p t n", n=P)
        qi_twice = at(O_S + 640, IH * P).rearrange("p (h c d) -> p h c d", h=IH, c=2)
        qi_lhs = at(O_S + 1152, NS * 32).rearrange("p (b m) -> p b m", b=NS)
        wi_lhs = at(O_S + 1408, 4 * NS).rearrange("p (c b) -> p c b", c=4)
        wi_place = at(O_S + 1440, 512)
        work = at(O_WORK, 1152)
        norm_tmp = at(O_S, 2560)
        scores = at(O_SC, PAST // 2 + 1)
        top_values = at(O_SC + 1028, TOPK_S)
        idx = at(O_SC + 1284, TOPK_S)
        second_values = at(O_WORK, TOPK_S)
        half_idx = at(O_WORK + 256, TOPK_S)
        second_idx = at(O_WORK + 512, TOPK_S)
        page_rows = stat[:, 0:NS].bitcast(I32)
        page_rep = stat[:, NS:2 * NS].bitcast(I32)
        ssq = stat[:, 16:21]
        rstd = stat[:, 24:29]
        ki_ms = stat[:, 32:37]
        ki_r = stat[:, 40:45]
        k_ms = stat[:, 48:58]
        k_r = stat[:, 60:70]
        q_ms = stat[:, 72:112]
        q_r = stat[:, 112:152]
        new_dots = stat[:, 152:156]
        top8 = stat[:, 160:192]
        mu_var = stat[:, 192:202].rearrange("p (t m) -> p t m", m=2)
        vg_r = stat[:, 204:209]
        minus_half = stat[:, 212:252]

        norm_tmp2 = at(O_S, 2048).rearrange("p (h n) -> p h n", h=4)
        soft = [norm_tmp2, at(O_QR, 2048).rearrange("p (h n) -> p h n", h=4)]
        probsT = at(O_VG, 4 * 512).rearrange("p (c n) -> p c n", c=4)
        gm_w0 = stat[:, 252:256]
        pages_i = at(O_SC + 2312, N_PAGES * NS).bitcast(I32)
        pages_f = at(O_SC + 2440, N_PAGES * NS)
        k_sel = at(O_QR, 2048).rearrange("p (a n) -> p a n", n=P)
        v_sel = at(O_VG, 2048).rearrange("p (a n) -> p a n", n=P)
        k_selT = at(O_S, 2048).rearrange("p (b n) -> p b n", b=NS)
        soft_s = at(O_PT, 2 * 257).rearrange("p (g n) -> p g n", g=2)
        page_hot = at(O_WORK, 256).rearrange("p (a n) -> p a n", n=N_PAGES)
        q_lhs = at(O_WORK + 256, 256).rearrange("p (b m) -> p b m", b=NS)
        probsT_s = at(O_WORK + 512, 512).rearrange("p (a n) -> p a n", n=P)
        sel_tmp = at(O_WORK + 1024, 128)
        new_probs = sel_tmp[:, 0:2 * NH].rearrange("p (g h) -> p g h", g=2)
        new_spread = sel_tmp[:, 16:16 + NS * NH]
        slot_f = at(O_PT + 520, 16)
        slot_i = at(O_PT + 540, 16).bitcast(I32)
        off_i = at(O_PT + 560, 16).bitcast(I32)
        page_f = at(O_PT + 580, 16)
        off_f = at(O_PT + 600, 16)
        sel_rows = at(O_PT + 620, 16).bitcast(I32)
        idx_u = idx.bitcast(U32)
        key_bias = scores[:, 0:TOPK_S + 1]
        idx_f = scores[:, 512:512 + TOPK_S]
        sstat = sb("sstat", [P, 64])
        mx4 = [sstat[:, 0:4], sstat[:, 4:8]]
        sum4 = [sstat[:, 8:12], sstat[:, 12:16]]
        inv4 = [sstat[:, 16:20], sstat[:, 20:24]]
        mx2, sum2, inv2 = sstat[:, 24:26], sstat[:, 26:28], sstat[:, 28:30]
        idx_max = sstat[:, 48:49]

        x2 = at(0, (NT + 1) * D).rearrange("p (t n) -> p t n", n=D)
        mod2 = {m: at(o, 2 * D).rearrange("p (g n) -> p g n", g=2)
                for m, o in (("gate2", 5120), ("gate1", 7168), ("shift2", 9216), ("scale2", 11264))}
        t2 = at(13312, (NT + 1) * D).rearrange("p (t n) -> p t n", n=D)
        gain2 = at(23552, D)
        w_tmp = at(25600, 1024).rearrange("p (b n) -> p b n", b=2)
        w_router = at(26624, KD * (NEG + NE)).rearrange("p (k n) -> p k n", k=KD)
        b_router = at(26912, NEG + NE)
        junk2 = at(19456, D)
        router_at = [27648]

        def rt(n):
            router_at[0] += n
            assert router_at[0] <= ARENA
            return at(router_at[0] - n, n)

        T5 = NT + 1
        logits_T = rt(TOK)
        logits = rt(T5 * (NEG + NE)).rearrange("p (t n) -> p t n", t=T5)
        e_logits, hot1, hot2, e_tmp, chosen, place = (rt(T5 * NE).rearrange("p (t n) -> p t n", t=T5) for _ in range(6))
        before_sum = rt((T5 + 1) * NE).rearrange("p (t n) -> p t n", n=NE)
        g_tmp = rt(T5 * NEG).rearrange("p (t n) -> p t n", t=T5)
        g_exp = rt(T5 * NEG).rearrange("p (t n) -> p t n", t=T5)
        slot_hot = rt(2 * T5 * P).rearrange("p (a n) -> p a n", n=P)
        item_hot = rt(2 * T5 * 2 * N_ITEMS).rearrange("p (a n) -> p a n", n=2 * N_ITEMS)
        over_cmp = at(26960, NE * 8).rearrange("p (e m) -> p e m", m=8)
        over_hot = at(26960, N_OVER * NE).rearrange("p (j e) -> p j e", e=NE)
        r = sb("router", [P, 400])
        g_max, e_max1, e_max2, w_max, g_sum, p_first, e_ratio = (r[:, 5 * i:5 * i + 5] for i in range(7))
        rank = r[:, 40:50].rearrange("p (c t) -> p c t", c=2)
        gate_of = r[:, 50:60].rearrange("p (c t) -> p c t", c=2)
        token_of = r[:, 60:70].rearrange("p (c t) -> p c t", c=2)
        rank_i = r[:, 70:80].bitcast(I32)
        slot_of_i, item_of_i = r[:, 80:90].bitcast(I32), r[:, 90:100].bitcast(I32)
        slot_of, item_of = r[:, 100:110], r[:, 110:120]
        n_over, over_end, over_shift, counts = (r[:, 120 + 32 * i:152 + 32 * i] for i in range(4))
        over_expert_f, over_expert = r[:, 248:264], r[:, 264:288].bitcast(I32)
        item_counts = r[:, 388:391].bitcast(I32)
        gate_tab = r[:, 288:288 + N_ITEMS]
        token_tab = r[:, 336:337 + N_ITEMS].bitcast(I32)

        flat_ring = ring.rearrange("p r n -> p (r n)")
        GU, DN = KD * 2 * DE, 2 * D
        w_gu = [w.rearrange("p (k n) -> p k n", k=KD) for w in (
            ring[:, 1, 0:GU], ring[:, 2, 0:GU], ring[:, 0, 0:GU], hT.rearrange("p k n -> p (k n)")[:, 0:GU],
            at(7168, GU), at(11264, GU))]
        w_dn = [at(o, DN).rearrange("p (f n) -> p f n", f=2) for o in (15360, 17408, 24832, 26880, 28928, 30976)]
        x_rows = at(19456, 2 * D).rearrange("p (b n) -> p b n", b=2)
        y_rows = at(21504, 1024).rearrange("p (b n) -> p b n", b=2)
        silu_g = at(22528, 2 * DE).rearrange("p (b n) -> p b n", b=2)
        hidden = at(23040, 2 * DE).rearrange("p (b n) -> p b n", b=2)
        x_T = at(23552, 2 * KD * SB).rearrange("p (b k n) -> p b k n", b=2, k=KD)
        hidden_T = at(24576, 4 * SB).rearrange("p (b f n) -> p b f n", b=2, f=2)
        next_token = r[:, 392:394].bitcast(I32)
        picked = flat_ring[:, 0:2 * T5 * D].rearrange("p (t c n) -> p t c n", t=T5, c=2)

        bank_full = [sem(f"bank_full{b}") for b in range(8)]
        bank_free = [sem(f"bank_free{b}") for b in range(8)]
        banks = Banks(bank_full, bank_free)
        ring_full = [sem(f"ring_full{i}") for i in range(RING)]
        const_in = sem("const_in")
        c_in = sem("c_in")
        bias_in = sem("bias_in")
        ada_bias_in = sem("ada_bias_in")
        vg_s_stored = sem("vg_s_stored")
        ln_in = sem("ln_in")
        gmlp_in, ws_in = sem("gmlp_in"), sem("ws_in")
        x_in = [sem(f"x_in{t}") for t in range(NT + 1)]
        pages_in = sem("pages_in")
        c_silu = sem("c_silu")
        zeroed, raw_zeroed = sem("zeroed"), sem("raw_zeroed")
        ssq_ready = sem("ssq_ready")
        rstd_asked, rstd_ready = sem("rstd_asked"), sem("rstd_ready")
        h_ready = sem("h_ready")
        a_ready = sem("a_ready")
        k_ready = sem("k_ready")
        q_ready = sem("q_ready")
        vg_ready = sem("vg_ready")
        qi_dup_ready = sem("qi_dup_ready")
        qi_lhs_ready = sem("qi_lhs_ready")
        relu_p_read = sem("relu_p_read")
        page_rows_ready = sem("page_rows_ready")
        ki_in = [sem(f"ki_in{i}") for i in range(2)]
        ki_used = sem("ki_used")
        outs, y_outs = sem("outs"), sem("y_outs")
        late_in = sem("late_in")
        over_zeroed = sem("over_zeroed")
        x2_in = sem("x2_in")
        router_in = sem("router_in")
        x2_half, x2_ready = sem("x2_half"), sem("x2_ready")
        ssq2_ready = sem("ssq2_ready")
        t2_ready = sem("t2_ready")
        t2_stored = sem("t2_stored")
        g_diff_ready, g_exp_ready = sem("g_diff_ready"), sem("g_exp_ready")
        e_diff_ready, e_exp_ready = sem("e_diff_ready"), sem("e_exp_ready")
        chosen_ready = sem("chosen_ready")
        tables_hot_ready, tables_ready = sem("tables_hot_ready"), sem("tables_ready")
        w_got = [sem(f"w_got{k}") for k in range(BUFFERS)]
        x_got = [sem(f"x_got{i}") for i in range(2)]
        y_stored = [sem(f"y_stored{i}") for i in range(2)]
        (xT_full, xT_out, gu_full, silu_done, hidden_done, hT_full, hT_out, y_full, y_out) = (
            sem(n) for n in ("xT_full", "xT_out", "gu_full", "silu_done", "hidden_done", "hT_full", "hT_out", "y_full",
                             "y_out"))
        token_copied = sem("token_copied")
        pe_passed, pool_passed, pe_finished, pool_finished = (
            sem(n) for n in ("pe_passed", "pool_passed", "pe_finished", "pool_finished"))
        picked_in = [sem(f"picked_in{t}") for t in range(T5)]
        y_ready = sem("y_ready")
        ws_masked = sem("ws_masked")
        gm_ready, gm_tile = sem("gm_ready"), sem("gm_tile")
        max_ready, exp_ready, probs_ready = sem("max_ready"), sem("exp_ready"), sem("probs_ready")
        idx_ready = sem("idx_ready")
        pages_all_in = sem("pages_all_in")
        sel_rows_ready = sem("sel_rows_ready")
        k_sel_in, v_sel_in = sem("k_sel_in"), sem("v_sel_in")
        key_bias_ready = sem("key_bias_ready")
        q_lhs_ready = sem("q_lhs_ready")
        max_s_ready, probs_s_ready = sem("max_s_ready"), sem("probs_s_ready")
        new_spread_ready = sem("new_spread_ready")
        merged = sem("merged")
        values_done = sem("values_done")
        vector_lane, scalar_lane, pool_lane = sem("vector_lane"), sem("scalar_lane"), sem("pool_lane")
        n_outs = [0]
        last_use = {}
        H_ORDER = (0, NT, 1, 2, 3)
        ORDER = [(0, P, 0), (1, P, 1), ("S", NS, NT), (2, P, 2), (3, P, 3)]

        def lone_wait(engine, semaphore, value, passed):
            engine.wait_ge(semaphore, value)
            engine.sem_inc(passed, 1)

        def load_n_items(engine, which=0):
            least, most = (NE, N_ITEMS) if which == 0 else (16 * NE, 16 * N_ITEMS)
            return engine.value_load(item_counts[0:1, which:which + 1], min_val=least, max_val=most)

        def each_item(engine, item):
            for k in range(BUFFERS):
                item(0, k, True)
            with engine.Fori(1, LATE) as i:
                for k in range(BUFFERS):
                    item(i, k, False)
            n_items = load_n_items(engine)
            with engine.Fori(LATE, N_ITEMS // BUFFERS) as i:
                for k in range(BUFFERS):
                    with engine.If(i * BUFFERS + k < n_items):
                        item(i, k, False)
            return n_items

        def ring_wait(pe, name):
            n = SLOT_OF[name]
            pe.wait_ge(ring_full[n % RING], 16 * (n // RING + 1))

        def ring_at(name, width):
            kk = STREAM[SLOT_OF[name]][1] // width
            return ring[:, SLOT_OF[name] % RING, 0:kk * width].rearrange("p (k n) -> p k n", k=kk)

        def pair(b0):
            return psum[:, b0:b0 + 2, 0:HALF]

        def halves(ap):
            return ap.rearrange("p (s n) -> p s n", s=2)

        block = ctx.enter_context(nc.Block())

        @block.tensor
        def _(pe):
            def grouped(name, b, width, weights, lhs, bias=None):
                banks.begin(pe, name, b)
                if bias is not None:
                    pe.matmul(psum[0:32, b, 0:width], ident[0:12, bias:bias + 1].broadcast_to([12, 32]),
                              ada_bias[0:12, :], start=True, stop=False, tile_position=(0, 0))
                for k in range(KD):
                    j = k % 4
                    mm = pe.matmul(psum[32 * j:32 * j + 32, b, 0:width], lhs[:, k, :], weights[:, k, :],
                                   start=(k < 4 and (j > 0 or bias is None)), stop=(k >= 4),
                                   tile_position=(0, 32 * j))
                banks.filled(mm, name)

            def ada_product(c, b):
                ring_wait(pe, f"ada{c}")
                grouped(("ada", c), b, 512, ring_at(f"ada{c}", 512), c_T, bias=c)
                last_use[f"ada{c}"] = ("ada", c)

            def ada_spread(c):
                banks.wait_drained(pe, ("ada", c))
                for name, sel, b, rows in (("adaP", "sel_p", 2 + c % 2, P), ("adaS", "sel_s", 4 + c % 2, NS)):
                    banks.begin(pe, (name, c), b)
                    part = G[:, c % 2, :] if c < 4 else late_G[c - 4]
                    mm = pe.matmul(psum[0:rows, b, :], C(sel), part, start=True, stop=True)
                    banks.filled(mm, (name, c))

            pe.wait_ge(const_in, 16)
            pe.wait_ge(c_silu, 1)
            for c in range(5):
                if c == 0:
                    pe.wait_ge(ada_bias_in, 16)
                if c < 4:
                    ada_product(c, c % 2)
                if c >= 1:
                    ada_spread(c - 1)

            def h_transposes(i):
                t = H_ORDER[i]
                n = P if t < NT else NS
                pe.wait_ge(h_ready, i + 1)
                for j in range(2):
                    b = 6 + j - 2 * (i % 2)
                    banks.begin(pe, ("hT", t, j), b)
                    for k in range(4):
                        mm = pe.transpose(psum[:, b, k * n:(k + 1) * n], xbuf[0:n, t, (4 * j + k) * P:(4 * j + k + 1) * P],
                                          ident[0:n, 0:n])
                    banks.filled(mm, ("hT", t, j))

            def rows_tile(name, width, t, b):
                if t == 0:
                    ring_wait(pe, name)
                w = ring_at(name, width)
                banks.begin(pe, (name, t), b)
                for k in range(KD):
                    mm = pe.matmul(psum[:, b, 0:width], hT[:, k, t * P:(t + 1) * P], w[:, k, :],
                                   start=(k == 0), stop=(k == KD - 1))
                banks.filled(mm, (name, t))
                last_use[name] = (name, t)

            def samples_products(name, width):
                grouped((name, "s"), 2, width, ring_at(name, width), hTs)
                last_use[name] = (name, "s")

            def samples_sums(name, width):
                banks.wait_drained(pe, (name, "s"))
                banks.begin(pe, (name, "S"), 3)
                mm = pe.matmul(psum[0:NS, 3, 0:width], C("sel_s"), G[:, 1, 0:width], start=True, stop=True)
                banks.filled(mm, (name, "S"))

            def rows_slice(name, width):
                for t in range(NT):
                    rows_tile(name, width, t, t % 2)
                    if t == 0:
                        samples_products(name, width)
                    if t == 1:
                        samples_sums(name, width)
                last_use[name] = (name, NT - 1)

            def feature_block(name, w, rhs, b0, f, first=True, last=True):
                kk = w.shape[1]
                for k in range(kk):
                    for s in range(2):
                        mm = pe.matmul(psum[:, b0 + s, 0:HALF], w[:, k, f * P:(f + 1) * P],
                                       rhs[:, k, s * HALF:(s + 1) * HALF],
                                       start=(first and k == 0), stop=(last and k == kk - 1))
                return mm

            def wait_hT(*tiles):
                for t in tiles:
                    for j in range(2):
                        banks.wait_drained(pe, ("hT", t, j))

            h_transposes(0)
            h_transposes(1)
            wait_hT(0)
            rows_tile("A", NA, 0, 0)
            wait_hT(NT)
            samples_products("A", NA)
            h_transposes(2)
            h_transposes(3)
            wait_hT(1)
            rows_tile("A", NA, 1, 1)
            samples_sums("A", NA)
            h_transposes(4)
            wait_hT(2)
            rows_tile("A", NA, 2, 0)
            wait_hT(3)
            rows_tile("A", NA, 3, 1)

            pe.wait_ge(a_ready, 1)
            for t in range(NT):
                b = 4 + t % 2
                banks.begin(pe, ("qkiT", t), b)
                for j in range(3):
                    src = araw[:, t, j * P:(j + 1) * P] if j < 2 else ki_twice[:, t, :]
                    mm = pe.transpose(psum[:, b, j * P:(j + 1) * P], src, ident)
                banks.filled(mm, ("qkiT", t))
            pe.wait_ge(qi_dup_ready, 1)
            banks.begin(pe, "qi_sample", 4)
            for h in range(IH):
                mm = pe.transpose(psum[:, 4, h * NS:(h + 1) * NS], qi_twice[0:NS, h].rearrange("p c d -> p (c d)"),
                                  ident[0:NS, 0:NS])
            banks.filled(mm, "qi_sample")
            banks.begin(pe, "wi_sample", 5)
            for c in range(4):
                mm = pe.transpose(psum[:, 5, c * NS:(c + 1) * NS], wi_place[0:NS, c * P:(c + 1) * P], ident[0:NS, 0:NS])
            banks.filled(mm, "wi_sample")

            for qb in range(1, NT):
                L = (qb + 1) * P
                if qb == 1:
                    for t in range(NT):
                        banks.wait_drained(pe, ("qkiT", t))
                banks.begin(pe, ("dots", qb), 0, 1, 2, 3)
                for h in range(IH):
                    o = HD * (h % 2)
                    mm = pe.matmul(psum[:, h, 0:L], qiT[o:o + ID, h // 2, qb * P:(qb + 1) * P], kiT[o:o + ID, 0:L],
                                   start=True, stop=True)
                banks.filled(mm, ("dots", qb))
                rows_tile("B", NB, qb - 1, 6 + (qb - 1) % 2)

            for b in range(NS):
                pe.wait_ge(ki_in[b % 2], 16 * (b // 2 + 1))
                for j in range(2):
                    banks.begin(pe, ("kiT", b, j), 4 + j)
                    for k in range(4):
                        r = 4 * j + k
                        mm = pe.transpose(psum[:, 4 + j, k * P:(k + 1) * P], ki_pages[:, b % 2, r * P:(r + 1) * P], ident)
                    banks.filled(mm, ("kiT", b, j))
                q = 32 * (b % 4)
                for j in range(2):
                    banks.wait_drained(pe, ("kiT", b, j))
                    if b % 4 == 0 and j == 0:
                        banks.wait_drained(pe, "qi_sample")
                        banks.begin(pe, ("dotsS", b // 4), 0 + 2 * (b // 4), 1 + 2 * (b // 4))
                    mm = pe.matmul(psum[q:q + 32, 2 * (b // 4) + j, :], qi_lhs[:, b, :],
                                   ki_T[:, b % 2, j * 512:(j + 1) * 512], start=True, stop=True, tile_position=(0, q))
                if b % 4 < 3:
                    mm.then_inc(ki_used, 1)
                else:
                    banks.filled(mm, ("dotsS", b // 4))
                if b == 1:
                    rows_tile("B", NB, 3, 7)
                elif b in (3, 5, 7):
                    rows_tile("C", NC, b // 2 - 1, 6 + (b // 2 - 1) % 2)
            banks.wait_drained(pe, "wi_sample")
            banks.wait_drained(pe, ("dotsS", 0))
            banks.wait_drained(pe, ("dotsS", 1))
            banks.begin(pe, "scoresS", 0, 1, 2, 3)
            for par in range(2):
                for j in range(2):
                    for g in range(2):
                        mm = pe.matmul(psum[0:NS, 2 * par + j, :], wi_lhs[:, 2 * g + par, :],
                                       relu_s[:, g, j * 512:(j + 1) * 512], start=(g == 0), stop=(g == 1))
            banks.filled(mm, "scoresS")

            samples_products("B", NB)
            rows_tile("C", NC, 3, 7)
            samples_sums("B", NB)
            samples_products("C", NC)
            rows_tile("D", ND, 0, 0)
            samples_sums("C", NC)
            samples_products("D", ND)
            rows_tile("D", ND, 1, 1)
            samples_sums("D", ND)
            rows_tile("D", ND, 2, 0)
            rows_tile("D", ND, 3, 1)

            def blocks(ring_name, key, rhs, n, b_of):
                ring_wait(pe, ring_name)
                w = ring_at(ring_name, 512)
                for f in range(n):
                    banks.begin(pe, (key, f), b_of(f), b_of(f) + 1)
                    mm = feature_block((key, f), w, rhs, b_of(f), f)
                    banks.filled(mm, (key, f))
                last_use[ring_name] = (key, n - 1)

            blocks("U", "U", hT, 4, lambda f: 2 * (f % 2))

            pe.wait_ge(q_ready, 1)
            for t in range(NT):
                b = 4 + t % 2
                banks.begin(pe, ("qT", t), b)
                for j in range(4):
                    mm = pe.transpose(psum[:, b, j * P:(j + 1) * P], qraw[:, t, j * P:(j + 1) * P], ident)
                banks.filled(mm, ("qT", t))
            pe.wait_ge(k_ready, 1)
            banks.begin(pe, "kT", 6)
            for t in range(NT):
                mm = pe.transpose(psum[:, 6, t * P:(t + 1) * P], kraw[:, t, :], ident)
            banks.filled(mm, "kT")
            banks.begin(pe, "qkT_s", 7)
            for j in range(5):
                src = qraw[0:NS, NT, j * P:(j + 1) * P] if j < 4 else kraw[0:NS, NT, :]
                mm = pe.transpose(psum[:, 7, j * NS:(j + 1) * NS], src, ident[0:NS, 0:NS])
            banks.filled(mm, "qkT_s")

            pe.wait_ge(vg_ready, 1)
            pe.wait_ge(ws_masked, 1)
            for j in range(4):
                b = 4 + j % 2
                banks.begin(pe, ("mix", j), b)
                for c in range(NT):
                    for par in range(2):
                        g = 2 * j + par
                        mm = pe.matmul(psum[GD * par:GD * par + GD, b, c * P:(c + 1) * P], vg[:, c, g * GD:(g + 1) * GD],
                                       wsT[:, g, :], start=True, stop=True, tile_position=(0, GD * par))
                banks.filled(mm, ("mix", j))
            banks.begin(pe, "vgT_s", 6)
            for j in range(4):
                mm = pe.transpose(psum[:, 6, j * NS:(j + 1) * NS], vg[0:NS, NT, j * P:(j + 1) * P], ident[0:NS, 0:NS])
            banks.filled(mm, "vgT_s")

            groups = [(qb, kv) for qb in range(NT) for kv in range(NKV)]

            def att_scores(g):
                qb, kv = groups[g]
                L = (qb + 1) * P
                o = HD * kv
                if g == 0:
                    for t in range(NT):
                        banks.wait_drained(pe, ("qT", t))
                    banks.wait_drained(pe, "kT")
                banks.begin(pe, ("att_s", g), 0, 1, 2, 3)
                for j in range(4):
                    mm = pe.matmul(psum[:, j, 0:L], qT[o:o + HD, j, qb * P:(qb + 1) * P], kT[o:o + HD, 0:L],
                                   start=True, stop=True)
                banks.filled(mm, ("att_s", g))

            def att_values(g):
                qb, kv = groups[g]
                pe.wait_ge(probs_ready, g + 1)
                for c in range(qb + 1):
                    b = 4 + c % 2
                    banks.begin(pe, ("probsT", g, c), b)
                    for j in range(4):
                        mm = pe.transpose(psum[:, b, j * P:(j + 1) * P], soft[g % 2][:, j, c * P:(c + 1) * P], ident)
                    banks.filled(mm, ("probsT", g, c))
                if kv == 0:
                    banks.begin(pe, ("att", qb), 6 + qb % 2)
                for c in range(qb + 1):
                    banks.wait_drained(pe, ("probsT", g, c))
                    mm = pe.matmul(psum[HD * kv:HD * kv + HD, 6 + qb % 2, :], araw[:, c, VV + HD * kv:VV + HD * kv + HD],
                                   probsT[:, c, :], start=(c == 0), stop=(c == qb), tile_position=(0, HD * kv))
                if kv == 1:
                    banks.filled(mm, ("att", qb))
                else:
                    mm.then_inc(values_done, 1)

            def gate_block(n):
                c, f = n // 4, n % 4
                name = f"G{c}"
                if f == 0:
                    ring_wait(pe, name)
                banks.begin(pe, (name, f), 2 * (f % 2), 2 * (f % 2) + 1)
                banks.filled(feature_block((name, f), ring_at(name, 512), hT, 2 * (f % 2), f), (name, f))
                last_use[name] = (name, f)

            att_scores(0)
            for g in range(len(groups)):
                if g + 1 < len(groups):
                    att_scores(g + 1)
                att_values(g)
                gate_block(2 * g)
                if g == len(groups) - 1:
                    pe.wait_ge(idx_ready, 1)
                    banks.begin(pe, "idxT", 4)
                    for h in range(2):
                        mm = pe.transpose(psum[:, 4, h * NS:(h + 1) * NS], idx_f[0:NS, h * P:(h + 1) * P],
                                          ident[0:NS, 0:NS])
                    banks.filled(mm, "idxT")
                gate_block(2 * g + 1)
                ada_product(4 + g, 6 + (g // NKV + 1) % 2)

            ring_wait(pe, "WG")
            pe.wait_ge(gm_ready, 1)

            def gmlp_blocks(*fs):
                for f in fs:
                    b = 2 + 4 * (f % 2)
                    banks.begin(pe, ("WG", f), b, b + 1)
                    banks.filled(feature_block(("WG", f), ring_at("WG", D), uT, b, f), ("WG", f))
                    last_use["WG"] = ("WG", f)

            gmlp_blocks(0, 1, 2, 3)
            pe.wait_ge(k_sel_in, 16 * 2 * NS)
            for b in range(NS):
                bank = 6 + b % 2
                banks.begin(pe, ("k_selT", b), bank)
                for h in range(2):
                    mm = pe.transpose(psum[:, bank, h * P:(h + 1) * P], k_sel[:, h * NS + b, :], ident)
                banks.filled(mm, ("k_selT", b))
            pe.wait_ge(key_bias_ready, 1)
            pe.wait_ge(q_lhs_ready, 2)
            spread = C("spread").rearrange("p (g n) -> p g n", g=2)
            for g in range(2):
                banks.begin(pe, ("att_ss", g), g)
                pe.matmul(psum[:, g, 0:TOPK_S + 1], spread[0:NS, g, :], key_bias[0:NS, :], start=True, stop=False,
                          skip_group_check=True)
                for i in range(4):
                    b = 4 * g + i
                    banks.wait_drained(pe, ("k_selT", b))
                    pe.matmul(psum[32 * i:32 * i + 32, g, 0:TOPK_S], q_lhs[:, b, :], k_selT[:, b, :],
                              start=False, stop=True, skip_group_check=True, tile_position=(0, 32 * i))
                    mm = pe.matmul(psum[32 * i:32 * i + 32, g, TOPK_S:TOPK_S + 1], q_lhs[:, b, :],
                                   kT[:, SEQ + b:SEQ + b + 1], start=False, stop=True, skip_group_check=True,
                                   tile_position=(0, 32 * i))
                banks.filled(mm, ("att_ss", g))
            gmlp_blocks(4, 5)
            pe.wait_ge(probs_s_ready, 1)
            banks.begin(pe, "probsT_s", 2)
            for g in range(2):
                for h in range(2):
                    a = 2 * g + h
                    mm = pe.transpose(psum[:, 2, a * P:(a + 1) * P], soft_s[:, g, h * P:(h + 1) * P], ident)
            banks.filled(mm, "probsT_s")
            banks.begin(pe, "new_probs", 3)
            rows_of = C("gather").rearrange("p (g b) -> p g b", g=2)
            for g in range(2):
                mm = pe.matmul(psum[0:NS, 3, 0:NH], rows_of[:, g, :], new_probs[:, g, :], start=(g == 0), stop=(g == 1))
            banks.filled(mm, "new_probs")
            gmlp_blocks(6, 7)
            pe.wait_ge(new_spread_ready, 1)
            pe.wait_ge(v_sel_in, 16 * 2 * NS)
            banks.wait_drained(pe, "probsT_s")
            banks.begin(pe, "att_samples", 4)
            pe.matmul(psum[:, 4, 0:NS * NH], araw[0:NS, NT, VV:VV + NKV * HD], new_spread[0:NS, :], start=True, stop=False,
                      skip_group_check=True)
            for b in range(NS):
                for h in range(2):
                    o = 32 * (b % 4)
                    mm = pe.matmul(psum[:, 4, b * NH:(b + 1) * NH], v_sel[:, h * NS + b, :],
                                   probsT_s[:, 2 * (b // 4) + h, o:o + NH], start=False, stop=True, skip_group_check=True)
            banks.filled(mm, "att_samples")

            ring_wait(pe, "WA")
            banks.wait_drained(pe, "att_samples")
            for t in range(NT):
                banks.wait_drained(pe, ("att", t))
            for f in range(KD):
                b = 4 * (f % 2)
                banks.begin(pe, ("WA", f), b, b + 1)
                banks.filled(feature_block(("WA", f), ring_at("WA", D), attT, b, f), ("WA", f))
            last_use["WA"] = ("WA", KD - 1)
            for c in range(4, 10):
                ada_spread(c)

            pe.wait_ge(merged, KD)
            rows_slice("O0", 512)
            rows_slice("O1", 512)

            def t2_transposes(i):
                _, n, t = ORDER[i]
                pe.wait_ge(t2_ready, i + 1)
                for j in range(2):
                    b = 4 + j + 2 * (i % 2)
                    banks.begin(pe, ("t2T", t, j), b)
                    for k in range(4):
                        mm = pe.transpose(psum[:, b, k * n:(k + 1) * n], t2[0:n, t, (4 * j + k) * P:(4 * j + k + 1) * P],
                                          ident[0:n, 0:n])
                    banks.filled(mm, ("t2T", t, j))

            def router_logits(s, tiles):
                for t in tiles:
                    for j in range(2):
                        banks.wait_drained(pe, ("t2T", t, j))
                banks.begin(pe, ("logits", s), s)
                for k in range(KD):
                    mm = pe.matmul(psum[0:NEG + NE, s, 0:HALF], w_router[:, k, :], hT[:, k, s * HALF:(s + 1) * HALF],
                                   start=(k == 0), stop=(k == KD - 1))
                banks.filled(mm, ("logits", s))

            for i in range(4):
                t2_transposes(i)
            pe.wait_ge(router_in, 32)
            router_logits(0, (0, 1, 2))
            t2_transposes(4)
            router_logits(1, (3, NT))
            for s in range(2):
                banks.wait_drained(pe, ("logits", s))
            banks.begin(pe, "logits_rows", 2)
            for t in range(T5):
                n = P if t < NT else NS
                mm = pe.transpose(psum[0:n, 2, t * 36:t * 36 + 36], logits_T[0:36, t * P:t * P + n], ident[0:36, 0:36])
            banks.filled(mm, "logits_rows")
            pe.wait_ge(chosen_ready, 1)
            banks.begin(pe, "places", 3)
            pe.matmul(psum[:, 3, 0:(T5 + 1) * NE], C("ones"), before_sum.rearrange("p t n -> p (t n)"), start=True,
                      stop=False, skip_group_check=True)
            mm = pe.matmul(psum[:, 3, 0:T5 * NE], C("before"), chosen.rearrange("p t n -> p (t n)"), start=False,
                           stop=True, skip_group_check=True)
            banks.filled(mm, "places")
            for c in (10, 11):
                ada_spread(c)
            pe.wait_ge(tables_hot_ready, 1)
            banks.begin(pe, "tables", 4)
            for a in range(2 * T5):
                mm = pe.matmul(psum[:, 4, 0:2 * N_ITEMS], slot_hot[:, a, :], item_hot[:, a, :],
                               start=(a == 0), stop=(a == 2 * T5 - 1))
            banks.filled(mm, "tables")

            def x_transposes(p, full):
                for k in range(KD):
                    mm = pe.transpose(psum[:, p, k * SB:(k + 1) * SB], x_rows[0:SB, p, k * P:(k + 1) * P],
                                      ident[0:SB, 0:SB])
                mm.then_inc(full, 1)

            def gate_up(p, w, full):
                for k in range(KD):
                    for half in range(2):
                        col = DE * (1 - half)
                        mm = pe.matmul(psum[SB * half:SB * half + SB, 2 + p, 0:DE], x_T[:, p, k, :],
                                       w[:, k, col:col + DE], start=(k == 0), stop=(k == KD - 1),
                                       tile_position=(0, SB * half))
                mm.then_inc(full, 1)

            def hidden_transposes(p, full):
                for f in range(2):
                    mm = pe.transpose(psum[:, 4 + p, f * SB:(f + 1) * SB], hidden[0:SB, p, f * P:(f + 1) * P],
                                      ident[0:SB, 0:SB])
                mm.then_inc(full, 1)

            def down(p, w, full):
                for f in range(2):
                    for half in range(2):
                        mm = pe.matmul(psum[SB * half:SB * half + SB, 6 + p, :], hidden_T[:, p, f, :],
                                       w[:, f, 512 * half:512 * half + 512], start=(f == 0), stop=(f == 1),
                                       tile_position=(0, SB * half))
                mm.then_inc(full, 1)

            for name in ("logits_rows", "places", "tables", ("adaP", 10), ("adaP", 11), ("adaS", 10), ("adaS", 11)):
                banks.wait_drained(pe, name)
            pe.wait_ge(x_got[0], 16)
            x_transposes(0, xT_full)

            def pe_item(i, k, first):
                e, p = i * BUFFERS + k, k % 2
                pe.wait_ge(w_got[k], i * 32 + 32)
                pe.wait_ge(xT_out, e + 1)
                if not (first and k < 2):
                    pe.wait_ge(hidden_done, e - 1)
                gate_up(p, w_gu[k], gu_full)
                if not (first and k < 1):
                    pe.wait_ge(xT_out, e)
                lone_wait(pe, x_got[1 - p], i * (8 * BUFFERS) + 16 * ((k + 1) // 2) + 16, pe_passed)
                x_transposes(1 - p, xT_full)
                if not (first and k < 2):
                    pe.wait_ge(hT_out, e - 1)
                lone_wait(pe, hidden_done, e + 1, pe_passed)
                hidden_transposes(p, hT_full)
                pe.wait_ge(hT_out, e + 1)
                if not (first and k < 2):
                    pe.wait_ge(y_out, e - 1)
                down(p, w_dn[k], y_full)

            n_items = each_item(pe, pe_item)
            pe.wait_ge(pe_passed, n_items * 2)
            lone_wait(pe, xT_out, n_items + 1, pe_finished)

        @block.sync
        def _(sp):
            sp.dma_start(const[:, :], io["consts"]).then_inc(const_in, 16)
            sp.dma_start(ada_bias[0:12, :], io["b_ada"]).then_inc(ada_bias_in, 16)
            sp.dma_start(c_T[:, :, :], io["c_T"].rearrange("p (k n) -> p k n", k=KD)).then_inc(c_in, 16)
            for n, (name, size) in enumerate(STREAM):
                if n == 1:
                    sp.dma_start(gain1, io["norm_mix_g"].partition_broadcast(P)).then_inc(bias_in, 16)
                if n == 2:
                    sp.dma_start(gains[:, :], io["head_gains"].partition_broadcast(P)).then_inc(bias_in, 16)
                if n >= RING:
                    banks.wait_full(sp, last_use[STREAM[n - RING][0]])
                sp.dma_start(ring[:, n % RING, 0:size], io["stream"][n, :, 0:size]).then_inc(ring_full[n % RING], 16)
            def expert_src(e):
                return io["experts"].rearrange("e p n -> (e p) n")[bass.ds(e * P, P), :]

            def load_gate_up(k, e):
                sp.dma_start(w_gu[k].rearrange("p k n -> p (k n)"), expert_src(e)[:, 0:GU]).then_inc(w_got[k], 16)

            def load_down(k, e):
                sp.dma_start(w_dn[k].rearrange("p f n -> p (f n)"), expert_src(e)[:, GU:GU + DN]).then_inc(w_got[k], 16)

            banks.wait_full(sp, last_use["WA"])
            load_gate_up(0, 0)
            banks.wait_full(sp, last_use["O0"])
            load_gate_up(1, 1)
            banks.wait_full(sp, last_use["O1"])
            load_gate_up(2, 2)
            sp.wait_ge(t2_ready, T5)
            load_gate_up(4, 4)
            for t in range(T5):
                for j in range(2):
                    banks.wait_drained(sp, ("t2T", t, j))
            sp.wait_ge(t2_stored, 16 * T5)
            load_gate_up(5, 5)
            load_down(0, 0)
            load_down(1, 1)
            for s in range(2):
                banks.wait_full(sp, ("logits", s))
            load_gate_up(3, 3)
            banks.wait_full(sp, ("adaS", 11))
            banks.wait_drained(sp, "logits_rows")
            load_down(2, 2)
            banks.wait_full(sp, "tables")
            sp.wait_ge(x_got[0], 16)
            for k in (3, 4, 5):
                load_down(k, k)
            sp.wait_ge(over_zeroed, 16)

            def store_item(i, k):
                e, p = i * BUFFERS + k, k % 2
                sp.wait_ge(y_out, e + 1)
                for half in range(2):
                    dst = io["expert_rows"][bass.ds(e * SB, SB), 512 * half:512 * half + 512]
                    sp.dma_start(dst, y_rows[SB * half:SB * half + SB, p, :]).then_inc(y_stored[p], 16)

            def load_next(i, k):
                e = i * BUFFERS + k
                sp.wait_ge(gu_full, e + 1)
                load_gate_up(k, e + BUFFERS)
                sp.wait_ge(y_full, e + 1)
                load_down(k, e + BUFFERS)

            def load_if_any(i, k, n_items):
                e = i * BUFFERS + k
                with sp.If(e + BUFFERS < n_items):
                    expert = sp.value_load(over_expert[0:1, bass.ds(e + BUFFERS - NE, 1)], min_val=0, max_val=NE - 1)
                    sp.wait_ge(gu_full, e + 1)
                    load_gate_up(k, expert)
                    sp.wait_ge(y_full, e + 1)
                    load_down(k, expert)

            for k in range(BUFFERS):
                load_next(0, k)
                store_item(0, k)
            with sp.Fori(1, LATE - 1) as i:
                for k in range(BUFFERS):
                    load_next(i, k)
                    store_item(i, k)
            n_items = load_n_items(sp)
            for k in range(BUFFERS):
                if LATE * BUFFERS + k < NE:
                    load_next(LATE - 1, k)
                else:
                    load_if_any(LATE - 1, k, n_items)
                store_item(LATE - 1, k)
            with sp.Fori(LATE, N_ITEMS // BUFFERS) as i:
                for k in range(BUFFERS):
                    load_if_any(i, k, n_items)
                    with sp.If(i * BUFFERS + k < n_items):
                        store_item(i, k)
            sp.wait_ge(pe_finished, 1)
            sp.wait_ge(pool_finished, 2)
            for t in range(T5):
                n = P if t < NT else NS
                sp.wait_ge(y_ready, t + 1)
                dst = io["y_p"][t * P:(t + 1) * P, :] if t < NT else io["y_s"]
                sp.dma_start(dst, x2[0:n, t, :]).then_inc(y_outs, 16)
            sp.wait_ge(y_outs, 16 * T5)

        @block.gpsimd
        def _(pool):
            lane = Lane(pool, pool_lane)

            def rsqrt(n_asked, out, in_, width):
                pool.wait_ge(rstd_asked, n_asked)
                pool.tensor_tensor(out, in_, minus_half[:, 0:width], ALU.pow).then_inc(rstd_ready, 1)

            def store(dst, src):
                pool.dma_start(dst, src).then_inc(outs, 16)
                n_outs[0] += 1

            for t in range(NT):
                pool.dma_start(xbuf[:, t, :], io["x_prompt"][t * P:(t + 1) * P, :]).then_inc(x_in[t], 16)
            pool.dma_start(xbuf[0:NS, NT, :], io["x_sample"]).then_inc(x_in[NT], 16)
            pool.dma_start(page_rep, io["page_rep"]).then_inc(pages_in, 16)
            pool.wait_ge(zeroed, 1)
            rsqrt(1, rstd, ssq, 5)
            pool.dma_start(ln, io["ln"].partition_broadcast(P)).then_inc(ln_in, 16)
            pool.dma_start(wsT, io["ws_T"].rearrange("p (g t) -> p g t", g=GG)).then_inc(ws_in, 16)
            gm_b = io["gm_b"].rearrange("(j c) t -> c j t", c=2)
            for par in range(2):
                rows = slice(GD * par, GD * par + GD)
                pool.dma_start(bT[rows], gm_b[par].partition_broadcast(GD)).then_inc(gmlp_in, 16)
                pool.dma_start(gm_w0[rows], io["ws_00"][par].partition_broadcast(GD)).then_inc(gmlp_in, 16)

            pool.wait_ge(page_rows_ready, 1)
            banks.wait_drained(pool, ("hT", NT, 1))
            for b in range(NS):
                if b >= 2:
                    banks.wait_full(pool, ("kiT", b - 2, 1))
                pool.indirect_dma_start(ki_pages[:, b % 2, :], None, io["cache_ki"],
                                        bass.IndirectOffsetOnAxis(page_rows[:, b:b + 1], 0)).then_inc(ki_in[b % 2], 16)
                if b == 1:
                    pool.wait_ge(ws_in, 16)
                    pool.affine_select(out=wsT, in_=wsT, pattern=[[0, GG], [1, CHUNK]], compare_op=ALU.is_ge, fill=0.0,
                                       base=0, channel_multiplier=-1).then_inc(ws_masked, 1)
                    rsqrt(2, ki_r, ki_ms, 5)
            pool.wait_ge(a_ready, 1)
            store(io["new_ki_p"].rearrange("(t p) d -> p t d", p=P), araw[:, 0:NT, KI:KI + ID])
            store(io["new_ki_s"], araw[0:NS, NT, KI:KI + ID])
            store(io["new_v_p"].rearrange("(t p) d -> p t d", p=P), araw[:, 0:NT, VV:VV + P])
            store(io["new_v_s"], araw[0:NS, NT, VV:VV + P])
            over_rows = io["expert_rows"][NE * SB:, :].rearrange("(p a) (b n) -> p (a b) n", p=P, n=256)
            pool.dma_start(over_rows, spread_dim(zeros[:, :], 1, over_rows.shape[1])).then_inc(over_zeroed, 16)
            rsqrt(3, q_r, q_ms, 40)
            rsqrt(4, k_r, k_ms, 10)
            pool.wait_ge(k_ready, 1)
            store(io["new_k_p"].rearrange("(t p) d -> p t d", p=P), kraw[:, 0:NT, :])
            store(io["new_k_s"], kraw[0:NS, NT, :])
            rsqrt(5, vg_r, mu_var[:, :, 1], 5)
            pool.wait_ge(vg_ready, 1)
            pool.dma_start(io["new_vg_s"], vg[0:NS, NT, :]).then_inc(vg_s_stored, 16)
            pool.dma_start(pages_i, io["pages"].partition_broadcast(P)).then_inc(pages_all_in, 16)
            for qb in range(NT):
                banks.wait_drained(pool, ("att", qb))
            pool.wait_ge(sel_rows_ready, 1)
            for dst, src, got in ((k_sel, "cache_k", k_sel_in), (v_sel, "cache_v", v_sel_in)):
                for a in range(2 * NS):
                    pool.indirect_dma_start(dst[:, a, :], None, io[src], bass.IndirectOffsetOnAxis(sel_rows[:, a:a + 1], 0))\
                        .then_inc(got, 16)
            pool.wait_ge(merged, KD)
            pool.dma_start(gain2, io["norm_ffn_g"].partition_broadcast(P)).then_inc(late_in, 16)
            for t in range(NT):
                pool.dma_start(x2[:, t, :], io["x_prompt"][t * P:(t + 1) * P, :]).then_inc(x2_in, 16)
            pool.dma_start(x2[0:NS, NT, :], io["x_sample"]).then_inc(x2_in, 16)
            pool.dma_start(w_router, io["w_router"].rearrange("p (k n) -> p k n", k=KD)).then_inc(router_in, 16)
            pool.dma_start(b_router, io["b_router"].partition_broadcast(P)).then_inc(router_in, 16)
            for i, (_, _, t) in enumerate(ORDER):
                rsqrt(6 + i, rstd[:, t:t + 1], ssq[:, t:t + 1], 1)
            pool.wait_ge(t2_stored, 16 * T5)
            pool.wait_ge(tables_ready, 1)
            for e in range(NE + 1):
                if e >= 2:
                    pool.wait_ge(xT_full, e - 1)
                pool.indirect_dma_start(x_rows[0:SB, e % 2, :], None, io["t2_rows"],
                                        bass.IndirectOffsetOnAxis(token_tab[0:SB, e:e + 1], 0)).then_inc(x_got[e % 2], 16)
            n_items = load_n_items(pool)
            pool.sem_inc(pool_passed, 2 * NE)
            with pool.Fori(0, N_OVER // 2) as i:
                for p in range(2):
                    e = i * 2 + NE + p
                    with pool.If(e < n_items):
                        lone_wait(pool, xT_full, e, pool_passed)
                        pool.tensor_copy(next_token[0:SB, 1 - p:2 - p], token_tab[0:SB, bass.ds(e + 1, 1)])\
                            .then_inc(token_copied, 1)
                        lone_wait(pool, token_copied, i * 2 + p + 1, pool_passed)
                        pool.indirect_dma_start(x_rows[0:SB, 1 - p, :], None, io["t2_rows"],
                                                bass.IndirectOffsetOnAxis(next_token[0:SB, 1 - p:2 - p], 0))\
                            .then_inc(x_got[1 - p], 16)
            stores = [load_n_items(pool, 1), load_n_items(pool, 2)]
            lone_wait(pool, pool_passed, n_items * 2, pool_finished)
            for p in range(2):
                pool.wait_ge(y_stored[p], stores[p])
            pool.sem_inc(pool_finished, 1)
            for t in range(T5):
                n = P if t < NT else NS
                for c in range(2):
                    a = c * T5 + t
                    pool.indirect_dma_start(picked[0:n, t, c, :], None, io["expert_rows"],
                                            bass.IndirectOffsetOnAxis(rank_i[0:n, a:a + 1], 0)).then_inc(picked_in[t], 16)
            pool.wait_ge(outs, 16 * n_outs[0])

        @block.scalar
        def _(act):
            lane = Lane(act, scalar_lane)
            act.wait_ge(c_in, 16)
            act.activation(c_T[:, :, :], c_T[:, :, :], ACT.Silu).then_inc(c_silu, 1)

            def evac(name, pairs, func=ACT.Copy, scale=1.0):
                banks.wait_full(act, name)
                for out, in_ in pairs:
                    ins = act.activation(out, in_, func, scale=scale)
                banks.drained(ins, name)

            def ada_out(c):
                if c >= 2:
                    banks.wait_full(act, ("adaS", c - 2))
                evac(("ada", c), [(G[:, c % 2, :], psum[:, c % 2, :])])

            act.wait_ge(zeroed, 1)
            for t in range(NT + 1):
                n = P if t < NT else NS
                act.wait_ge(x_in[t], 16)
                lane.wait()
                ins = act.activation(junk[0:n, :], xbuf[0:n, t, :], ACT.Square, accum_out=ssq[0:n, t:t + 1])
                lane.mark(ins) if t < NT else ins.then_inc(ssq_ready, 1)
            for c in range(4):
                ada_out(c)
            def hT_out(i):
                t = H_ORDER[i]
                n = P if t < NT else NS
                for j in range(2):
                    src = psum[:, 6 + j - 2 * (i % 2), 0:4 * n].rearrange("p (k n) -> p k n", k=4)
                    pairs = [(hT[:, 4 * j:4 * j + 4, t * P:t * P + n], src)]
                    if t == NT:
                        pairs.append((hTs[:, 4 * j:4 * j + 4, 0:NS], src))
                    evac(("hT", t, j), pairs)

            slices = {"A": [(araw, 0, NA, ACT.Copy)], "B": [(qraw, 0, NB, ACT.Copy)],
                      "C": [(kraw, 0, NKV * HD, ACT.Copy), (vg[:, :, 0:VG0], NKV * HD, VG0, ACT.Gelu_apprx_tanh)],
                      "D": [(vg[:, :, VG0:GM], 0, ND, ACT.Gelu_apprx_tanh)]}

            def rows_out(name, part, b):
                rows, t = (NS, NT) if part == "S" else (P, part)
                banks.wait_full(act, (name, part))
                for dst, o, w, func in slices[name]:
                    ins = act.activation(dst[0:rows, t, :], psum[0:rows, b, o:o + w], func)
                banks.drained(ins, (name, part))

            def products_out(name):
                width = sum(w for _, _, w, _ in slices[name])
                evac((name, "s"), [(G[:, 1, 0:width], psum[:, 2, 0:width])])

            hT_out(0)
            hT_out(1)
            banks.wait_full(act, ("adaS", 3))
            banks.wait_full(act, ("adaS", 2))
            act.wait_ge(raw_zeroed, 1)
            rows_out("A", 0, 0)
            products_out("A")
            hT_out(2)
            hT_out(3)
            rows_out("A", 1, 1)
            rows_out("A", "S", 3)
            hT_out(4)
            rows_out("A", 2, 0)
            rows_out("A", 3, 1)
            act.wait_ge(zeroed, 2)
            for t in range(NT):
                b = 4 + t % 2
                evac(("qkiT", t), [
                    (qiT[:, :, t * P:(t + 1) * P], psum[:, b, 0:2 * P].rearrange("p (j n) -> p j n", j=2)),
                    (kiT[:, t * P:(t + 1) * P], psum[:, b, 2 * P:3 * P])])
            src = psum[:, 4, 0:IH * NS].rearrange("p (h b) -> p b h", h=IH)
            act.wait_ge(qi_lhs_ready, 1)
            evac("qi_sample", [(qi_lhs[0:ID, :, 0:IH], src[0:ID]), (qi_lhs[ID:P, :, IH:2 * IH], src[ID:P])])
            evac("wi_sample", [(wi_lhs, psum[:, 5, 0:4 * NS].rearrange("p (c b) -> p c b", c=4))])
            index_scale = ID ** -0.5 * IH ** -0.5
            for qb in range(1, NT):
                L = (qb + 1) * P
                if qb > 1:
                    act.wait_ge(relu_p_read, qb - 1)
                evac(("dots", qb), [(relu_p[:, :, 0:L], psum[:, 0:4, 0:L])], ACT.Relu, index_scale)
                rows_out("B", qb - 1, 6 + (qb - 1) % 2)
            for b in range(NS):
                if b >= 2 and (b - 2) % 4 == 3:
                    banks.wait_full(act, ("dotsS", (b - 2) // 4))
                elif b >= 2:
                    act.wait_ge(ki_used, (b - 1) - (b - 1) // 4)
                for j in range(2):
                    evac(("kiT", b, j), [(ki_T[:, b % 2, j * 512:(j + 1) * 512], psum[:, 4 + j, :])])
                if b % 4 == 3:
                    g = b // 4
                    evac(("dotsS", g), [(relu_s[:, g, :].rearrange("p (j n) -> p j n", j=2), psum[:, 2 * g:2 * g + 2, :])],
                         ACT.Relu, index_scale)
                if b == 1:
                    rows_out("B", 3, 7)
                elif b in (3, 5, 7):
                    rows_out("C", b // 2 - 1, 6 + (b // 2 - 1) % 2)
            banks.wait_full(act, "scoresS")
            for half in range(2):
                view = scores[32 * half:32 * half + NS, 0:PAST // 2].rearrange("s (n r e) -> s e r n", r=8, e=2)
                for par in range(2):
                    src = psum[0:NS, 2 * par:2 * par + 2, :].rearrange("s j (r n) -> s (j r) n", r=4)
                    ins = act.activation(view[:, par], src[:, :, 64 * half:64 * half + 64], ACT.Copy)
            banks.drained(ins, "scoresS")
            products_out("B")
            rows_out("C", 3, 7)
            rows_out("B", "S", 3)
            products_out("C")
            rows_out("D", 0, 0)
            rows_out("C", "S", 3)
            products_out("D")
            rows_out("D", 1, 1)
            rows_out("D", "S", 3)
            rows_out("D", 2, 0)
            rows_out("D", 3, 1)
            for f in range(4):
                b = 2 * (f % 2)
                evac(("U", f), [(halves(uT[:, f, :]), pair(b))], ACT.Gelu_apprx_tanh)
            for t in range(NT):
                if t == 0:
                    banks.wait_drained(act, "scoresS")
                evac(("qT", t), [(qT[:, :, t * P:(t + 1) * P], psum[:, 4 + t % 2, :].rearrange("p (j n) -> p j n", j=4))])
            evac("kT", [(kT[:, 0:SEQ], psum[:, 6, :])])
            evac("qkT_s", [(qT[:, :, SEQ:TOK], psum[:, 7, 0:4 * NS].rearrange("p (j n) -> p j n", j=4)),
                           (kT[:, SEQ:TOK], psum[:, 7, 4 * NS:5 * NS])])
            def exponentials(g):
                L = (g // NKV + 1) * P
                act.wait_ge(max_ready, g + 1)
                for j in range(4):
                    s_j = soft[g % 2][:, j, 0:L]
                    ins = act.activation(s_j, s_j, ACT.Exp, bias=mx4[g % 2][:, j:j + 1], accum_out=sum4[g % 2][:, j:j + 1])
                ins.then_inc(exp_ready, 1)

            act.wait_ge(vg_ready, 1)
            exponentials(0)
            for g, (qb, kv) in enumerate([(qb, kv) for qb in range(NT) for kv in range(NKV)]):
                for c in range(qb + 1):
                    if g and kv == 1:
                        act.wait_ge(values_done, qb + 1)
                    elif g:
                        banks.wait_full(act, ("att", qb - 1))
                    evac(("probsT", g, c), [(probsT[:, c, :], psum[:, 4 + c % 2, :])])
                if kv == 1:
                    evac(("att", qb), [(attT[:, :, qb * P:(qb + 1) * P],
                                        psum[:, 6 + qb % 2, :].rearrange("p (j n) -> p j n", j=4))])
                if g + 1 < NT * NKV:
                    exponentials(g + 1)
                for n in (2 * g, 2 * g + 1):
                    c, f = n // 4, n % 4
                    to = 2 * c + f if f < 2 else KD + 2 * c + f - 2
                    evac((f"G{c}", f), [(halves(gates[:, to, :]), pair(2 * (f % 2)))], ACT.Sigmoid)
                if g == 3:
                    act.wait_ge(gm_ready, 1)
                if g == 5:
                    act.wait_ge(vg_s_stored, 16)
                evac(("ada", 4 + g), [(late_G[g], psum[:, 6 + (qb + 1) % 2, :])])
            for b in range(NS):
                if b == 0:
                    act.wait_ge(probs_ready, 8)
                evac(("k_selT", b), [(k_selT[:, b, :], psum[:, 6 + b % 2, 0:2 * P])])
            act.wait_ge(max_s_ready, 1)
            for g in range(2):
                ins = act.activation(soft_s[:, g, :], psum[:, g, 0:TOPK_S + 1], ACT.Exp, bias=mx2[:, g:g + 1],
                                     scale=HD ** -0.5, accum_out=sum2[:, g:g + 1])
                banks.drained(ins, ("att_ss", g))
            evac("probsT_s", [(probsT_s, psum[:, 2, :].rearrange("p (a n) -> p a n", n=P))])
            src = psum[:, 4, 0:NS * NH].rearrange("p (b v j) -> p v j b", b=NS, v=NKV)
            evac("att_samples", [(attT[0:HD, :, SEQ:TOK], src[0:HD, 0]), (attT[HD:P, :, SEQ:TOK], src[HD:P, 1])])
            act.wait_ge(merged, KD)
            def mod_out(c):
                m, half = ("gate1", "shift2", "scale2", "gate2")[c // 2 - 2], slice(512 * (c % 2), 512 * (c % 2) + 512)
                for g, name, b, rows in ((0, "adaP", 2 + c % 2, P), (1, "adaS", 4 + c % 2, NS)):
                    evac((name, c), [(mod2[m][0:rows, g, half], psum[0:rows, b, :])])

            for c in range(4, 8):
                mod_out(c)
            for name in ("O0", "O1"):
                if name == "O1":
                    banks.wait_full(act, ("O0", "S"))
                evac((name, "s"), [(G[:, 1, :], psum[:, 2, :])])
            for i, (_, n, t) in enumerate(ORDER):
                act.wait_ge(x2_ready, i + 1)
                if i:
                    act.wait_ge(ssq2_ready, i)
                ins = act.activation(junk2[0:n, :], x2[0:n, t, :], ACT.Square, accum_out=ssq[0:n, t:t + 1])
                ins.then_inc(ssq2_ready, 1)
            banks.wait_full(act, ("O1", 3))
            for i, (_, n, t) in enumerate(ORDER):
                cols = slice(t * P, t * P + n)
                for j in range(2):
                    evac(("t2T", t, j), [(hT[:, 4 * j:4 * j + 4, cols],
                                          psum[:, 4 + j + 2 * (i % 2), 0:4 * n].rearrange("p (k n) -> p k n", k=4))])
                dst = io["t2_rows"][t * P:t * P + n, :]
                act.dma_start(dst, t2[0:n, t, :]).then_inc(t2_stored, 16)
                if i >= 3:
                    s = i - 3
                    evac(("logits", s), [(logits_T[0:NEG + NE, s * HALF:(s + 1) * HALF], psum[0:NEG + NE, s, 0:HALF])])
            act.wait_ge(g_diff_ready, 1)
            act.activation(g_exp, g_tmp, ACT.Exp).then_inc(g_exp_ready, 1)
            act.wait_ge(e_diff_ready, 1)
            act.activation(e_ratio, e_ratio, ACT.Exp).then_inc(e_exp_ready, 1)
            for c in (10, 11):
                mod_out(c)

            def x_out(p, done):
                act.activation(x_T[:, p], psum[:, p, :].rearrange("p (k n) -> p k n", k=KD), ACT.Copy).then_inc(done, 1)

            def silu(p, done):
                act.activation(silu_g[0:SB, p, :], psum[SB:2 * SB, 2 + p, 0:DE], ACT.Silu).then_inc(done, 1)

            act.wait_ge(tables_ready, 1)
            act.wait_ge(xT_full, 1)
            x_out(0, xT_out)

            def act_item(i, k, first):
                e, p = i * BUFFERS + k, k % 2
                act.wait_ge(gu_full, e + 1)
                if not (first and k < 2):
                    act.wait_ge(hidden_done, e - 1)
                silu(p, silu_done)
                act.wait_ge(xT_full, e + 2)
                if not (first and k < 1):
                    act.wait_ge(gu_full, e)
                x_out(1 - p, xT_out)

            each_item(act, act_item)

        @block.vector
        def _(dve):
            lane = Lane(dve, vector_lane)
            asked = [0]

            def rsqrt_of(ms, sums, count, wait=True):
                asked[0] += 1
                dve.tensor_scalar(ms, sums, 1.0 / count, EPS, ALU.mult, ALU.add).then_inc(rstd_asked, 1)
                if wait:
                    dve.wait_ge(rstd_ready, asked[0])

            def rope(rope_tmp, view, heads):
                nt = view.shape[1]
                t1 = rope_tmp[:, 0:nt * heads * ROT].rearrange("p (t h r) -> p t h r", t=nt, h=heads)
                t2 = rope_tmp[:, nt * heads * ROT:2 * nt * heads * ROT].rearrange("p (t h r) -> p t h r", t=nt, h=heads)
                cos = spread_dim(C("cos").rearrange("p (t r) -> p t r", r=ROT), 2, heads)
                sin = spread_dim(C("sin").rearrange("p (t r) -> p t r", r=ROT), 2, heads)
                half = ROT // 2
                dve.tensor_tensor(t1, view[:, :, :, 0:ROT], cos, ALU.mult)
                dve.tensor_tensor(t2[:, :, :, 0:half], view[:, :, :, half:ROT], sin[:, :, :, 0:half], ALU.mult)
                lane.then(dve.tensor_tensor(t2[:, :, :, half:ROT], view[:, :, :, 0:half], sin[:, :, :, half:ROT], ALU.mult))
                return dve.tensor_tensor(view[:, :, :, 0:ROT], t1, t2, ALU.add)

            lane.then(dve.memset(stat[:, 16:212], 0.0))
            dve.memset(minus_half, -0.5).then_inc(zeroed, 1)
            dve.memset(hTs[:, :, :], 0.0)
            dve.memset(zeros[:, :], 0.0)
            dve.memset(araw[:, NT, :], 0.0)
            dve.memset(kraw[:, NT, :], 0.0).then_inc(raw_zeroed, 1)
            lane.mark(dve.memset(scores[0:32 + NS], TAKEN))
            dve.memset(qi_lhs, 0.0).then_inc(qi_lhs_ready, 1)
            dve.wait_ge(pages_in, 16)
            dve.wait_ge(const_in, 16)
            dve.tensor_scalar(page_rows, page_rep, float(PAGE // 16), C("page_seg"), ALU.mult, ALU.add)\
               .then_inc(page_rows_ready, 1)
            dve.wait_ge(ssq_ready, 1)
            rsqrt_of(ssq, ssq, D, wait=False)
            dve.wait_ge(bias_in, 32)
            for c in range(4):
                m, half = c // 2, slice(512 * (c % 2), 512 * (c % 2) + 512)
                for g, name, b, rows in ((0, "adaP", 2 + c % 2, P), (1, "adaS", 4 + c % 2, NS)):
                    banks.wait_full(dve, (name, c))
                    out = mod1[0:rows, g, m, half]
                    if m == 0:
                        ins = dve.tensor_copy(out, psum[0:rows, b, :])
                    else:
                        ins = dve.scalar_tensor_tensor(out, psum[0:rows, b, :], 1.0, gain1[0:rows, half], ALU.add, ALU.mult)
                    banks.drained(ins, (name, c))
            for c in range(4):
                banks.wait_drained(dve, ("adaP", c))
                banks.wait_drained(dve, ("adaS", c))
            dve.wait_ge(rstd_ready, 1)
            for t in H_ORDER:
                rows, g = (P, 0) if t < NT else (NS, 1)
                xt = xbuf[0:rows, t, :]
                lane.then(dve.scalar_tensor_tensor(xt, xt, rstd[0:rows, t:t + 1], mod1[0:rows, g, 1, :], ALU.mult, ALU.mult))
                dve.tensor_tensor(xt, xt, mod1[0:rows, g, 0, :], ALU.add).then_inc(h_ready, 1)
            dve.memset(vg[:, NT, :], 0.0)
            dve.memset(qraw[:, NT, :], 0.0).then_inc(zeroed, 1)

            for part in (0, 1, "S", 2, 3):
                banks.wait_drained(dve, ("A", part))
            ki = araw[:, :, KI:KI + ID]
            sq = ki_twice[:, :, 0:ID]
            lane.then(dve.tensor_tensor(sq, ki, ki, ALU.mult))
            lane.then(dve.tensor_reduce(ki_ms, sq, AX_X, ALU.add))
            rsqrt_of(ki_ms, ki_ms, ID)
            lane.then(dve.tensor_tensor(ki, ki, spread_dim(ki_r, 2, ID), ALU.mult))
            lane.then(dve.tensor_tensor(ki, ki, spread_dim(gains[:, 2 * HD:3 * HD], 1, NT + 1), ALU.mult))
            lane.then(rope(work, araw[:, :, 0:WI].rearrange("p t (h d) -> p t h d", d=ID), IH + 1))
            dve.tensor_copy(ki_twice.rearrange("p t (c d) -> p t c d", c=2), spread_dim(ki, 2, 2)).then_inc(a_ready, 1)
            qi_s = araw[0:NS, NT, QI:KI].rearrange("p (h d) -> p h d", h=IH)
            wi_s = araw[0:NS, NT, WI:VV]
            dve.tensor_copy(qi_twice[0:NS], spread_dim(qi_s, 2, 2))
            dve.tensor_tensor(wi_place[0:NS].rearrange("p (c h) -> p c h", h=IH),
                              C("place")[0:NS].rearrange("p (c h) -> p c h", h=IH), spread_dim(wi_s, 1, P), ALU.mult)\
               .then_inc(qi_dup_ready, 1)

            prod = work[0:NS, 0:IH * ID].rearrange("p (h d) -> p h d", h=IH)
            nd = new_dots[0:NS]
            lane.then(dve.tensor_tensor(prod, qi_s, spread_dim(araw[0:NS, NT, KI:KI + ID], 1, IH), ALU.mult))
            lane.then(dve.tensor_reduce(nd, prod, AX_X, ALU.add))
            lane.then(dve.tensor_scalar(nd, nd, ID ** -0.5 * IH ** -0.5, 0.0, ALU.mult, ALU.max))
            lane.then(dve.tensor_tensor(nd, nd, wi_s, ALU.mult))
            lane.then(dve.tensor_reduce(scores[32:32 + NS, PAST // 2:PAST // 2 + 1], nd, AX_X, ALU.add))

            w_at = {1: 0, 2: 256, 3: 640}
            for qb in range(1, NT):
                L = (qb + 1) * P
                s = work[:, w_at[qb]:w_at[qb] + L]
                banks.wait_drained(dve, ("dots", qb))
                lane.then(dve.tensor_scalar(s, relu_p[:, 0, 0:L], araw[:, qb, WI:WI + 1], None, ALU.mult))
                for h in range(1, IH):
                    ins = dve.scalar_tensor_tensor(s, relu_p[:, h, 0:L], araw[:, qb, WI + h:WI + h + 1], s,
                                                   ALU.mult, ALU.add)
                    if h < IH - 1:
                        lane.then(ins)
                ins.then_inc(relu_p_read, 1)
                dve.wait_ge(relu_p_read, qb)
                lane.mark(dve.tensor_tensor(s[:, L - P:L], s[:, L - P:L], C("causal"), ALU.add))
            lane.wait()
            for _ in range(TOPK_P // 8):
                for qb in range(1, NT):
                    lane.mark(dve.max(top8[:, 8 * (qb - 1):8 * qb], work[:, w_at[qb]:w_at[qb] + (qb + 1) * P]))
                lane.wait()
                for qb in range(1, NT):
                    s = work[:, w_at[qb]:w_at[qb] + (qb + 1) * P]
                    lane.mark(dve.match_replace(s, top8[:, 8 * (qb - 1):8 * qb], s, TAKEN))
                lane.wait()
            lane.then(dve.tensor_scalar(work, work, TAKEN / 2, -BIG, ALU.is_gt, ALU.mult))

            rounds = [0]

            def sample_rounds(n):
                s = scores[0:32 + NS, :]
                for r in range(rounds[0], min(rounds[0] + n, TOPK_S // 8)):
                    best = top_values[0:32 + NS, 8 * r:8 * r + 8]
                    lane.then(dve.max(best, s))
                    lane.mark(dve.max_index(idx_u[0:32 + NS, 8 * r:8 * r + 8], best, s))
                    lane.then(dve.match_replace(s, best, s, TAKEN))
                rounds[0] += n

            def norm_heads(raw, heads, ms, r, gain):
                view = raw.rearrange("p t (h d) -> p (t h) d", d=HD)
                sq = norm_tmp[:, 0:(NT + 1) * heads * HD].rearrange("p (a d) -> p a d", d=HD)
                lane.then(dve.tensor_tensor(sq, view, view, ALU.mult))
                lane.then(dve.tensor_reduce(ms, sq, AX_X, ALU.add))
                rsqrt_of(ms, ms, HD)
                lane.then(dve.tensor_tensor(view, view, spread_dim(r, 2, HD), ALU.mult))
                lane.then(dve.tensor_tensor(view, view, spread_dim(gain, 1, (NT + 1) * heads), ALU.mult))
                return rope(norm_tmp, raw.rearrange("p t (h d) -> p t h d", d=HD), heads)

            banks.wait_drained(dve, "scoresS")
            sample_rounds(ROUNDS[0])
            for part in (0, 1, "S", 2, 3):
                banks.wait_drained(dve, ("B", part))
            norm_heads(qraw, NH, q_ms, q_r, gains[:, 0:HD]).then_inc(q_ready, 1)
            for part in (0, 1, "S", 2, 3):
                banks.wait_drained(dve, ("C", part))
            dve.wait_ge(q_ready, 1)
            norm_heads(kraw, NKV, k_ms, k_r, gains[:, HD:2 * HD]).then_inc(k_ready, 1)
            sample_rounds(ROUNDS[1])
            for part in (0, 1, "S", 2, 3):
                banks.wait_drained(dve, ("D", part))
            dve.wait_ge(ln_in, 16)
            for t in range(NT + 1):
                lane.mark(dve.bn_stats(bn[:, t, :], vg[:, t, :]))
            lane.wait()
            for t in range(NT + 1):
                lane.mark(dve.bn_aggr(mu_var[:, t, :], bn[:, t, :]))
            lane.wait()
            rsqrt_of(mu_var[:, :, 1], mu_var[:, :, 1], 1)
            for t in range(NT + 1):
                lane.mark(dve.tensor_scalar(vg[:, t, :], vg[:, t, :], mu_var[:, t, 0:1], vg_r[:, t:t + 1],
                                            ALU.subtract, ALU.mult))
            lane.wait()
            lane.then(dve.tensor_tensor(vg, vg, spread_dim(ln[:, 0, :], 1, NT + 1), ALU.mult))
            dve.tensor_tensor(vg, vg, spread_dim(ln[:, 1, :], 1, NT + 1), ALU.add).then_inc(vg_ready, 1)
            sample_rounds(ROUNDS[2])
            dve.wait_ge(gmlp_in, 64)
            for j in range(4):
                banks.wait_drained(dve, ("U", j))
            mixed = norm_tmp[:, 0:SEQ]
            for j in range(4):
                banks.wait_full(dve, ("mix", j))
                banks.drained(dve.tensor_tensor(
                    mixed.rearrange("p (c t) -> p c t", t=P), psum[:, 4 + j % 2, :].rearrange("p (c t) -> p c t", t=P),
                    spread_dim(bT[:, j, :], 1, NT), ALU.add), ("mix", j))
                banks.wait_drained(dve, ("mix", j))
                dve.tensor_tensor(uT[:, j, 0:SEQ], uT[:, j, 0:SEQ], mixed, ALU.mult).then_inc(gm_tile, 1)
                dve.wait_ge(gm_tile, j + 1)
            banks.wait_full(dve, "vgT_s")
            ms = norm_tmp[:, 0:4 * NS].rearrange("p (j s) -> p j s", j=4)
            banks.drained(dve.tensor_tensor(ms, psum[:, 6, 0:4 * NS].rearrange("p (j s) -> p j s", j=4),
                                            spread_dim(gm_w0, 2, NS), ALU.mult), "vgT_s")
            banks.wait_drained(dve, "vgT_s")
            lane.then(dve.tensor_tensor(ms, ms, spread_dim(bT[:, :, 0], 2, NS), ALU.add))
            dve.tensor_tensor(uT[:, :, SEQ:TOK], uT[:, :, SEQ:TOK], ms, ALU.mult).then_inc(gm_ready, 1)
            dve.wait_ge(gm_ready, 1)

            for g, (qb, kv) in enumerate([(qb, kv) for qb in range(NT) for kv in range(NKV)]):
                L = (qb + 1) * P
                s, mx, su, inv = soft[g % 2][:, :, 0:L], mx4[g % 2], sum4[g % 2], inv4[g % 2]
                mask = C("causal") if qb == 0 else work[:, w_at[qb]:w_at[qb] + L]
                if g >= 2:
                    banks.wait_full(dve, ("probsT", g - 2, (g - 2) // NKV))
                banks.wait_full(dve, ("att_s", g))
                if g == 0:
                    for t in range(NT):
                        banks.wait_drained(dve, ("qT", t))
                    banks.wait_full(dve, "qkT_s")
                banks.drained(dve.scalar_tensor_tensor(s, psum[:, 0:4, 0:L], HD ** -0.5, spread_dim(mask, 1, 4),
                                                       ALU.mult, ALU.add), ("att_s", g))
                banks.wait_drained(dve, ("att_s", g))
                lane.then(dve.tensor_reduce(mx, s, AX_X, ALU.max))
                dve.tensor_scalar(mx, mx, -1.0, None, ALU.mult).then_inc(max_ready, 1)
                sample_rounds(1)
                dve.wait_ge(exp_ready, g + 1)
                lane.then(dve.reciprocal(inv, su))
                dve.tensor_tensor(s, s, spread_dim(inv, 2, L), ALU.mult).then_inc(probs_ready, 1)
                sample_rounds(ROUNDS[3 + g])
            sample_rounds(TOPK_S // 8)
            back = slice(None, None, -1)
            lane.mark(dve.tensor_copy(second_values[0:NS], top_values[32:32 + NS, back]))
            lane.then(dve.tensor_copy(half_idx[0:32 + NS], idx_u[0:32 + NS]))
            lane.mark(dve.tensor_tensor(second_values[0:NS], top_values[0:NS], second_values[0:NS], ALU.is_ge))
            lane.then(dve.tensor_scalar(second_idx[0:NS], half_idx[32:32 + NS, back], float(PAST // 2), None, ALU.add))
            lane.then(dve.tensor_tensor(half_idx[0:NS], half_idx[0:NS], second_idx[0:NS], ALU.subtract))
            lane.then(dve.tensor_tensor(half_idx[0:NS], half_idx[0:NS], second_values[0:NS], ALU.mult))

            lane.then(dve.tensor_tensor(idx_f[0:NS], half_idx[0:NS], second_idx[0:NS], ALU.add))
            dve.tensor_scalar(key_bias[0:NS, 0:TOPK_S], idx_f[0:NS], float(PAST), -BIG, ALU.is_equal, ALU.mult)\
               .then_inc(idx_ready, 1)
            lane.then(dve.tensor_reduce(idx_max[0:NS], idx_f[0:NS], AX_X, ALU.max))
            dve.tensor_scalar(key_bias[0:NS, TOPK_S:TOPK_S + 1], idx_max[0:NS], float(PAST), -BIG, ALU.is_lt, ALU.mult)\
               .then_inc(key_bias_ready, 1)
            dve.wait_ge(pages_all_in, 16)
            lane.then(dve.tensor_copy(pages_f, pages_i))
            banks.wait_full(dve, "idxT")
            banks.drained(dve.tensor_copy(slot_i, psum[:, 4, 0:2 * NS]), "idxT")
            banks.wait_drained(dve, "idxT")
            lane.mark(dve.tensor_scalar(off_i, slot_i, PAGE - 1, None, ALU.bitwise_and))
            lane.then(dve.tensor_scalar(slot_i, slot_i, 7, None, ALU.logical_shift_right))
            lane.mark(dve.tensor_copy(page_f, slot_i))
            lane.then(dve.tensor_copy(off_f, off_i))
            lane.then(dve.tensor_tensor(page_hot, spread_dim(C("iota")[:, 0:N_PAGES], 1, 2 * NS),
                                        spread_dim(page_f, 2, N_PAGES), ALU.is_equal))
            hot = page_hot.rearrange("p (h b) n -> p h (b n)", h=2)
            lane.then(dve.tensor_tensor(hot, hot, spread_dim(pages_f, 1, 2), ALU.mult))
            lane.then(dve.tensor_reduce(slot_f, page_hot, AX_X, ALU.add))
            dve.scalar_tensor_tensor(sel_rows, slot_f, float(PAGE), off_f, ALU.mult, ALU.add).then_inc(sel_rows_ready, 1)
            lane.then(dve.memset(q_lhs, 0.0))
            banks.wait_drained(dve, "qkT_s")
            for v in range(NKV):
                o = HD * v
                dve.tensor_copy(q_lhs[o:o + HD, :, 4 * v:4 * v + 4], qT[o:o + HD, :, SEQ:TOK].rearrange("p j b -> p b j"))\
                   .then_inc(q_lhs_ready, 1)
            def gated(name, f, b, g):
                banks.wait_full(dve, (name, f))
                banks.drained(dve.tensor_tensor(halves(gates[:, g, :]), halves(gates[:, g, :]), pair(b), ALU.mult), (name, f))

            def gmlp_gated(*fs):
                for f in fs:
                    gated("WG", f, 2 + 4 * (f % 2), KD + f)

            for n in range(16):
                banks.wait_drained(dve, (f"G{n // 4}", n % 4))
            gmlp_gated(0, 1, 2, 3)
            for g in range(2):
                banks.wait_full(dve, ("att_ss", g))
            lane.then(dve.tensor_reduce(mx2, psum[:, 0:2, 0:TOPK_S + 1], AX_X, ALU.max))
            dve.tensor_scalar(mx2, mx2, -HD ** -0.5, None, ALU.mult).then_inc(max_s_ready, 1)
            for g in range(2):
                banks.wait_drained(dve, ("att_ss", g))
            lane.then(dve.reciprocal(inv2, sum2))
            lane.then(dve.tensor_tensor(soft_s, soft_s, spread_dim(inv2, 2, TOPK_S + 1), ALU.mult))
            lane.mark(dve.tensor_scalar(new_probs[:, 0, :], C("head"), soft_s[:, 0, TOPK_S:TOPK_S + 1], None, ALU.mult))
            dve.tensor_scalar(new_probs[:, 1, :], C("head"), soft_s[:, 1, TOPK_S:TOPK_S + 1], None, ALU.mult)\
               .then_inc(probs_s_ready, 1)
            gmlp_gated(4, 5)
            banks.wait_full(dve, "new_probs")
            banks.drained(dve.tensor_copy(sstat[0:NS, 52:60], psum[0:NS, 3, 0:NH]), "new_probs")
            banks.wait_drained(dve, "new_probs")
            dve.tensor_tensor(new_spread[0:NS].rearrange("p (b h) -> p b h", b=NS),
                              C("own")[0:NS].rearrange("p (b h) -> p b h", b=NS),
                              spread_dim(sstat[0:NS, 52:60], 1, NS), ALU.mult).then_inc(new_spread_ready, 1)
            gmlp_gated(6, 7)

            for f in range(KD):
                gated("WA", f, 4 * (f % 2), f)
                banks.wait_drained(dve, ("WG", f))
                banks.wait_drained(dve, ("WA", f))
                lane.mark(dve.tensor_tensor(hT[:, f, :], gates[:, f, :], gates[:, KD + f, :], ALU.add))
                lane.wait()
                dve.tensor_copy(hTs[:, f, 0:NS], hT[:, f, SEQ:TOK]).then_inc(merged, 1)
            dve.wait_ge(late_in, 16)
            for c in (8, 9):
                half = slice(512 * (c % 2), 512 * (c % 2) + 512)
                for g, name, b, rows in ((0, "adaP", 2 + c % 2, P), (1, "adaS", 4 + c % 2, NS)):
                    banks.wait_full(dve, (name, c))
                    banks.drained(dve.scalar_tensor_tensor(mod2["scale2"][0:rows, g, half], psum[0:rows, b, :], 1.0,
                                                           gain2[0:rows, half], ALU.add, ALU.mult), (name, c))
            for c in (4, 5):
                banks.wait_drained(dve, ("adaP", c))
                banks.wait_drained(dve, ("adaS", c))
            def second_norm(i):
                _, rows, t = ORDER[i]
                g = 0 if t < NT else 1
                out = t2[0:rows, t, :]
                dve.wait_ge(ssq2_ready, i + 1)
                rsqrt_of(ssq[:, t:t + 1], ssq[:, t:t + 1], D)
                lane.then(dve.scalar_tensor_tensor(out, x2[0:rows, t, :], rstd[0:rows, t:t + 1],
                                                   mod2["scale2"][0:rows, g, :], ALU.mult, ALU.mult))
                dve.tensor_tensor(out, out, mod2["shift2"][0:rows, g, :], ALU.add).then_inc(t2_ready, 1)

            dve.wait_ge(x2_in, 16 * T5)
            for c in range(2):
                half = slice(512 * c, 512 * c + 512)
                for i, (part, rows, t) in enumerate(ORDER):
                    b = 3 if part == "S" else t % 2
                    banks.wait_full(dve, (f"O{c}", part))
                    tmp = w_tmp[0:rows, i % 2, :]
                    g = 1 if part == "S" else 0
                    if c + i:
                        dve.wait_ge(x2_half if c == 0 or i == 0 else x2_ready, 5 if c and i == 0 else i)
                    banks.drained(dve.tensor_tensor(tmp, psum[0:rows, b, :], mod2["gate1"][0:rows, g, half], ALU.mult),
                                  (f"O{c}", part))
                    banks.wait_drained(dve, (f"O{c}", part))
                    dve.tensor_tensor(x2[0:rows, t, half], x2[0:rows, t, half], tmp, ALU.add)\
                       .then_inc(x2_ready if c else x2_half, 1)
                    if c == 1 and i == 0:
                        for late in (6, 7, 8, 9):
                            banks.wait_drained(dve, ("adaP", late))
                            banks.wait_drained(dve, ("adaS", late))
                    if c == 1 and i:
                        second_norm(i - 1)
            second_norm(T5 - 1)

            lane.then(dve.memset(logits, 0.0))
            banks.wait_full(dve, "logits_rows")
            n36 = NEG + NE
            lane.mark(dve.tensor_tensor(logits[:, 0:NT, :], psum[:, 2, 0:NT * n36].rearrange("p (t n) -> p t n", t=NT),
                                        spread_dim(b_router, 1, NT), ALU.add))
            banks.drained(dve.tensor_tensor(logits[0:NS, NT, :], psum[0:NS, 2, NT * n36:T5 * n36], b_router[0:NS], ALU.add),
                          "logits_rows")
            banks.wait_drained(dve, "logits_rows")

            def first_best(hot, values, best, rev, tmp, width):
                lane.then(dve.tensor_reduce(best, values, AX_X, ALU.max))
                lane.then(dve.tensor_tensor(tmp, values, spread_dim(best, 2, width), ALU.is_equal))
                lane.then(dve.tensor_tensor(tmp, tmp, spread_dim(C(rev), 1, T5), ALU.mult))
                lane.then(dve.tensor_reduce(w_max, tmp, AX_X, ALU.max))
                lane.then(dve.tensor_tensor(hot, tmp, spread_dim(w_max, 2, width), ALU.is_equal))

            g_logits = logits[:, :, 0:NEG]
            first_best(g_exp, g_logits, g_max, "rev4", g_tmp, NEG)
            lane.then(dve.tensor_scalar(g_exp, g_exp, -1.0, BIG, ALU.add, ALU.mult))
            lane.mark(dve.tensor_tensor(e_logits.rearrange("p t (g e) -> p t g e", g=NEG),
                                        logits[:, :, NEG:n36].rearrange("p t (g e) -> p t g e", g=NEG),
                                        spread_dim(g_exp, 3, EPG), ALU.add))
            lane.wait()
            dve.tensor_tensor(g_tmp, g_logits, spread_dim(g_max, 2, NEG), ALU.subtract).then_inc(g_diff_ready, 1)
            first_best(hot1, e_logits, e_max1, "rev32", e_tmp, NE)
            lane.then(dve.scalar_tensor_tensor(e_logits, hot1, -BIG, e_logits, ALU.mult, ALU.add))
            first_best(hot2, e_logits, e_max2, "rev32", e_tmp, NE)
            dve.tensor_tensor(e_ratio, e_max2, e_max1, ALU.subtract).then_inc(e_diff_ready, 1)
            lane.then(dve.tensor_tensor(chosen, hot1, hot2, ALU.add))
            lane.mark(dve.tensor_tensor(chosen, chosen, spread_dim(C("valid"), 2, NE), ALU.mult))
            lane.then(dve.memset(before_sum[:, 0, :], 0.0))
            for t in range(T5):
                ins = dve.tensor_tensor(before_sum[:, t + 1, :], before_sum[:, t, :], chosen[:, t, :], ALU.add)
                lane.then(ins) if t < NT else ins.then_inc(chosen_ready, 1)
            dve.wait_ge(g_exp_ready, 1)
            lane.then(dve.tensor_reduce(g_sum, g_exp, AX_X, ALU.add))
            dve.wait_ge(e_exp_ready, 1)
            lane.then(dve.tensor_scalar(p_first, e_ratio, 1.0, None, ALU.add))
            lane.then(dve.tensor_tensor(p_first, p_first, g_sum, ALU.mult))
            lane.then(dve.reciprocal(gate_of[:, 0, :], p_first))
            lane.then(dve.tensor_tensor(gate_of[:, 0, :], gate_of[:, 0, :], C("valid"), ALU.mult))
            lane.mark(dve.tensor_tensor(gate_of[:, 1, :], gate_of[:, 0, :], e_ratio, ALU.mult))
            lane.mark(dve.tensor_copy(token_of, spread_dim(C("tok"), 1, 2)))

            banks.wait_full(dve, "places")
            lane.mark(dve.tensor_copy(place, psum[:, 3, 0:T5 * NE].rearrange("p (t n) -> p t n", t=T5)))
            banks.drained(dve.tensor_copy(counts, psum[:, 3, T5 * NE:(T5 + 1) * NE]), "places")
            banks.wait_drained(dve, "places")
            lane.then(dve.tensor_tensor(over_cmp, spread_dim(counts, 2, 8), spread_dim(C("over"), 1, NE), ALU.is_gt))
            lane.then(dve.tensor_reduce(n_over, over_cmp, AX_X, ALU.add))
            lane.then(dve.tensor_tensor_scan(over_end, C("ones")[:, 0:NE], n_over, 0.0, ALU.mult, ALU.add))
            lane.then(dve.tensor_tensor(over_shift, over_end, n_over, ALU.subtract))
            lane.then(dve.tensor_scalar(over_shift, over_shift, float(SB), float(SB * (NE - 1)), ALU.mult, ALU.add))
            lane.then(dve.tensor_tensor(over_shift, over_shift, C("first_slot"), ALU.subtract))
            lane.then(dve.tensor_scalar(e_tmp, place, float(SB), None, ALU.is_ge))
            lane.then(dve.tensor_tensor(e_tmp, e_tmp, spread_dim(over_shift, 1, T5), ALU.mult))
            lane.then(dve.tensor_tensor(place, place, e_tmp, ALU.add))
            lane.then(dve.tensor_tensor(place, place, spread_dim(C("first_slot"), 1, T5), ALU.add))
            for c, hot in enumerate((hot1, hot2)):
                lane.then(dve.tensor_tensor(e_tmp, hot, place, ALU.mult))
                lane.then(dve.tensor_reduce(rank[:, c, :], e_tmp, AX_X, ALU.add))
            flat = lambda a: a.rearrange("p c t -> p (c t)")
            lane.then(dve.tensor_copy(rank_i, flat(rank)))
            lane.mark(dve.tensor_scalar(slot_of_i, rank_i, SB - 1, None, ALU.bitwise_and))
            lane.then(dve.tensor_scalar(item_of_i, rank_i, 6, None, ALU.logical_shift_right))
            lane.mark(dve.tensor_copy(slot_of, slot_of_i))
            lane.then(dve.tensor_copy(item_of, item_of_i))
            for half in range(2):
                lane.mark(dve.tensor_tensor(slot_hot[:, :, SB * half:SB * half + SB],
                                            spread_dim(C("iota")[:, 0:SB], 1, 2 * T5), spread_dim(slot_of, 2, SB),
                                            ALU.is_equal))
            gate_cols = item_hot[:, :, N_ITEMS:2 * N_ITEMS]
            token_cols = item_hot[:, :, 0:N_ITEMS]
            lane.then(dve.tensor_tensor(gate_cols, spread_dim(C("iota")[:, 0:N_ITEMS], 1, 2 * T5),
                                        spread_dim(item_of, 2, N_ITEMS), ALU.is_equal))
            lane.then(dve.tensor_tensor(token_cols, gate_cols, spread_dim(flat(token_of), 2, N_ITEMS), ALU.mult))
            dve.tensor_tensor(gate_cols, gate_cols, spread_dim(flat(gate_of), 2, N_ITEMS), ALU.mult)\
               .then_inc(tables_hot_ready, 1)
            lane.then(dve.tensor_tensor(over_hot[0:1], spread_dim(over_end[0:1], 1, N_OVER),
                                        spread_dim(C("iota")[0:1, 0:N_OVER], 2, NE), ALU.is_le))
            lane.then(dve.tensor_reduce(over_expert_f[0:1], over_hot[0:1], AX_X, ALU.add))
            lane.mark(dve.memset(over_expert[0:1], 0))
            lane.mark(dve.memset(token_tab[:, N_ITEMS:], 0))
            lane.then(dve.tensor_scalar(item_counts[0:1, 0:1], over_end[0:1, NE - 1:NE], float(NE), None, ALU.add))
            lane.mark(dve.tensor_scalar(over_expert[0:1, 0:N_OVER], over_expert_f[0:1], float(NE - 1), None, ALU.min))
            lane.then(dve.tensor_scalar(item_counts[0:1, 1:2], over_end[0:1, NE - 1:NE], float(NE + 1), None, ALU.add))
            lane.mark(dve.tensor_scalar(item_counts[0:1, 1:2], item_counts[0:1, 1:2], 1, 5, ALU.logical_shift_right,
                                        ALU.logical_shift_left))
            lane.mark(dve.tensor_scalar(item_counts[0:1, 2:3], item_counts[0:1, 0:1], 1, 5, ALU.logical_shift_right,
                                        ALU.logical_shift_left))
            banks.wait_full(dve, "tables")
            banks.drained(dve.tensor_copy(gate_tab, psum[:, 4, N_ITEMS:2 * N_ITEMS]), "tables")
            dve.tensor_copy(token_tab[:, 0:N_ITEMS], psum[:, 4, 0:N_ITEMS]).then_inc(tables_ready, 1)

            def hidden_of(p, done):
                dve.tensor_tensor(hidden[0:SB, p, :], silu_g[0:SB, p, :], psum[0:SB, 2 + p, 0:DE], ALU.mult).then_inc(done, 1)

            def hidden_out(p, done):
                dve.tensor_copy(hidden_T[:, p], psum[:, 4 + p, 0:2 * SB].rearrange("p (f n) -> p f n", f=2)).then_inc(done, 1)

            def y_scaled(p, gate, done):
                dve.tensor_scalar(y_rows[:, p, :], psum[:, 6 + p, :], gate, None, ALU.mult).then_inc(done, 1)

            def dve_item(i, k, first):
                e, p = i * BUFFERS + k, k % 2
                dve.wait_ge(silu_done, e + 1)
                if not (first and k < 2):
                    dve.wait_ge(hT_full, e - 1)
                hidden_of(p, hidden_done)
                dve.wait_ge(hT_full, e + 1)
                if not (first and k < 2):
                    dve.wait_ge(y_full, e - 1)
                hidden_out(p, hT_out)
                dve.wait_ge(y_full, e + 1)
                if not (first and k < 2):
                    dve.wait_ge(y_stored[p], i * (16 * BUFFERS) + 32 * (k // 2))
                gate = gate_tab[:, e:e + 1] if first else gate_tab[:, bass.ds(e, 1)]
                y_scaled(p, gate, y_out)

            dve.wait_ge(tables_ready, 1)
            each_item(dve, dve_item)

            for c in (10, 11):
                banks.wait_drained(dve, ("adaP", c))
                banks.wait_drained(dve, ("adaS", c))
            for t in range(T5):
                rows, g = (P, 0) if t < NT else (NS, 1)
                dve.wait_ge(picked_in[t], 32)
                a, b = picked[0:rows, t, 0, :], picked[0:rows, t, 1, :]
                lane.then(dve.tensor_tensor(a, a, b, ALU.add))
                lane.then(dve.tensor_tensor(a, a, mod2["gate2"][0:rows, g, :], ALU.mult))
                dve.tensor_tensor(x2[0:rows, t, :], x2[0:rows, t, :], a, ALU.add).then_inc(y_ready, 1)


def _tiles(w, width):
    k = w.shape[0] // P
    return w.reshape(k, P, width).transpose(1, 0, 2).reshape(P, k * width)


def _stream(inputs):
    w_in, w_ada = inputs["w_in"][0], inputs["w_ada"][0]
    o = np.cumsum([0, NH * HD, NKV * HD, NKV * HD, IH * ID, ID, IH, GM, GM, 2 * D])
    q, k, v, qi, ki, wi, u, vg, gates = (w_in[:, o[i]:o[i + 1]] for i in range(9))
    q = q.reshape(D, NH, HD)[:, HEAD_ORDER].reshape(D, NH * HD)
    wa = inputs["w_proj_attn"][0].reshape(NH, HD, D)[HEAD_ORDER].reshape(NH * HD, D)
    parts = {f"ada{c}": w_ada[:, 512 * c:512 * c + 512] for c in range(12)}
    parts |= {"A": np.concatenate([qi, ki, wi, v], 1), "B": q, "C": np.concatenate([k, vg[:, :VG0]], 1),
              "D": vg[:, VG0:], "U": u}
    parts |= {f"G{c}": np.concatenate([gates[:, 256 * c:256 * c + 256], gates[:, D + 256 * c:D + 256 * c + 256]], 1)
              for c in range(4)}
    parts |= {"WA": wa, "WG": inputs["w_proj_gmlp"][0]}
    parts |= {f"O{c}": inputs["w_out"][0][:, 512 * c:512 * c + 512] for c in range(2)}
    out = np.zeros((len(STREAM), P, KD * 512), np.float32)
    for n, (name, size) in enumerate(STREAM):
        w = parts[name]
        out[n, :, :size] = _tiles(w, w.shape[1])
    return out


def _layout(inputs):
    x = {k: np.asarray(v) for k, v in inputs.items()}
    c = np.concatenate([x["c_sample"], x["c_prompt"]], 0)
    c_T = np.zeros((P, KD, 32), np.float32)
    c_T[:, :, :NS + 1] = c.reshape(NS + 1, KD, P).transpose(2, 1, 0)
    a = {
        "consts": np.concatenate(list(CONSTS.values()), 1),
        "stream": _stream(x),
        "c_T": c_T.reshape(P, -1),
        "b_ada": x["b_ada"].reshape(12, 512),
        "norm_mix_g": x["norm_mix_g"][0],
        "norm_ffn_g": x["norm_ffn_g"][0],
        "head_gains": np.concatenate([x["q_norm_g"][0], x["k_norm_g"][0], x["kidx_norm_g"][0]]),
        "ln": np.concatenate([x["gm_ln_g"], x["gm_ln_b"]], 0),
        "x_prompt": x["x_prompt"][0],
        "x_sample": x["x_sample"][:, 0],
        "page_rep": np.repeat(x["page_table"].T, 8, axis=0),
        "pages": x["page_table"].reshape(-1),
        "cache_ki": x["cache_kidx"].reshape(POOL_PAGES * 8, 16 * ID),
        "cache_k": x["cache_k"].reshape(POOL_PAGES * PAGE, NKV * HD),
        "cache_v": x["cache_v"].reshape(POOL_PAGES * PAGE, NKV * HD),
        "ws_T": x["gm_spatial_w"][0].transpose(2, 0, 1).reshape(P, GG * CHUNK),
        "ws_00": x["gm_spatial_w"][0][:, 0, 0].reshape(4, 2).T,
        "gm_b": x["gm_spatial_b"][0],
        "w_router": _tiles(np.concatenate([x["w_router_group"][0], x["w_router_expert"][0]], 1), NEG + NE),
        "b_router": np.concatenate([x["b_router_group"][0], x["b_router_expert"][0]]),
        "experts": np.concatenate([
            np.concatenate([x["w_expert_gate"][0], x["w_expert_up"][0]], 2)
            .reshape(NE, KD, P, 2 * DE).transpose(0, 2, 1, 3).reshape(NE, P, KD * 2 * DE),
            x["w_expert_down"][0].reshape(NE, 2, P, D).transpose(0, 2, 1, 3).reshape(NE, P, 2 * D)], 2),
    }
    return {k: np.ascontiguousarray(v) for k, v in a.items()}


OUTS = {
    "y_p": (SEQ, D), "y_s": (NS, D),
    "new_k_p": (SEQ, NKV * HD), "new_v_p": (SEQ, NKV * HD), "new_ki_p": (SEQ, ID),
    "new_k_s": (NS, NKV * HD), "new_v_s": (NS, NKV * HD), "new_ki_s": (NS, ID), "new_vg_s": (NS, GM),
}
SCRATCH = {"t2_rows": (TOK, D), "expert_rows": (N_ITEMS * SB, D)}


def kernel(**inputs):
    import concourse.bacc as bacc
    from concourse.bass_utils import run_bass_kernel_spmd

    arrays = _layout(inputs)
    nc = bacc.Bacc("TRN2", target_bir_lowering=False, num_devices=1)
    io = {k: nc.dram_tensor(f"in_{k}", a.shape, mybir.dt.from_np(a.dtype), kind="ExternalInput").ap()
          for k, a in arrays.items()}
    io |= {k: nc.dram_tensor(f"out_{k}", s, F32, kind="ExternalOutput").ap() for k, s in OUTS.items()}
    io |= {k: nc.dram_tensor(k, s, F32, kind="Internal").ap() for k, s in SCRATCH.items()}
    decoder_step(nc, io)
    run = run_bass_kernel_spmd(nc, [{f"in_{k}": a for k, a in arrays.items()}], core_ids=[0])
    got = {k: run.results[0][f"out_{k}"] for k in OUTS}
    return (
        got["y_p"].reshape(1, SEQ, D), got["y_s"].reshape(NS, 1, D),
        got["new_k_p"].reshape(1, 1, SEQ, NKV, HD), got["new_v_p"].reshape(1, 1, SEQ, NKV, HD),
        got["new_ki_p"].reshape(1, 1, SEQ, ID),
        got["new_k_s"].reshape(1, NS, 1, NKV, HD), got["new_v_s"].reshape(1, NS, 1, NKV, HD),
        got["new_ki_s"].reshape(1, NS, 1, ID), got["new_vg_s"].reshape(1, NS, 1, GM),
    )
```
